# Optimizing a Trainium2 kernel written in Bass

```python
import jax
import jax.numpy as jnp
from jax import lax
import numpy as np

D_MODEL = 1024
BATCH = 1
SEQ = 512
DEPTH = 2

HEAD_DIM = 64
CHUNK = 64
MIX_HALF = D_MODEL // 2
N_EVEN = (DEPTH + 1) // 2
N_ODD = DEPTH // 2
NORM_EPS = 1e-6

RWKV_HEADS = MIX_HALF // HEAD_DIM
RWKV_DECAY_RANK = 64
RWKV_ICLR_RANK = 64
RWKV_GATE_RANK = 128
RWKV_IN = 3 * MIX_HALF + RWKV_DECAY_RANK + RWKV_ICLR_RANK + RWKV_GATE_RANK
RWKV_GN_EPS = 64e-5
RWKV_DECAY_SCALE = float(np.exp(-0.5))

GLA_HEADS = 4
GLA_DV = MIX_HALF // GLA_HEADS
GLA_DK = GLA_DV // 2
GLA_KEY = GLA_HEADS * GLA_DK
GLA_GATE_RANK = 16
GLA_GATE_NORM = 16.0
GLA_IN = 2 * GLA_KEY + MIX_HALF + GLA_GATE_RANK + MIX_HALF

HGRN_HEADS = 4
HGRN_DV = MIX_HALF // HGRN_HEADS
HGRN_DK = HGRN_DV // 2
HGRN_KEY = HGRN_HEADS * HGRN_DK
HGRN_IN = 2 * HGRN_KEY + 2 * MIX_HALF

SSD_HEADS = MIX_HALF // HEAD_DIM
SSD_GROUPS = 2
SSD_STATE = 64
SSD_CONV = 4
SSD_XBC = MIX_HALF + 2 * SSD_GROUPS * SSD_STATE
SSD_IN = MIX_HALF + SSD_XBC + SSD_HEADS

EVEN_IN = RWKV_IN + GLA_IN
ODD_IN = HGRN_IN + SSD_IN

N_EXPERTS = 16
N_EXPERT_GROUPS = 4
EXPERTS_PER_GROUP = N_EXPERTS // N_EXPERT_GROUPS
TOP_K = 2
D_EXPERT = D_MODEL // 2
MOE_BLOCK = 128

kernel_name = 'hybrid_rwkv7_gla_hgrn2_ssd_grouped_moe_adaln'

def split_cols(u, sizes):
    idx = [int(s) for s in np.cumsum(sizes)[:-1]]
    return jnp.split(u, idx, axis=-1)

def rms_norm(x, gain):
    xf = x.astype(jnp.float32)
    y = xf * lax.rsqrt(jnp.mean(xf * xf, axis=-1, keepdims=True) + NORM_EPS)
    return y.astype(x.dtype) * gain

def token_shift(u):
    return jnp.pad(u[:, :-1], ((0, 0), (1, 0), (0, 0)))

def causal_depthwise_conv(x, w, b):
    y = lax.conv_general_dilated(x, w[:, None, :], window_strides=(1,), padding=[(SSD_CONV - 1, 0)],
                                 dimension_numbers=('NWC', 'WIO', 'NWC'), feature_group_count=x.shape[-1])
    return y + b

def to_chunks(t):
    bsz, s, h, d = t.shape
    return t.reshape(bsz, s // CHUNK, CHUNK, h, d).transpose(1, 0, 3, 2, 4)

def chunked_gated_linear_attention(q, k, v, log_decay):
    bsz, s, h, dk = q.shape
    dv = v.shape[-1]
    causal = jnp.tril(jnp.ones((CHUNK, CHUNK), dtype=bool))

    def step(state, inp):
        qc, kc, vc, gc = inp
        b = jnp.cumsum(gc, axis=2)
        o_inter = jnp.einsum('bhid,bhdv->bhiv', qc * jnp.exp(b), state)
        diff = jnp.where(causal[:, :, None], b[:, :, :, None, :] - b[:, :, None, :, :], -jnp.inf)
        scores = jnp.einsum('bhid,bhjd,bhijd->bhij', qc, kc, jnp.exp(diff))
        o_intra = jnp.einsum('bhij,bhjv->bhiv', scores, vc)
        b_last = b[:, :, -1:, :]
        state = (jnp.exp(b_last[:, :, 0, :])[..., None] * state
                 + jnp.einsum('bhjd,bhjv->bhdv', kc * jnp.exp(b_last - b), vc))
        return state, o_inter + o_intra

    state0 = jnp.zeros((bsz, h, dk, dv), jnp.float32)
    _, o = lax.scan(step, state0, (to_chunks(q), to_chunks(k), to_chunks(v), to_chunks(log_decay)))
    return o.transpose(1, 0, 3, 2, 4).reshape(bsz, s, h, dv)

def rwkv7_recurrence(r, w, kk, a, kt, v):
    bsz, s, h, n = r.shape

    def step(state, inp):
        r_t, w_t, kk_t, a_t, kt_t, v_t = inp
        removed = jnp.einsum('bhvk,bhk->bhv', state, kk_t)
        state = (state * w_t[:, :, None, :]
                 - removed[..., None] * (kk_t * a_t)[:, :, None, :]
                 + v_t[..., None] * kt_t[:, :, None, :])
        return state, jnp.einsum('bhvk,bhk->bhv', state, r_t)

    xs = tuple(t.transpose(1, 0, 2, 3) for t in (r, w, kk, a, kt, v))
    _, y = lax.scan(step, jnp.zeros((bsz, h, n, n), jnp.float32), xs)
    return y.transpose(1, 0, 2, 3)

def ssd_chunked(xh, dt, a_neg, bm, cm):
    bsz, s, h, p = xh.shape
    g, n = bm.shape[2], bm.shape[3]
    rep = h // g
    nc = s // CHUNK
    causal = jnp.tril(jnp.ones((CHUNK, CHUNK), dtype=bool))
    x = (xh * dt[..., None]).reshape(bsz, nc, CHUNK, g, rep, p)
    bc = bm.reshape(bsz, nc, CHUNK, g, n)
    cc = cm.reshape(bsz, nc, CHUNK, g, n)
    da = (dt * a_neg).reshape(bsz, nc, CHUNK, g, rep).transpose(0, 1, 3, 4, 2)
    cum = jnp.cumsum(da, axis=-1)
    seg = jnp.exp(jnp.where(causal, cum[..., :, None] - cum[..., None, :], -jnp.inf))
    cb = jnp.einsum('bclgn,bcsgn->bcgls', cc, bc)
    y_diag = jnp.einsum('bcgls,bcgrls,bcsgrp->bclgrp', cb, seg, x)
    decay_to_end = jnp.exp(cum[..., -1:] - cum)
    chunk_states = jnp.einsum('bcsgn,bcgrs,bcsgrp->bcgrpn', bc, decay_to_end, x)
    chunk_decay = jnp.exp(cum[..., -1])

    def step(hs, inp):
        st, dec = inp
        return dec[..., None, None] * hs + st, hs

    h0 = jnp.zeros((bsz, g, rep, p, n), jnp.float32)
    _, prev = lax.scan(step, h0, (chunk_states.transpose(1, 0, 2, 3, 4, 5), chunk_decay.transpose(1, 0, 2, 3)))
    prev = prev.transpose(1, 0, 2, 3, 4, 5)
    y_off = jnp.einsum('bclgn,bcgrpn,bcgrl->bclgrp', cc, prev, jnp.exp(cum))
    return (y_diag + y_off).reshape(bsz, s, h, p)

def rwkv7_group(ua, mu, w0, w_up, a0, a_up, g_up, k_k, k_a, r_k, ln_gain, ln_bias):
    bsz, s, _ = ua.shape
    f32 = jnp.float32
    ua = ua + mu * (token_shift(ua) - ua)
    r, k, v, wd, ad, gd = split_cols(ua, [MIX_HALF, MIX_HALF, MIX_HALF, RWKV_DECAY_RANK, RWKV_ICLR_RANK, RWKV_GATE_RANK])
    d = (w0 + jnp.tanh(wd) @ w_up).astype(f32)
    w = jnp.exp(-RWKV_DECAY_SCALE * jax.nn.sigmoid(d))
    a = jax.nn.sigmoid((a0 + ad @ a_up).astype(f32))
    gate = jax.nn.sigmoid(gd) @ g_up
    hd = lambda t: t.astype(f32).reshape(bsz, s, RWKV_HEADS, HEAD_DIM)
    r, k, v, w, a = hd(r), hd(k), hd(v), hd(w), hd(a)
    kk = k * k_k.astype(f32).reshape(RWKV_HEADS, HEAD_DIM)
    kk = kk * lax.rsqrt(jnp.sum(kk * kk, axis=-1, keepdims=True) + 1e-12)
    kt = k * (1.0 + (a - 1.0) * k_a.astype(f32).reshape(RWKV_HEADS, HEAD_DIM))
    y = rwkv7_recurrence(r, w, kk, a, kt, v)
    mean = jnp.mean(y, axis=-1, keepdims=True)
    var = jnp.mean((y - mean) ** 2, axis=-1, keepdims=True)
    y = ((y - mean) * lax.rsqrt(var + RWKV_GN_EPS) * ln_gain.astype(f32).reshape(RWKV_HEADS, HEAD_DIM)
         + ln_bias.astype(f32).reshape(RWKV_HEADS, HEAD_DIM))
    y = y + jnp.sum(r * kt * r_k.astype(f32), axis=-1, keepdims=True) * v
    return (y.reshape(bsz, s, MIX_HALF) * gate).astype(ua.dtype)

def gla_group(ub, alpha_up, alpha_bias, norm_gain):
    bsz, s, _ = ub.shape
    f32 = jnp.float32
    q, k, v, ad, g = split_cols(ub, [GLA_KEY, GLA_KEY, MIX_HALF, GLA_GATE_RANK, MIX_HALF])
    log_a = jax.nn.log_sigmoid((ad @ alpha_up + alpha_bias).astype(f32)) / GLA_GATE_NORM
    hd = lambda t: t.astype(f32).reshape(bsz, s, GLA_HEADS, -1)
    o = chunked_gated_linear_attention(hd(q) * GLA_DK ** -0.5, hd(k), hd(v), hd(log_a))
    o = rms_norm(o, norm_gain)
    return (o.reshape(bsz, s, MIX_HALF) * jax.nn.silu(g)).astype(ub.dtype)

def hgrn_lower_bounds(c_lb):
    p = jax.nn.softmax(c_lb.astype(jnp.float32), axis=0)
    cum = jnp.cumsum(p, axis=0)
    return cum - cum[0:1]

def hgrn2_group(uc, lb, norm_gain):
    bsz, s, _ = uc.shape
    f32 = jnp.float32
    q, fr, i, g = split_cols(uc, [HGRN_KEY, HGRN_KEY, MIX_HALF, MIX_HALF])
    f = lb + (1.0 - lb) * jax.nn.sigmoid(fr.astype(f32))
    hd = lambda t: t.astype(f32).reshape(bsz, s, HGRN_HEADS, -1)
    o = chunked_gated_linear_attention(hd(q), hd(1.0 - f), hd(i), hd(jnp.log(f)))
    o = rms_norm(o, norm_gain)
    return (o.reshape(bsz, s, MIX_HALF) * jax.nn.silu(g)).astype(uc.dtype)

def ssd_group(ud, conv_w, conv_b, dt_bias, a_log, skip, norm_gain):
    bsz, s, _ = ud.shape
    f32 = jnp.float32
    z, xbc, dt_raw = split_cols(ud, [MIX_HALF, SSD_XBC, SSD_HEADS])
    xbc = jax.nn.silu(causal_depthwise_conv(xbc, conv_w, conv_b))
    xs, bm, cm = split_cols(xbc, [MIX_HALF, SSD_GROUPS * SSD_STATE, SSD_GROUPS * SSD_STATE])
    dt = jax.nn.softplus((dt_raw + dt_bias).astype(f32))
    a_neg = -jnp.exp(a_log.astype(f32))
    xh = xs.astype(f32).reshape(bsz, s, SSD_HEADS, HEAD_DIM)
    y = ssd_chunked(xh, dt, a_neg,
                    bm.astype(f32).reshape(bsz, s, SSD_GROUPS, SSD_STATE),
                    cm.astype(f32).reshape(bsz, s, SSD_GROUPS, SSD_STATE))
    y = y + skip.astype(f32)[:, None] * xh
    y = y.reshape(bsz, s, MIX_HALF) * jax.nn.silu(z.astype(f32))
    y = rms_norm(y.reshape(bsz, s, SSD_GROUPS, -1), norm_gain.astype(f32).reshape(SSD_GROUPS, -1))
    return y.reshape(bsz, s, MIX_HALF).astype(ud.dtype)

def grouped_moe(h, w_router, router_bias, w_gate, w_up, w_down):
    bsz, s, d = h.shape
    t = bsz * s
    hf = h.reshape(t, d)
    scores = jax.nn.sigmoid((hf @ w_router).astype(jnp.float32))
    sel = (scores + router_bias.astype(jnp.float32)).reshape(t, N_EXPERT_GROUPS, EXPERTS_PER_GROUP)
    group_score = jnp.sum(lax.top_k(sel, TOP_K)[0], axis=-1)
    group = jnp.argmax(group_score, axis=-1)
    in_group = jnp.take_along_axis(sel, group[:, None, None], axis=1)[:, 0]
    _, local = lax.top_k(in_group, TOP_K)
    expert = group[:, None] * EXPERTS_PER_GROUP + local
    gate = jnp.take_along_axis(scores, expert, axis=1)
    gate = gate / jnp.sum(gate, axis=-1, keepdims=True)
    n_assign = t * TOP_K
    flat_e = expert.reshape(n_assign)
    order = jnp.argsort(flat_e)
    sorted_e = flat_e[order]
    tok = (order // TOP_K).astype(jnp.int32)
    counts = jnp.bincount(flat_e, length=N_EXPERTS)
    padded = (counts + MOE_BLOCK - 1) // MOE_BLOCK * MOE_BLOCK
    pad_end = jnp.cumsum(padded)
    pad_start = pad_end - padded
    start = jnp.cumsum(counts) - counts
    dest = pad_start[sorted_e] + (jnp.arange(n_assign) - start[sorted_e])
    n_blocks = -(-n_assign // MOE_BLOCK) + N_EXPERTS
    n_pad = n_blocks * MOE_BLOCK
    buf_tok = jnp.zeros((n_pad,), jnp.int32).at[dest].set(tok)
    buf_w = jnp.zeros((n_pad,), h.dtype).at[dest].set(gate.reshape(n_assign)[order].astype(h.dtype))
    block_expert = jnp.minimum(jnp.searchsorted(pad_end, jnp.arange(n_blocks) * MOE_BLOCK, side='right'), N_EXPERTS - 1)
    xb = hf[buf_tok].reshape(n_blocks, MOE_BLOCK, d)

    def expert_block(args):
        xblk, e = args
        return (jax.nn.silu(xblk @ w_gate[e]) * (xblk @ w_up[e])) @ w_down[e]

    yb = lax.map(expert_block, (xb, block_expert)).reshape(n_pad, d)
    out = jnp.zeros((t, d), h.dtype).at[buf_tok].add(yb * buf_w[:, None])
    return out.reshape(bsz, s, d)

def setup_inputs(seed: int = 0) -> dict:
    key = jax.random.key(seed)
    keys = jax.random.split(key, 36)
    ki = iter(range(36))

    def nrm(shape, scale):
        return scale * jax.random.normal(keys[next(ki)], shape, jnp.float32)

    def unif(shape, lo, hi):
        return jax.random.uniform(keys[next(ki)], shape, jnp.float32, lo, hi)

    dt0 = jnp.exp(unif((N_ODD, SSD_HEADS), float(np.log(1e-3)), float(np.log(1e-1))))
    return {
        'x': nrm((BATCH, SEQ, D_MODEL), 1.0),
        'c': nrm((BATCH, D_MODEL), 1.0),
        'norm_gain': 1.0 + nrm((DEPTH, 2, D_MODEL), 0.05),
        'w_ada': nrm((DEPTH, D_MODEL, 6 * D_MODEL), 0.5 * D_MODEL ** -0.5),
        'b_ada': nrm((DEPTH, 6 * D_MODEL), 0.05),
        'w_in_even': nrm((N_EVEN, D_MODEL, EVEN_IN), D_MODEL ** -0.5),
        'w_in_odd': nrm((N_ODD, D_MODEL, ODD_IN), D_MODEL ** -0.5),
        'w_out': nrm((DEPTH, D_MODEL, D_MODEL), D_MODEL ** -0.5),
        'a_mu': unif((N_EVEN, RWKV_IN), 0.0, 1.0),
        'a_w0': unif((N_EVEN, MIX_HALF), -2.0, 2.0),
        'a_w_up': nrm((N_EVEN, RWKV_DECAY_RANK, MIX_HALF), RWKV_DECAY_RANK ** -0.5),
        'a_a0': nrm((N_EVEN, MIX_HALF), 0.5),
        'a_a_up': nrm((N_EVEN, RWKV_ICLR_RANK, MIX_HALF), RWKV_ICLR_RANK ** -0.5),
        'a_g_up': nrm((N_EVEN, RWKV_GATE_RANK, MIX_HALF), RWKV_GATE_RANK ** -0.5),
        'a_k_k': 0.85 + nrm((N_EVEN, MIX_HALF), 0.05),
        'a_k_a': 1.0 + nrm((N_EVEN, MIX_HALF), 0.05),
        'a_r_k': nrm((N_EVEN, RWKV_HEADS, HEAD_DIM), 0.1),
        'a_ln_gain': 1.0 + nrm((N_EVEN, MIX_HALF), 0.05),
        'a_ln_bias': nrm((N_EVEN, MIX_HALF), 0.02),
        'b_alpha_up': nrm((N_EVEN, GLA_GATE_RANK, GLA_KEY), GLA_GATE_RANK ** -0.5),
        'b_alpha_bias': nrm((N_EVEN, GLA_KEY), 0.5),
        'b_norm_gain': 1.0 + nrm((N_EVEN, GLA_DV), 0.05),
        'c_lb': nrm((DEPTH, HGRN_KEY), 0.5),
        'c_norm_gain': 1.0 + nrm((N_ODD, HGRN_DV), 0.05),
        'd_conv_w': nrm((N_ODD, SSD_CONV, SSD_XBC), SSD_CONV ** -0.5),
        'd_conv_b': nrm((N_ODD, SSD_XBC), 0.02),
        'd_dt_bias': dt0 + jnp.log(-jnp.expm1(-dt0)),
        'd_a_log': jnp.log(unif((N_ODD, SSD_HEADS), 1.0, 16.0)),
        'd_skip': 1.0 + nrm((N_ODD, SSD_HEADS), 0.05),
        'd_norm_gain': 1.0 + nrm((N_ODD, MIX_HALF), 0.05),
        'w_router': nrm((D_MODEL, N_EXPERTS), D_MODEL ** -0.5),
        'router_bias': nrm((N_EXPERTS,), 0.01),
        'w_gate': nrm((DEPTH, N_EXPERTS, D_MODEL, D_EXPERT), D_MODEL ** -0.5),
        'w_up': nrm((DEPTH, N_EXPERTS, D_MODEL, D_EXPERT), D_MODEL ** -0.5),
        'w_down': nrm((DEPTH, N_EXPERTS, D_EXPERT, D_MODEL), D_EXPERT ** -0.5),
        'final_gain': 1.0 + nrm((D_MODEL,), 0.05),
    }

def reference(x, c, norm_gain, w_ada, b_ada, w_in_even, w_in_odd, w_out,
              a_mu, a_w0, a_w_up, a_a0, a_a_up, a_g_up, a_k_k, a_k_a, a_r_k, a_ln_gain, a_ln_bias,
              b_alpha_up, b_alpha_bias, b_norm_gain, c_lb, c_norm_gain,
              d_conv_w, d_conv_b, d_dt_bias, d_a_log, d_skip, d_norm_gain,
              w_router, router_bias, w_gate, w_up, w_down, final_gain):
    lower_bounds = hgrn_lower_bounds(c_lb)
    cond = jax.nn.silu(c)
    for l in range(DEPTH):
        j = l // 2
        mod = cond @ w_ada[l] + b_ada[l]
        sh_m, sc_m, g_m, sh_f, sc_f, g_f = [m[:, None, :] for m in jnp.split(mod, 6, axis=-1)]
        h = rms_norm(x, norm_gain[l, 0]) * (1.0 + sc_m) + sh_m
        if l % 2 == 0:
            ua, ub = split_cols(h @ w_in_even[j], [RWKV_IN, GLA_IN])
            y_first = rwkv7_group(ua, a_mu[j], a_w0[j], a_w_up[j], a_a0[j], a_a_up[j], a_g_up[j],
                                  a_k_k[j], a_k_a[j], a_r_k[j], a_ln_gain[j], a_ln_bias[j])
            y_second = gla_group(ub, b_alpha_up[j], b_alpha_bias[j], b_norm_gain[j])
        else:
            uc, ud = split_cols(h @ w_in_odd[j], [HGRN_IN, SSD_IN])
            y_first = hgrn2_group(uc, lower_bounds[l], c_norm_gain[j])
            y_second = ssd_group(ud, d_conv_w[j], d_conv_b[j], d_dt_bias[j], d_a_log[j], d_skip[j], d_norm_gain[j])
        x = x + g_m * (jnp.concatenate([y_first, y_second], axis=-1) @ w_out[l])
        h = rms_norm(x, norm_gain[l, 1]) * (1.0 + sc_f) + sh_f
        x = x + g_f * grouped_moe(h, w_router, router_bias, w_gate[l], w_up[l], w_down[l])
    return rms_norm(x, final_gain)


_drawn_inputs = setup_inputs


def setup_inputs(seed=0):
    import zlib

    import numpy as np

    out = dict(_drawn_inputs(seed))
    spreads = {}
    factors = {'a_k_k': 5.539,
     'a_ln_bias': 3.963,
     'c_norm_gain': 3.399,
     'd_conv_b': 4.907,
     'd_skip': 4.042,
     'd_norm_gain': 3.048}
    for name, (base, spread) in spreads.items():
        noise = np.random.default_rng([zlib.crc32(name.encode()), seed]).standard_normal(out[name].shape)
        drawn = base * np.exp(spread * noise) if base else spread * noise
        out[name] = jnp.asarray(drawn.astype(out[name].dtype))
    for name, factor in factors.items():
        out[name] = (out[name] * factor).astype(out[name].dtype)
    return out
```

```python
from contextlib import ExitStack

import concourse.bass as bass
from concourse import mybir

F32 = mybir.dt.float32
I32 = mybir.dt.int32
ALU = mybir.AluOpType
ACT = mybir.ActivationFunctionType
AX_X = mybir.AxisListType.X

P = 128
D = 1024
T = 512
KD = D // P
NT = T // P
DEPTH = 2
EPS = 1e-6
HALF = D // 2
RW = 0.6065306597126334
RW_CHUNK = 64
GN_EPS = 64e-5
E = 16
GRP = 4
FE = 512
MAX_BLOCKS = 24
BIG = 1e30
RING = 3
SLOT = 8 * 512

ROWS1 = [("a_mu", 14), ("a_w0", 4), ("a_a0", 4), ("a_k_k", 4), ("a_k_a", 4), ("a_r_k", 4), ("a_ln_gain", 4),
         ("a_ln_bias", 4), ("b_alpha_bias", 2), ("b_norm_gain", 1), ("c_lb", 4), ("c_norm_gain", 1),
         ("d_conv_w", 24), ("d_conv_b", 6), ("d_norm_gain", 4), ("final_gain", 8), ("c", 8)]
ROWS2 = [("b_ada", 96), ("norm_gain", 32)]


def columns():
    at = {}
    for tile, rows in enumerate((ROWS1, ROWS2)):
        c = 0
        for name, n in rows:
            at[name] = (tile, c)
            c += n
    return at


def chunk_plan():
    plan = [("ada", 0, i) for i in range(12)] + [("in", 0, i) for i in range(7)] + [("ada", 1, i) for i in range(12)]
    plan += [("out", 0, i) for i in range(2)]
    plan += [("in", 1, i) for i in range(6)] + [("out", 1, i) for i in range(2)]
    return plan


IN_PIECES = [
    [[(0, 512)], [(512, 512)], [(1024, 512)], [(1536, 512)], [(2048, 256), (2816, 16)], [(2304, 512)], [(2832, 512)]],
    [[(0, 512)], [(512, 512)], [(1024, 512)], [(1536, 512)], [(2048, 512)], [(2560, 264)]],
]


def zone(tensor, start, end):
    place = [start]

    def take(*shape):
        n = 1
        for size in shape:
            n *= size
        ap = tensor[:, place[0]:place[0] + n]
        place[0] += n
        assert place[0] <= end
        if len(shape) == 2:
            ap = ap.rearrange("p (a b) -> p a b", b=shape[1])
        if len(shape) == 3:
            ap = ap.rearrange("p (a b c) -> p a b c", b=shape[1], c=shape[2])
        return ap

    return take, place


def bc(ap, n, at):
    u = ap.unsqueeze(at)
    shape = list(u.shape)
    shape[at] = n
    return u.to_broadcast(shape)


def trunk(nc, A, out):
    h_dram = nc.dram_tensor("h_rows", [T, D], F32, kind="Internal").ap()
    y_dram = nc.dram_tensor("expert_rows", [MAX_BLOCKS * P, D], F32, kind="Internal").ap()
    COL = columns()
    PLAN = chunk_plan()

    with ExitStack() as ctx:
        def sb(name, cols, dt=F32):
            return ctx.enter_context(nc.sbuf_tensor(name, [P, cols], dt))

        made = {}

        def sem(name):
            if name not in made:
                made[name] = ctx.enter_context(nc.semaphore(name))
            return made[name]

        PS = ctx.enter_context(nc.psum_tensor("banks", [P, 8, 512], F32))

        ring = sb("ring", RING * SLOT)
        xT_ = sb("x_features", KD * T)
        xT = xT_[:, :].rearrange("p (k t) -> p k t", t=T)
        h_ = sb("h_features", KD * T)
        h = h_[:, :].rearrange("p (k t) -> p k t", t=T)
        y_ = sb("y_features", KD * T)
        y = y_[:, :].rearrange("p (k t) -> p k t", t=T)
        work = sb("work", 20992)
        KEEP = 7168

        cst, _ = zone(sb("constants", 128 * 19 + 1024), 0, 128 * 19 + 1024)
        ident = cst(P)
        ones = cst(P)
        upper = cst(P)
        headones = cst(P)
        strict_up = cst(P)
        strict_lo = cst(P)
        incl_up = cst(P)
        LV = [1, 2, 4, 8, 16, 32, 64]
        lev_up = {hh: cst(P) for hh in LV}
        lev_lo = {hh: cst(P) for hh in LV[:5]}
        reset64 = cst(T)
        reset128 = cst(T)

        small, _ = zone(sb("small", 3608), 0, 3608)
        prm = small(2, P)
        mod = small(2, 48)
        amul = small(2, 2, 8)
        cond = small(8)
        wup = small(512)
        gup = small(512)
        alup = small(256)
        wr = small(8, E)
        rs = work[:, 20480:20992]
        acc = small(2, 512)
        negw0 = small(4)
        nega0 = small(4)
        nabias = small(2)
        omu = small(14)
        lb = small(2)
        omlb = small(2)
        lbt = small(12)
        dtb = small(8)
        alog = small(8)
        skipc = small(4)
        rbias = small(E)
        iota16 = small(E)
        iota24 = small(MAX_BLOCKS)
        iota128 = small(P)
        tokid = small(NT)
        pidx = small(1)
        epsc = small(4)
        ebl = small(2, NT)
        lsum = small(8)
        idx_tok = sb("idx_tok", MAX_BLOCKS + 2, I32)
        scratch_i = sb("scratch_ints", P, I32)
        idx_cur = sb("idx_cur", 2, I32)
        idx_dest = sb("idx_dest", 2 * NT, I32)
        table = sb("block_experts", 32, I32)

        def prm_col(name, i=0, n=1):
            tile, c = COL[name]
            return prm[:, tile, c + i:c + i + n]

        def slot(n, cols):
            s = n % RING
            return ring[:, s * SLOT:s * SLOT + 8 * cols].rearrange("p (k n) -> p k n", n=cols)

        def slot_w(kind, l, i):
            if kind == "in":
                return sum(w for _, w in IN_PIECES[l][i])
            return 512

        where = {c: n for n, c in enumerate(PLAN) if c is not None}

        slot_loaded = [sem(f"slot{i}_loaded") for i in range(RING)]

        def arrived(eng, key):
            n = where[key]
            eng.wait_ge(slot_loaded[n % RING], 16 * (n // RING + 1))

        def ring_ap(key):
            n = where[key]
            return slot(n, slot_w(*key))

        def w_src(key):
            kind, l, i = key
            if kind == "ada":
                return A["w_ada"][l].rearrange("(k p) n -> p k n", p=P)[:, :, i * 512:(i + 1) * 512]
            if kind == "out":
                return A["w_out"][l].rearrange("(k p) n -> p k n", p=P)[:, :, i * 512:(i + 1) * 512]
            w = (A["w_in_even"], A["w_in_odd"])[l][0].rearrange("(k p) n -> p k n", p=P)
            c, n = IN_PIECES[l][i][0]
            return w[:, :, c:c + n]

        ring2 = [work[:, 4096 * i:4096 * (i + 1)] for i in range(3)]
        mo, mo_at = zone(work, 3 * 4096, 20992)
        xg = mo(2, D)
        xTb = mo(8, P)
        sgt = mo(FE)
        actb = mo(FE)
        aT = mo(4, P)
        yb = mo(D)
        ro, _ = zone(work, mo_at[0], 20480)
        moe_w = []
        for j in range(2):
            base = [ring[:, s * SLOT:s * SLOT + 4096] for s in range(3)] if j == 0 else ring2
            moe_w.append((base[0].rearrange("p (k n) -> p k n", n=512), base[1].rearrange("p (k n) -> p k n", n=512),
                          base[2].rearrange("p (k n) -> p k n", n=1024)))

        cg = zone(work, 0, 3 * 4096)[0](4, D)

        sc = ro(NT, E)
        sel = ro(NT, E)
        r1 = ro(NT, 8)
        r2 = ro(NT, 8)
        gs = ro(NT, GRP)
        gm = ro(NT, GRP)
        m1 = ro(NT)
        idc = ro(NT, E)
        oh = ro(2, NT * E)
        both = ro(NT, E)
        gk = ro(2, NT)
        gsum = ro(NT)
        rank = ro(NT, E)
        cnt = ro(E)
        nov = ro(E)
        ove = ro(E)
        over = ro(E)
        qq = ro(NT, E)
        q0 = ro(NT, E)
        blk = ro(NT, E)
        rin = ro(NT, E)
        selb = ro(2, NT)
        selr = ro(2, NT)
        destf = ro(2, NT)
        ohb = ro(MAX_BLOCKS)
        ohr = ro(P)
        tabf = ro(32)

        la, la_at = zone(work, KEEP, 20992)
        lq = la(2, T)
        lk = la(2, T)
        lg = la(2, T)
        lv = la(NT, 512)
        lgate = la(4, T)
        lqp = la(4, T)
        lkp = la(2, T)
        lA = la(16, P)
        le = la(1024)
        lS = la(2, P)

        kz, _ = zone(work, 0, KEEP)
        rr = kz(4, T)
        kk_ = kz(4, T)
        vv = kz(4, T)
        wad = kz(T)
        gdp = kz(T)
        rz, rz_at = zone(work, KEEP, 20992)
        LKT = rz(8, P)
        PKT = rz(8, P)
        PBT = rz(8, P)
        Gm = rz(8, P)
        G2 = rz(8, P)
        uz, _ = zone(work, rz_at[0] - 2048, rz_at[0])
        R0 = uz(512)
        Un = uz(512)
        U0 = uz(512)
        WnT = uz(4, P)
        t_sg = rz(4, P)
        t_cs = rz(4, P)
        t_eb = rz(4, P)
        t_a = rz(4, P)
        t_kk = rz(4, P)
        t_kt = rz(4, P)
        t_ka = rz(4, P)
        t_be = rz(4, P)
        t_1 = rz(4, P)
        alp = rz(8, P)
        rho = rz(8, P)
        Vt = rz(512)
        kaT = rz(512)
        beT = rz(512)
        alT = rz(512)
        XT = h_[:, 0:1024].rearrange("p (a b) -> p a b", b=P)
        X = h_[:, 1024:2048].rearrange("p (a b) -> p a b", b=P)
        Tm = h_[:, 2048:3072].rearrange("p (a b) -> p a b", b=P)
        TT = h_[:, 3072:4096].rearrange("p (a b) -> p a b", b=P)
        ST = small(8, 64)

        sz, _ = zone(work, 0, KEEP)
        zs = sz(4, T)
        xsF = sz(4, T)
        Bf = sz(T)
        Cp = sz(2, T)
        dt = sz(NT, 8)
        da = sz(NT, 8)
        dz = sz(NT, 8)
        dz2 = sz(NT, 8)
        dpl = sz(NT, 8)
        cumc = sz(NT, 8)
        dte = sz(8)
        sw, _ = zone(work, KEEP, 20992)
        cva = lA[:, 0:4, :].rearrange("p a b -> p (a b)")
        cve = lA[:, 4:8, :].rearrange("p a b -> p (a b)")
        xsT = sw(NT, 512)
        Bt = sw(NT, P)
        Es = sw(8, P)
        MT = sw(8, P)
        ec = sw(8, P)
        Csp = sw(8, P)
        xdt = sw(512)
        xdd = sw(512)
        CBm = sw(2, P)
        Sst = sw(4, 64)
        Stm = sw(4, 64)
        yF = sw(4, T)

        def pairs_of(eng, l):
            return eng.value_load(table[0:1, 30 + l:31 + l], min_val=8, max_val=MAX_BLOCKS // 2)

        def further_pairs(eng, l):
            return eng.value_load(table[0:1, 26 + l:27 + l], min_val=7, max_val=MAX_BLOCKS // 2 - 1)

        PARTS = ("gate", "up", "down")
        w_loaded = [[sem(f"l{l}_{w}_{j}_loaded") for j in ("even", "odd") for w in PARTS]
                    for l in range(DEPTH)]
        gathered = [[sem(f"l{l}_{j}_rows_gathered") for j in ("even", "odd")] for l in range(DEPTH)]

        BLOCKS = [
            [(0, 128 * j, 128, "shift", j) for j in range(4)] + [(1, 128 * j, 128, "shift", 4 + j) for j in range(4)]
            + [(2, 128 * j, 128, "shift", 8 + j) for j in range(4)]
            + [(3, 0, 128, "shift", 12), (3, 128, 128, "shift", 13), (3, 256, 128, "q", 0), (3, 384, 128, "q", 1)]
            + [(4, 0, 128, "k", 0), (4, 128, 128, "k", 1), (4, 256, 16, "lora", 0)]
            + [(5, 0, 512, "v", t) for t in range(NT)] + [(6, 128 * j, 128, "gate", j) for j in range(4)],
            [(0, 0, 128, "q", 0), (0, 128, 128, "q", 1), (0, 256, 128, "f", 0), (0, 384, 128, "f", 1)]
            + [(1, 0, 512, "v", t) for t in range(NT)] + [(2, 128 * j, 128, "gate", j) for j in range(4)]
            + [(3, 128 * j, 128, "z", j) for j in range(4)] + [(4, 128 * j, 128, "conv", j) for j in range(4)]
            + [(5, 0, 128, "conv", 4), (5, 128, 128, "conv", 5), (5, 256, 8, "dt", 0)],
        ]
        NB = [len(b) for b in BLOCKS]
        WITH_ACT = ("shift", "gate", "f", "z")

        def act_blocks(l, n):
            return sum(b[3] in WITH_ACT for b in BLOCKS[0][:NB[0] if l else n]) + \
                (sum(b[3] in WITH_ACT for b in BLOCKS[1][:n]) if l else 0)

        def chunk_blocks(l, i):
            return l * NB[0] + sum(b[0] <= i for b in BLOCKS[l])

        shifted = [rr[:, j, :] for j in range(4)] + [kk_[:, j, :] for j in range(4)] \
            + [vv[:, j, :] for j in range(4)] + [wad, gdp]
        lgf = lg.rearrange("p t s -> p (t s)")
        lev_n = len(LV)

        def halves(ap, hh):
            v = ap.rearrange("p (n two h) -> p n two h", two=2, h=hh)
            return v[:, :, 0, :], v[:, :, 1, :]

        def x_at(n, k):
            return [k + 1, 8 + k + 1, 17, 17 + k + 1, 26][n]

        def ada_chunks(eng, link, l):
            for i in range(12):
                arrived(eng, ("ada", l, i))
                if i >= 2 or l:
                    eng.wait_ge(sem("ada_summed"), 12 * l + i - 1)
                w = ring_ap(("ada", l, i))
                a = acc[:, i % 2, :]
                if l == 0:
                    link(eng.tensor_scalar(a, w[:, 0, :], cond[:, 0:1], None, ALU.mult))
                    for k in range(1, KD):
                        ins = eng.scalar_tensor_tensor(out=a, in0=w[:, k, :], scalar=cond[:, k:k + 1], in1=a,
                                                       op0=ALU.mult, op1=ALU.add)
                        if k < KD - 1:
                            link(ins)
                else:
                    link(eng.tensor_tensor(w, w, cond.unsqueeze(2).to_broadcast([P, KD, 512]), ALU.mult))
                    link(eng.tensor_tensor(w[:, 0:4, :], w[:, 0:4, :], w[:, 4:8, :], ALU.add))
                    link(eng.tensor_tensor(w[:, 0:2, :], w[:, 0:2, :], w[:, 2:4, :], ALU.add))
                    ins = eng.tensor_tensor(a, w[:, 0, :], w[:, 1, :], ALU.add)
                ins.then_inc(sem("ada_used"), 1)

        block = ctx.enter_context(nc.Block())

        @block.sync
        def _(sp):
            def rows_of(name):
                a = A[name]
                names = "a b c d"[:2 * len(a.shape) - 1]
                flat = a.rearrange(f"{names} -> ({names})") if len(a.shape) > 1 else a
                return flat.rearrange("(r c) -> r c", c=P)

            for tile, rows in enumerate((ROWS1, ROWS2)):
                c = 0
                for name, k in rows:
                    sp.dma_start(work[c:c + k, 4096 + tile * P:4096 + (tile + 1) * P],
                                 rows_of(name)).then_inc(sem("rows_loaded"), 16)
                    c += k
            sp.dma_start(work[:, 0:4096].rearrange("p (a d) -> p a d", d=D),
                         A["x"][0].rearrange("(a p) d -> p a d", p=P)).then_inc(sem("x_loaded"), 16)

            def load(n):
                if n >= RING:
                    kind, l, i = PLAN[n - RING]
                    if kind == "ada":
                        sp.wait_ge(sem("ada_used"), 12 * l + i + 1)
                    elif kind == "in":
                        sp.wait_ge(sem("proj_done"), chunk_blocks(l, i))
                    else:
                        sp.wait_ge(sem("outproj_done"), 8 * l + 4 * (i + 1))
                kind, l, i = PLAN[n]
                dst, src = ring_ap(PLAN[n]), w_src(PLAN[n])
                if kind == "in" and len(IN_PIECES[l][i]) == 2:
                    (_, w), (c2, w2) = IN_PIECES[l][i]
                    sp.dma_start(dst[:, :, w:w + w2], A["w_in_even"][0].rearrange("(k p) n -> p k n", p=P)
                                 [:, :, c2:c2 + w2]).then_inc(sem("second_piece_loaded"), 16)
                    dst = dst[:, :, 0:w]
                sp.dma_start(dst, src).then_inc(slot_loaded[n % RING], 16)

            ws = [A["w_gate"], A["w_up"], A["w_down"]]
            n = 0
            for l in range(DEPTH):
                while n < len(PLAN) and PLAN[n][1] <= (1 if PLAN[n][0] == "ada" else l):
                    load(n)
                    n += 1
                sp.wait_ge(sem("outproj_done"), 8 * (l + 1))
                sp.wait_ge(sem("x_ready"), 8 + 9 * l + 1)
                for j in range(2):
                    for i in range(3):
                        sp.dma_start(moe_w[j][i], ws[i][l, j].rearrange("(k p) n -> p k n", p=P))\
                          .then_inc(w_loaded[l][3 * j + i], 16)
                sp.wait_ge(sem("table_ready"), l + 1)
                further = further_pairs(sp, l)
                with sp.Fori(0, further) as it:
                    for j in range(2):
                        e = sp.value_load(table[0:1, bass.ds(it * 2 + (j + 2), 1)], min_val=0, max_val=E - 1)
                        for i in range(3):
                            sp.wait_ge(sem(f"l{l}_{PARTS[i]}_done"), it * 2 + (j + 1))
                            src = ws[i][l][bass.ds(e, 1)].rearrange("o (k p) n -> p (o k) n", p=P)
                            sp.dma_start(moe_w[j][i], src).then_inc(w_loaded[l][3 * j + i], 16)
                sp.wait_ge(sem(f"l{l}_down_done"), further * 2 + 2)
                sp.sem_inc(sem("sync_passed"), 1)

        @block.gpsimd
        def _(pool):
            steps = [0]

            def link(ins):
                steps[0] += 1
                ins.then_inc(sem("pool_order"), 1)
                pool.wait_ge(sem("pool_order"), steps[0])

            def fill(ap, value):
                link(pool.memset(ap, value))

            def keep_where(ap, base, pattern, mult, cmp=ALU.is_ge, fill_value=0.0):
                link(pool.affine_select(out=ap, in_=ap, compare_op=cmp, fill=fill_value, base=base,
                                        pattern=pattern, channel_multiplier=mult))

            fill(ident, 0.0)
            keep_where(ident, 0, [[-1, P]], 1, ALU.not_equal, 1.0)
            fill(epsc[:, 0:1], EPS)
            fill(epsc[:, 1:2], GN_EPS)
            fill(epsc[:, 2:3], 1e-12)
            fill(epsc[:, 3:4], 1.0)
            pool.memset(ones, 1.0).then_inc(sem("pool_const"), 1)
            fill(upper, 1.0)
            keep_where(upper, 0, [[1, P]], -1)
            fill(headones, 1.0)
            hv = headones.rearrange("p (n h) -> p n h", h=64)
            keep_where(hv, 0, [[-64, 2], [0, 64]], 1)
            keep_where(hv, 63, [[64, 2], [0, 64]], -1)
            for m, base, step, mult in ((strict_up, -1, 1, -1), (incl_up, 0, 1, -1), (strict_lo, -1, -1, 1)):
                link(pool.tensor_copy(m, headones))
                keep_where(m, base, [[step, P]], mult)
            for hh in LV:
                for m, half, lo in ((lev_up.get(hh), 1, 0), (lev_lo.get(hh), 0, hh)):
                    if m is None:
                        continue
                    fill(m, 0.0)
                    v = m.rearrange("p (n two h) -> p n two h", two=2, h=hh)[:, :, half, :]
                    nb = P // (2 * hh)
                    fill(v, 1.0)
                    keep_where(v, -lo, [[-2 * hh, nb], [0, hh]], 1)
                    keep_where(v, lo + hh - 1, [[2 * hh, nb], [0, hh]], -1)
            for m, c in ((reset64, 64), (reset128, 128)):
                fill(m, 1.0)
                fill(m.rearrange("p (n c) -> p n c", c=c)[:, :, 0:1], 0.0)
            for ap, n, mult in ((iota16, E, 0), (iota24, MAX_BLOCKS, 0), (iota128, P, 0), (pidx, 1, 1)):
                link(pool.iota(scratch_i[:, 0:n], pattern=[[1, n]], base=0, channel_multiplier=mult))
                link(pool.tensor_copy(ap, scratch_i[:, 0:n]))
            link(pool.iota(scratch_i[:, 0:NT], pattern=[[P, NT]], base=0, channel_multiplier=1))
            link(pool.tensor_copy(tokid, scratch_i[:, 0:NT]))
            pool.memset(idx_tok[:, :], 0).then_inc(sem("pool_const"), 1)

            pool.wait_ge(sem("setup_step"), 1)
            ada_chunks(pool, link, 1)

            for l in range(DEPTH):
                pool.wait_ge(sem("table_ready"), l + 1)
                pool.wait_ge(sem(f"l{l}_rows_stored"), 16)
                further = further_pairs(pool, l)
                sg, sc_ = sem(f"l{l}_xt_turned"), sem(f"l{l}_idx_copied")

                def gather(b, j, it_wait, n):
                    if it_wait is not None:
                        pool.wait_ge(sg, it_wait)
                    pool.tensor_copy(idx_cur[:, j:j + 1], idx_tok[:, b]).then_inc(sc_, 1)
                    pool.wait_ge(sc_, n)
                    pool.sem_inc(sem("pool_passed"), 1)
                    pool.indirect_dma_start(
                        xg[:, j, :], None, h_dram, bass.IndirectOffsetOnAxis(ap=idx_cur[:, j:j + 1], axis=0))\
                        .then_inc(gathered[l][j], 16)

                gather(bass.ds(0, 1), 0, None, 1)
                gather(bass.ds(1, 1), 1, None, 2)
                with pool.Fori(0, further) as it:
                    for j in range(2):
                        gather(bass.ds(it * 2 + (j + 2), 1), j, it * 2 + (j + 1), it * 2 + (j + 3))
                gather(bass.ds(further * 2 + 2, 1), 0, further * 2 + 1, further * 2 + 3)

                pool.wait_ge(sem(f"l{l}_rows_stored"), (further * 2 + 3) * 16)
                pool.sem_inc(sem("pool_passed"), 1)
                for t in range(NT):
                    if t >= 2:
                        pool.wait_ge(sem("comb_turned"), NT * l + t - 1)
                    for k in range(2):
                        pool.indirect_dma_start(
                            cg[:, (t % 2) * 2 + k, :], None, y_dram,
                            bass.IndirectOffsetOnAxis(ap=idx_dest[:, k * NT + t:k * NT + t + 1], axis=0))\
                            .then_inc(sem(f"expert_rows{t % 2}"), 16)

        @block.scalar
        def _(act):
            steps = [0]

            def link(ins):
                steps[0] += 1
                ins.then_inc(sem("act_order"), 1)
                act.wait_ge(sem("act_order"), steps[0])

            act.dma_start(wup[0:64, :], A["a_w_up"][0]).then_inc(sem("params_loaded"), 16)
            act.dma_start(wup[64:128, :], A["a_a_up"][0]).then_inc(sem("params_loaded"), 16)
            act.dma_start(gup, A["a_g_up"][0]).then_inc(sem("params_loaded"), 16)
            act.dma_start(alup[0:16, :], A["b_alpha_up"][0]).then_inc(sem("params_loaded"), 16)
            act.dma_start(wr, A["w_router"].rearrange("(k p) e -> p k e", p=P)).then_inc(sem("params_loaded"), 16)
            act.dma_start(dtb, A["d_dt_bias"].to_broadcast([P, 8])).then_inc(sem("params_loaded"), 16)
            act.dma_start(alog, A["d_a_log"].to_broadcast([P, 8])).then_inc(sem("params_loaded"), 16)
            act.dma_start(rbias, A["router_bias"].unsqueeze(0).to_broadcast([P, E])).then_inc(sem("params_loaded"), 16)
            act.dma_start(rs[:, 0:8], A["d_skip"].to_broadcast([P, 8])).then_inc(sem("params_loaded"), 16)

            act.wait_ge(sem("zeros_ready"), 1)
            act.dma_start(y_dram[E * P:, :].rearrange("(b p) d -> p b d", p=P), bc(y_[:, 0:D], MAX_BLOCKS - E, 1))\
               .then_inc(sem("rows_cleared"), 16)

            act.wait_ge(sem("params_ready"), 1)
            act.activation(cond, prm_col("c", 0, 8), ACT.Exp, scale=-1.0).then_inc(sem("setup_exp"), 1)

            act.wait_ge(sem("setup_step"), 2)
            act.activation(lbt[:, 4:8], lbt[:, 4:8], ACT.Exp).then_inc(sem("setup_exp"), 1)

            def norm(n):
                l, place = n // 2, n % 2
                for k in range(KD):
                    act.wait_ge(sem("x_ready"), x_at(n, k))
                    act.activation(h[:, k, :], xT[:, k, :], ACT.Square).then_inc(sem("sq_ready"), 1)
                act.wait_ge(sem("ms_ready"), n + 1)
                link(act.activation(rs, PS[:, 7, :], ACT.Ln, bias=epsc[:, 0:1], scale=1.0 / D))
                act.activation(rs, rs, ACT.Exp, scale=-0.5).then_inc(sem("rstd_ready"), 1)
                if n < 4:
                    act.wait_ge(sem("amul_ready"), l + 1)
                for k in range(KD):
                    act.wait_ge(sem("xn_ready"), KD * n + k + 1)
                    if n < 4:
                        act.activation(h[:, k, :], h[:, k, :], ACT.Identity, scale=amul[:, l, place, k:k + 1],
                                       bias=mod[:, l, 24 * place + k:24 * place + k + 1]).then_inc(sem("h_ready"), 1)
                    else:
                        act.activation(h[:, k, :], h[:, k, :], ACT.Copy, scale=prm_col("final_gain", k))\
                           .then_inc(sem("h_ready"), 1)

            def projections(l):
                for n, (c, c0, w, kind, j) in enumerate(BLOCKS[l]):
                    if kind not in WITH_ACT:
                        continue
                    act.wait_ge(sem("proj_done"), l * NB[0] + n + 1)
                    ps = PS[:, n % 4, :]
                    if kind == "shift":
                        ins = act.activation(shifted[j], ps, ACT.Copy, scale=omu[:, j:j + 1])
                    elif kind == "gate":
                        ins = act.activation(lgate[:, j, :], ps, ACT.Exp, scale=-1.0)
                    elif kind == "f":
                        ins = act.activation(lg[:, j, :], ps, ACT.Exp, scale=-1.0)
                    else:
                        ins = act.activation(zs[:, j, :], ps, ACT.Exp, scale=-1.0)
                    ins.then_inc(sem("proj_act"), 1)
                    if l == 1 and kind == "z" and j == 3:
                        for i in range(6):
                            act.wait_ge(sem("conv_sum"), i + 1)
                            act.activation(cve, cva, ACT.Exp, scale=-1.0).then_inc(sem("conv_exp"), 1)

            def linear_attention(l):
                if l == 0:
                    act.wait_ge(sem("log_pre"), 1)
                    link(act.activation(le, le, ACT.Exp))
                    act.activation(le, le, ACT.Ln, bias=epsc[:, 3:4]).then_inc(sem("log_done"), 1)
                else:
                    act.wait_ge(sem("log_pre"), 2)
                    act.activation(lgf, lgf, ACT.Ln).then_inc(sem("log_done"), 1)
                for n in range(lev_n):
                    act.wait_ge(sem("lev_diff"), lev_n * l + n + 1)
                    act.activation(le, le, ACT.Exp).then_inc(sem("lev_exp"), 1)
                act.wait_ge(sem("lev_ready"), (lev_n + 1) * (l + 1))
                act.activation(le, lgf, ACT.Exp).then_inc(sem("start_decay"), 1)
                act.wait_ge(sem("kd_diff"), l + 1)
                act.activation(le, le, ACT.Exp).then_inc(sem("end_decay"), 1)
                act.wait_ge(sem("o_ready"), l + 1)
                for hd in range(4):
                    act.activation(h[:, hd, :], PS[:, hd, :], ACT.Square).then_inc(sem("o_sq"), 1)
                for hd in range(4):
                    act.wait_ge(sem("o_ms"), 4 * l + hd + 1)
                    link(act.activation(h[:, 4 + hd, :], PS[:, 4 + hd % 2, :], ACT.Ln, bias=epsc[:, 0:1], scale=1.0 / P))
                    act.activation(h[:, 4 + hd, :], h[:, 4 + hd, :], ACT.Exp, scale=-0.5).then_inc(sem("o_rstd"), 1)

            def f2(ap):
                return ap.rearrange("p a b -> p (a b)")

            def rwkv():
                link(act.activation(wad[0:64, :], wad[0:64, :], ACT.Tanh))
                act.activation(gdp, gdp, ACT.Exp, scale=-1.0).then_inc(sem("setup_exp"), 1)
                act.wait_ge(sem("rows_cleared"), 16)
                for t in range(NT):
                    act.wait_ge(sem("lora_done"), t + 1)
                    for j in range(4):
                        act.activation(t_sg[:, j, :], PS[:, 0, j * P:(j + 1) * P], ACT.Exp, scale=-1.0,
                                       bias=negw0[:, j:j + 1])
                        ins = act.activation(t_a[:, j, :], PS[:, 1, j * P:(j + 1) * P], ACT.Exp, scale=-1.0,
                                             bias=nega0[:, j:j + 1])
                    ins.then_inc(sem("lora_exp"), 1)
                    link(act.activation(y[:, 0:4, t * P:(t + 1) * P], PS[:, 2, :].rearrange("p (a b) -> p a b", b=P),
                                        ACT.Copy))
                    act.wait_ge(sem("cs_ready"), t + 1)
                    act.activation(t_eb, t_cs, ACT.Exp, scale=-RW)
                    link(act.activation(t_sg, t_sg, ACT.Exp, scale=-RW))
                    act.activation(t_cs, t_cs, ACT.Exp, scale=RW).then_inc(sem("decays_ready"), 1)
                    act.wait_ge(sem("kk_ss"), t + 1)
                    link(act.activation(f2(t_1), PS[:, 3, :], ACT.Ln, bias=epsc[:, 2:3]))
                    act.activation(t_1, t_1, ACT.Exp, scale=-0.5).then_inc(sem("kk_rn"), 1)
                    act.wait_ge(sem("turns"), t + 1)
                    for i, dst in enumerate((Vt, kaT, beT)):
                        act.activation(dst, PS[:, i, :], ACT.Copy)
                    act.activation(alT, PS[:, 4, :], ACT.Copy).then_inc(sem("turned"), 1)
                    for n in range(9):
                        act.wait_ge(sem("g_ready"), 9 * t + n + 1)
                        dst, b = ((Gm, 0), (G2, 2))[n % 2] if n < 8 else (G2, 2)
                        act.activation(dst, PS[:, b:b + 2, :].rearrange("p a (b c) -> p (a b) c", c=P), ACT.Copy)\
                           .then_inc(sem("g_copied"), 1)
                    act.wait_ge(sem("rw_ready"), 2 * t + 1)
                    act.activation(R0, PS[:, 2, :], ACT.Copy)
                    act.activation(f2(WnT), PS[:, 3, :], ACT.Copy).then_inc(sem("rw_copied"), 1)
                    act.wait_ge(sem("rw_ready"), 2 * t + 2)
                    act.activation(U0, PS[:, 4, :], ACT.Copy).then_inc(sem("rw_copied"), 1)
                    act.wait_ge(sem("y1_ready"), t + 1)
                    act.activation(f2(t_sg), PS[:, 6, :], ACT.Copy).then_inc(sem("ys_copied"), 1)
                    act.wait_ge(sem("gn_sum"), 2 * t + 2)
                    link(act.activation(f2(t_eb), PS[:, 1, :], ACT.Ln, bias=epsc[:, 1:2], scale=1.0 / 64))
                    act.activation(t_eb, t_eb, ACT.Exp, scale=-0.5).then_inc(sem("gn_rstd"), 1)
                    act.wait_ge(sem("rwkv_done"), t + 1)

            def ssd():
                act.wait_ge(sem("setup_step"), 4)
                act.activation(dz, dz, ACT.Exp)
                act.activation(alog, alog, ACT.Exp).then_inc(sem("setup_exp"), 1)
                for t in range(NT):
                    act.wait_ge(sem("seg_diff"), t + 1)
                    act.activation(Es, Es, ACT.Exp).then_inc(sem("seg_exp"), 1)
                    act.activation(ec, PS[:, 2:4, :].rearrange("p a (b c) -> p (a b) c", c=P), ACT.Exp)
                    act.activation(dte, dte, ACT.Exp).then_inc(sem("seg_exp"), 1)
                act.wait_ge(sem("yz_ready"), 1)
                for j in range(4):
                    act.activation(xsT[:, j, :], yF[:, j, :], ACT.Square).then_inc(sem("o_sq"), 1)
                for g in range(2):
                    act.wait_ge(sem("o_ms"), 8 + g + 1)
                    dst = Es if g == 0 else MT
                    half = f2(dst)[:, 0:512]
                    link(act.activation(half, PS[:, g, :], ACT.Ln, bias=epsc[:, 0:1], scale=1.0 / 256))
                    act.activation(half, half, ACT.Exp, scale=-0.5).then_inc(sem("o_rstd"), 1)

            def experts(l):
                for t in range(NT):
                    act.wait_ge(sem("ht_ready"), NT * l + t + 1)
                    b = 2 * (t % 2)
                    act.activation(y_[:, t * D:(t + 1) * D], PS[:, b:b + 2, :].rearrange("p a b -> p (a b)"), ACT.Copy)\
                       .then_inc(sem("ht_copied"), 1)
                act.wait_ge(sem("ht_copied"), NT * (l + 1))
                row_dma = sem(f"l{l}_rows_stored")
                act.dma_start(h_dram.rearrange("(a p) d -> p a d", p=P),
                              y_[:, :].rearrange("p (a d) -> p a d", d=D)).then_inc(row_dma, 16)
                act.wait_ge(sem("logits_ready"), l + 1)
                act.activation(sc, PS[:, 4, 0:NT * E].rearrange("p (a b) -> p a b", b=E), ACT.Exp, scale=-1.0)\
                   .then_inc(sem("logits_exp"), 1)

                def x_copy(n):
                    act.wait_ge(sem(f"l{l}_xt_turned"), n)
                    act.activation(xTb, PS[:, 2:4, :].rearrange("p a (b c) -> p (a b) c", c=P), ACT.Copy)\
                       .then_inc(sem(f"l{l}_xt_copied"), 1)

                act.wait_ge(sem("table_ready"), l + 1)
                pairs = pairs_of(act, l)
                x_copy(1)
                with act.Fori(0, pairs) as it:
                    for j in range(2):
                        b1 = it * 2 + (j + 1)
                        act.wait_ge(sem(f"l{l}_gate_done"), b1)
                        act.activation(sgt, PS[:, 0, :], ACT.Exp, scale=-1.0).then_inc(sem(f"l{l}_gate_exp"), 1)
                        x_copy(b1 + 1)
                        act.wait_ge(sem(f"l{l}_down_done"), b1)
                        act.wait_ge(row_dma, b1 * 16)
                        act.activation(yb, PS[:, 5:7, :].rearrange("p a b -> p (a b)"), ACT.Copy)\
                           .then_inc(sem(f"l{l}_y_copied"), 1)
                        act.wait_ge(sem(f"l{l}_y_copied"), b1)
                        act.dma_start(y_dram[bass.ds((it * 2 + j) * P, P), :], yb).then_inc(row_dma, 16)

            norm(0)
            projections(0)
            linear_attention(0)
            rwkv()
            norm(1)
            experts(0)
            norm(2)
            projections(1)
            linear_attention(1)
            ssd()
            norm(3)
            experts(1)
            norm(4)
            for t in range(NT):
                act.wait_ge(sem("out_turned"), t + 1)
                b = 2 * (t % 2)
                act.activation(y_[:, t * D:(t + 1) * D], PS[:, b:b + 2, :].rearrange("p a b -> p (a b)"), ACT.Copy)\
                   .then_inc(sem("out_copied"), 1)
                act.wait_ge(sem("out_copied"), t + 1)
                act.dma_start(out[0, t * P:(t + 1) * P, :], y_[:, t * D:(t + 1) * D]).then_inc(sem("out_stored"), 16)
            act.wait_ge(sem("out_stored"), 16 * NT)

        @block.tensor
        def _(pe):
            mm = nc.tensor.matmul
            tr = nc.tensor.transpose

            pe.wait_ge(sem("rows_loaded"), 16 * (len(ROWS1) + len(ROWS2)))
            pe.wait_ge(sem("pool_const"), 1)
            n1 = sum(n for _, n in ROWS1)
            tr(PS[:, 0, 0:n1], work[0:n1, 4096:4096 + P], ident[0:n1, 0:n1])
            tr(PS[:, 0, P:2 * P], work[:, 4096 + P:4096 + 2 * P], ident).then_inc(sem("x_turned"), 1)
            pe.wait_ge(sem("x_loaded"), 16)
            for k in range(KD):
                if k >= 4:
                    pe.wait_ge(sem("x_ready"), k - 3)
                for t in range(NT):
                    ins = tr(PS[:, 1 + k % 4, t * P:(t + 1) * P], work[:, t * D + k * P:t * D + (k + 1) * P], ident)
                ins.then_inc(sem("x_turned"), 1)

            def ada_sums(l, i):
                pe.wait_ge(sem("ada_used"), 12 * l + i + 1)
                for j in range(4):
                    ins = mm(PS[:, 7, 4 * i + j:4 * i + j + 1], lhsT=acc[:, i % 2, j * P:(j + 1) * P],
                             rhs=ones[:, 0:1], start=True, stop=True)
                ins.then_inc(sem("ada_summed"), 1)

            def norm(n):
                if n in (0, 2):
                    pe.wait_ge(sem("amul_ready"), n // 2 + 1)
                for k in range(KD):
                    pe.wait_ge(sem("sq_ready"), KD * n + k + 1)
                    ins = mm(PS[:, 7, :], lhsT=ones, rhs=h[:, k, :], start=(k == 0), stop=(k == KD - 1))
                ins.then_inc(sem("ms_ready"), 1)

            def projections(l):
                last = -1
                for n, (c, c0, w, kind, j) in enumerate(BLOCKS[l]):
                    if c != last:
                        arrived(pe, ("in", l, c))
                        last = c
                    if kind == "lora":
                        pe.wait_ge(sem("second_piece_loaded"), 16)
                    if n == 0:
                        pe.wait_ge(sem("h_ready"), KD * 2 * l + KD)
                    if n >= 4:
                        pe.wait_ge(sem("proj_copied"), l * NB[0] + n - 3)
                    W = ring_ap(("in", l, c))
                    b = n % 4
                    if kind == "v":
                        for k in range(KD):
                            ins = mm(PS[:, b, :], lhsT=h[:, k, j * P:(j + 1) * P], rhs=W[:, k, 0:512],
                                     start=(k == 0), stop=(k == KD - 1))
                    elif kind == "dt":
                        for t in range(NT):
                            for k in range(KD):
                                ins = mm(PS[:, b, 8 * t:8 * t + 8], lhsT=h[:, k, t * P:(t + 1) * P],
                                         rhs=W[:, k, c0:c0 + 8], start=(k == 0), stop=(k == KD - 1))
                    else:
                        for k in range(KD):
                            ins = mm(PS[0:w, b, :], lhsT=W[:, k, c0:c0 + w], rhs=h[:, k, :],
                                     start=(k == 0), stop=(k == KD - 1))
                    ins.then_inc(sem("proj_done"), 1)

            def linear_attention(l):
                pe.wait_ge(sem("proj_copied"), NB[0] + l * NB[1])
                if l == 0:
                    for j in range(2):
                        ins = mm(PS[:, 4 + j, :], lhsT=alup[0:16, j * P:(j + 1) * P], rhs=le[0:16, 0:T],
                                 start=True, stop=True)
                    ins.then_inc(sem("alpha_ready"), 1)
                for n in range(lev_n + 1):
                    at = (lev_n + 1) * l + n
                    pe.wait_ge(sem("lev_ready"), at + 1)
                    if at:
                        pe.wait_ge(sem("lev_merged"), at)
                    for t in range(NT):
                        for hd in range(4):
                            ins = mm(PS[:, t, hd * P:(hd + 1) * P], lhsT=lkp[:, hd // 2, t * P:(t + 1) * P],
                                     rhs=lqp[:, hd, t * P:(t + 1) * P], start=True, stop=True)
                    ins.then_inc(sem("lev_scored"), 1)
                pe.wait_ge(sem("kd_ready"), l + 1)
                for t in range(NT):
                    for j in range(2):
                        ins = tr(PS[:, 4 + t // 2, (t % 2) * 256 + j * P:(t % 2) * 256 + (j + 1) * P],
                                 lkp[:, j, t * P:(t + 1) * P], ident)
                ins.then_inc(sem("kd_turned"), 1)
                pe.wait_ge(sem("lev_merged"), (lev_n + 1) * (l + 1))
                kdT = lq.rearrange("p a b -> p (a b)").rearrange("p (t c) -> p t c", c=256)
                for t in range(NT):
                    if t:
                        pe.wait_ge(sem("ls_ready"), 3 * l + t)
                    for hd in range(4):
                        o = PS[:, hd, t * P:(t + 1) * P]
                        ins = mm(o, lhsT=lv[:, t, hd * P:(hd + 1) * P], rhs=lA[:, 4 * t + hd, :],
                                 start=True, stop=(t == 0))
                        if t:
                            ins = mm(o, lhsT=lS[:, hd // 2, :], rhs=lqp[:, hd, t * P:(t + 1) * P],
                                     start=False, stop=True)
                    if t == NT - 1:
                        ins.then_inc(sem("o_ready"), 1)
                        break
                    if t == 0:
                        pe.wait_ge(sem("kdT_ready"), l + 1)
                    for hd in range(4):
                        p0 = 64 * (hd % 2)
                        ins = mm(PS[p0:p0 + 64, 6, (hd // 2) * P:(hd // 2 + 1) * P], lhsT=kdT[:, t, hd * 64:hd * 64 + 64],
                                 rhs=lv[:, t, hd * P:(hd + 1) * P], start=True, stop=True)
                    ins.then_inc(sem("ls_ps"), 1)
                for hd in range(4):
                    pe.wait_ge(sem("o_sq"), 4 * l + hd + 1)
                    if hd >= 2:
                        pe.wait_ge(sem("o_rstd"), 4 * l + hd - 1)
                    mm(PS[:, 4 + hd % 2, :], lhsT=ones, rhs=h[:, hd, :], start=True, stop=True).then_inc(sem("o_ms"), 1)

            def f2(ap):
                return ap.rearrange("p a b -> p (a b)")

            def rwkv():
                pe.wait_ge(sem("yhalf"), 1)
                pe.wait_ge(sem("setup_step"), 3)
                for t in range(NT):
                    ts = slice(t * P, (t + 1) * P)
                    if t:
                        pe.wait_ge(sem("rwkv_done"), t)
                    for j in range(4):
                        js = slice(j * P, (j + 1) * P)
                        mm(PS[:, 0, js], lhsT=wup[0:64, js], rhs=wad[0:64, ts], start=True, stop=True)
                    for j in range(4):
                        js = slice(j * P, (j + 1) * P)
                        mm(PS[:, 1, js], lhsT=wup[64:128, js], rhs=wad[64:128, ts], start=True, stop=True)
                    for j in range(4):
                        js = slice(j * P, (j + 1) * P)
                        ins = mm(PS[:, 2, js], lhsT=gup[:, js], rhs=gdp[:, ts], start=True, stop=True)
                    ins.then_inc(sem("lora_done"), 1)
                    pe.wait_ge(sem("kk_sq"), t + 1)
                    mm(PS[:, 3, :], lhsT=headones, rhs=f2(t_1), start=True, stop=True).then_inc(sem("kk_ss"), 1)
                    pe.wait_ge(sem("feat_ready"), t + 1)
                    mm(PS[:, 3, :], lhsT=headones, rhs=f2(t_1), start=True, stop=True).then_inc(sem("bonus_sum"), 1)
                    for b, src in ((0, vv[:, :, ts]), (1, t_ka), (2, t_be), (4, t_sg)):
                        for j in range(4):
                            ins = tr(PS[:, b, j * P:(j + 1) * P], src[:, j, :], ident)
                    ins.then_inc(sem("turns"), 1)
                    for n, (b, lhs, rhs, flip) in enumerate(((5, t_be, alp, 0), (0, t_be, alp, 1), (2, t_ka, alp, 0),
                                                             (5, t_ka, rho, 0), (0, t_be, rho, 0))):
                        if n == 1:
                            pe.wait_ge(sem("turned"), t + 1)
                        if n == 2:
                            pe.wait_ge(sem("bonus_used"), t + 1)
                        if n >= 3:
                            pe.wait_ge(sem("score_copied"), 5 * t + n - 2)
                        for hd in range(8):
                            o = PS[:, b + hd // 4, (hd % 4) * P:(hd % 4 + 1) * P]
                            left, right = lhs[:, hd // 2, :], rhs[:, hd, :]
                            if flip:
                                left, right = right, left
                            ins = mm(o, lhsT=left, rhs=right, start=True, stop=True)
                        ins.then_inc(sem("score_ready"), 1)

                    def heads(bank, lhs, rhs, name):
                        for hd in range(8):
                            o = PS[:, bank + hd // 4, (hd % 4) * P:(hd % 4 + 1) * P]
                            ins = mm(o, lhsT=lhs[:, hd, :], rhs=rhs[:, hd, :], start=True, stop=True)
                        ins.then_inc(sem(name), 1)

                    pe.wait_ge(sem("score_copied"), 5 * t + 5)
                    for n in range(5):
                        pe.wait_ge(sem("inv_ready"), 10 * t + 2 * n + 1)
                        if n < 4:
                            heads(0, XT, Tm, "g_ready")
                        heads(2, X, TT, "g_ready")
                        if n < 4:
                            pe.wait_ge(sem("g_copied"), 9 * t + 2 * n + 1)
                            heads(4, TT, Gm, "p_ready")
                        pe.wait_ge(sem("g_copied"), 9 * t + (2 * n + 2 if n < 4 else 9))
                        heads(0, Tm, G2, "p_ready")
                    pe.wait_ge(sem("inv_ready"), 10 * (t + 1))
                    for hd in range(8):
                        mm(PS[:, 2, hd * 64:hd * 64 + 64], lhsT=LKT[:, hd, :], rhs=Vt[:, hd * 64:hd * 64 + 64],
                           start=True, stop=True)
                    for hd in range(8):
                        p0 = 64 * (hd % 2)
                        ins = mm(PS[p0:p0 + 64, 3, (hd // 2) * P:(hd // 2 + 1) * P], lhsT=alT[:, hd * 64:hd * 64 + 64],
                                 rhs=TT[:, hd, :], start=True, stop=True)
                    ins.then_inc(sem("rw_ready"), 1)
                    pe.wait_ge(sem("rw_copied"), 2 * t + 1)
                    for hd in range(8):
                        ins = mm(PS[:, 4, hd * 64:hd * 64 + 64], lhsT=TT[:, hd, :], rhs=R0[:, hd * 64:hd * 64 + 64],
                                 start=True, stop=True)
                    ins.then_inc(sem("rw_ready"), 1)
                    pe.wait_ge(sem("rw_copied"), 2 * t + 2)
                    for c in range(2):
                        po = 64 * c
                        pe.wait_ge(sem("st_done"), 2 * t + c + 1)
                        for hd in range(8):
                            mm(PS[po:po + 64, 3, hd * 64:hd * 64 + 64], lhsT=WnT[:, hd // 2, po:po + 64],
                               rhs=ST[:, hd, :], start=True, stop=True)
                        for hd in range(8):
                            p0 = 64 * (hd % 2)
                            at = (hd // 2) * P + po
                            ins = mm(PS[p0:p0 + 64, 6, at:at + 64], lhsT=ST[:, hd, :], rhs=rho[:, hd, po:po + 64],
                                     start=True, stop=True)
                        ins.then_inc(sem("un_ready"), 1)
                        pe.wait_ge(sem("un_done"), 2 * t + c + 1)
                        for hd in range(8):
                            p0 = 64 * (hd % 2)
                            hs = slice(hd * 64, hd * 64 + 64)
                            o = PS[p0:p0 + 64, 4, (hd // 2) * 64:(hd // 2) * 64 + 64]
                            mm(o, lhsT=kaT[po:po + 64, hs], rhs=Vt[po:po + 64, hs], start=True, stop=False)
                            ins = mm(o, lhsT=beT[po:po + 64, hs], rhs=Un[po:po + 64, hs], start=False, stop=True)
                        ins.then_inc(sem("st_ps"), 1)
                    for hd in range(8):
                        p0 = 64 * (hd % 2)
                        hs = slice(hd * 64, hd * 64 + 64)
                        o = PS[p0:p0 + 64, 5, (hd // 2) * P:(hd // 2 + 1) * P]
                        mm(o, lhsT=Vt[:, hs], rhs=PKT[:, hd, :], start=True, stop=False)
                        ins = mm(o, lhsT=Un[:, hs], rhs=PBT[:, hd, :], start=False, stop=True)
                    ins.then_inc(sem("y1_ready"), 1)
                    for n, (b, src) in enumerate(((0, t_cs), (1, t_eb))):
                        pe.wait_ge(sem("gn_in"), 2 * t + n + 1)
                        mm(PS[:, b, :], lhsT=headones, rhs=f2(src), start=True, stop=True).then_inc(sem("gn_sum"), 1)
                    for i in range(3 * t, 3 * t + 3):
                        ada_sums(1, i)

            def ssd():
                pe.wait_ge(sem("yhalf"), 2)
                for t in range(NT):
                    for j in range(4):
                        tr(PS[:, t, j * P:(j + 1) * P], xsF[:, j, t * P:(t + 1) * P], ident)
                for t in range(NT):
                    ins = tr(PS[:, 4, t * P:(t + 1) * P], Bf[:, t * P:(t + 1) * P], ident)
                ins.then_inc(sem("xs_turned"), 1)
                pe.wait_ge(sem("da_ready"), 1)
                mm(PS[:, 5, 0:32], lhsT=upper, rhs=da.rearrange("p a b -> p (a b)"), start=True, stop=True)\
                    .then_inc(sem("xs_turned"), 1)
                pe.wait_ge(sem("xs_copied"), 1)
                for t in range(NT):
                    ts = slice(t * P, (t + 1) * P)
                    if t:
                        pe.wait_ge(sem("ssd_y_copied"), t)
                    for hd in range(8):
                        mm(PS[:, 2 + hd // 4, (hd % 4) * P:(hd % 4 + 1) * P],
                           lhsT=da[:, t, hd:hd + 1].to_broadcast([P, P]), rhs=upper, start=True, stop=True)
                    for g in range(2):
                        ins = mm(PS[:, 4, g * P:(g + 1) * P], lhsT=Bf[:, ts], rhs=Cp[:, g, ts], start=True, stop=True)
                    ins.then_inc(sem("cb_ready"), 1)
                    pe.wait_ge(sem("ssd_in"), t + 1)
                    for hd in range(8):
                        p0 = 64 * (hd % 2)
                        o = PS[p0:p0 + 64, 0, (hd // 2) * P:(hd // 2 + 1) * P]
                        ins = mm(o, lhsT=xdt[:, hd * 64:hd * 64 + 64], rhs=MT[:, hd, :], start=True, stop=(t == 0))
                        if t:
                            ins = mm(o, lhsT=Sst[:, hd % 4, :], rhs=Csp[:, hd, :], start=False, stop=True)
                    ins.then_inc(sem("ssd_y_ready"), 1)
                    if t < NT - 1:
                        for g in range(2):
                            ins = mm(PS[64 * g:64 * g + 64, 1, 0:256], lhsT=Bt[:, t, 64 * g:64 * g + 64],
                                     rhs=xdd[:, 256 * g:256 * g + 256], start=True, stop=True)
                        ins.then_inc(sem("ssd_st_ps"), 1)
                for j in range(4):
                    pe.wait_ge(sem("o_sq"), 8 + j + 1)
                    ins = mm(PS[:, j // 2, :], lhsT=ones, rhs=xsT[:, j, :], start=(j % 2 == 0), stop=(j % 2 == 1))
                    if j % 2:
                        ins.then_inc(sem("o_ms"), 1)

            def outproj(l):
                pe.wait_ge(sem("mix_done"), l + 1)
                for n in range(KD):
                    if n % 4 == 0:
                        arrived(pe, ("out", l, n // 4))
                    if n >= 4:
                        pe.wait_ge(sem("x_ready"), 8 + 9 * l + n - 3)
                    W = ring_ap(("out", l, n // 4))
                    for k in range(KD):
                        ins = mm(PS[:, n % 4, :], lhsT=W[:, k, (n % 4) * P:(n % 4 + 1) * P], rhs=y[:, k, :],
                                 start=(k == 0), stop=(k == KD - 1))
                    ins.then_inc(sem("outproj_done"), 1)

            def experts(l):
                pe.wait_ge(sem("h_ready"), KD * (2 * l + 2))
                for t in range(NT):
                    for k in range(KD):
                        ins = mm(PS[:, 4, t * E:(t + 1) * E], lhsT=h[:, k, t * P:(t + 1) * P], rhs=wr[:, k, :],
                                 start=(k == 0), stop=(k == KD - 1))
                ins.then_inc(sem("logits_ready"), 1)
                for t in range(NT):
                    if t >= 2:
                        pe.wait_ge(sem("ht_copied"), NT * l + t - 1)
                    for k in range(KD):
                        ins = tr(PS[:, 2 * (t % 2) + k // 4, (k % 4) * P:(k % 4 + 1) * P], h[:, k, t * P:(t + 1) * P], ident)
                    ins.then_inc(sem("ht_ready"), 1)
                pe.wait_ge(sem("choices_ready"), l + 1)
                for t in range(NT):
                    for s in range(t + 1):
                        mm(PS[:, 5, t * E:(t + 1) * E], lhsT=(upper if s == t else ones), rhs=both[:, s, :],
                           start=(s == 0), stop=(s == t))
                for s in range(NT):
                    ins = mm(PS[:, 5, NT * E:(NT + 1) * E], lhsT=ones, rhs=both[:, s, :], start=(s == 0), stop=(s == NT - 1))
                ins.then_inc(sem("rank_ready"), 1)
                for n in range(2 * NT):
                    pe.wait_ge(sem("place_ready"), 2 * NT * l + n + 1)
                    mm(PS[:, 6, 0:MAX_BLOCKS], lhsT=ohr, rhs=ohb, start=(n == 0), stop=(n == 2 * NT - 1))\
                        .then_inc(sem("place_used"), 1)
                pe.wait_ge(sem("table_ready"), l + 1)
                pairs = pairs_of(pe, l)

                def turn_x(j, loads):
                    pe.wait_ge(gathered[l][j], loads)
                    for k in range(KD):
                        ins = tr(PS[:, 2 + k // 4, (k % 4) * P:(k % 4 + 1) * P], xg[:, j, k * P:(k + 1) * P], ident)
                    ins.then_inc(sem(f"l{l}_xt_turned"), 1)

                turn_x(0, 16)
                with pe.Fori(0, pairs) as it:
                    for j in range(2):
                        b1 = it * 2 + (j + 1)
                        wg, wu, wd = moe_w[j]
                        pe.wait_ge(sem(f"l{l}_xt_copied"), b1)
                        pe.wait_ge(w_loaded[l][3 * j], (it + 1) * 16)
                        for k in range(KD):
                            ins = mm(PS[:, 0, :], lhsT=xTb[:, k, :], rhs=wg[:, k, :], start=(k == 0), stop=(k == KD - 1))
                        ins.then_inc(sem(f"l{l}_gate_done"), 1)
                        pe.wait_ge(w_loaded[l][3 * j + 1], (it + 1) * 16)
                        for k in range(KD):
                            ins = mm(PS[:, 1, :], lhsT=xTb[:, k, :], rhs=wu[:, k, :], start=(k == 0), stop=(k == KD - 1))
                        ins.then_inc(sem(f"l{l}_up_done"), 1)
                        turn_x(1 - j, (it + 1) * 16 if j == 0 else (it + 2) * 16)
                        pe.wait_ge(sem(f"l{l}_act_done"), b1)
                        for k in range(4):
                            ins = tr(PS[:, 4, k * P:(k + 1) * P], actb[:, k * P:(k + 1) * P], ident)
                        ins.then_inc(sem(f"l{l}_at_turned"), 1)
                        pe.wait_ge(sem(f"l{l}_at_copied"), b1)
                        pe.wait_ge(w_loaded[l][3 * j + 2], (it + 1) * 16)
                        for n in range(2):
                            for k in range(4):
                                ins = mm(PS[:, 5 + n, :], lhsT=aT[:, k, :], rhs=wd[:, k, n * 512:(n + 1) * 512],
                                         start=(k == 0), stop=(k == 3))
                        ins.then_inc(sem(f"l{l}_down_done"), 1)
                for t in range(NT):
                    pe.wait_ge(sem("combined"), NT * l + t + 1)
                    if t >= 2:
                        pe.wait_ge(sem("comb_added"), NT * l + t - 1)
                    for k in range(KD):
                        ins = tr(PS[:, 2 * (t % 2) + k // 4, (k % 4) * P:(k % 4 + 1) * P],
                                 cg[:, (t % 2) * 2, k * P:(k + 1) * P], ident)
                    ins.then_inc(sem("comb_turned"), 1)

            pe.wait_ge(sem("pool_const"), 2)
            pe.wait_ge(sem("params_loaded"), 16 * 9)
            for i in range(12):
                ada_sums(0, i)
            norm(0)
            projections(0)
            linear_attention(0)
            rwkv()
            outproj(0)
            norm(1)
            experts(0)
            norm(2)
            projections(1)
            linear_attention(1)
            ssd()
            outproj(1)
            norm(3)
            experts(1)
            norm(4)
            pe.wait_ge(sem("h_ready"), KD * 5)
            for t in range(NT):
                if t >= 2:
                    pe.wait_ge(sem("out_copied"), t - 1)
                for k in range(KD):
                    ins = tr(PS[:, 2 * (t % 2) + k // 4, (k % 4) * P:(k % 4 + 1) * P], h[:, k, t * P:(t + 1) * P], ident)
                ins.then_inc(sem("out_turned"), 1)

        @block.vector
        def _(dve):
            steps = {}

            def link(ins):
                signal(ins, "dve_order")

            def signal(ins, name):
                steps[name] = steps.get(name, 0) + 1
                ins.then_inc(sem(name), 1)
                dve.wait_ge(sem(name), steps[name])

            def tt(out, a, b, op):
                return dve.tensor_tensor(out, a, b, op)

            def tsc(out, a, s1, op0, s2=None, op1=None):
                return dve.tensor_scalar(out, a, s1, s2, op0, op1) if op1 else dve.tensor_scalar(out, a, s1, None, op0)

            def stt(out, a, s, b, op0, op1):
                return dve.scalar_tensor_tensor(out=out, in0=a, scalar=s, in1=b, op0=op0, op1=op1)

            def f2(ap):
                return ap.rearrange("p a b -> p (a b)")

            def sigmoid_tail(ap):
                link(tsc(ap, ap, 1.0, ALU.add))
                link(dve.reciprocal(ap, ap))

            signal(dve.memset(y_[:, 0:D], 0.0), "zeros_ready")
            dve.wait_ge(sem("x_turned"), 1)
            n1 = sum(n for _, n in ROWS1)
            link(dve.tensor_copy(prm[:, 0, 0:n1], PS[:, 0, 0:n1]))
            signal(dve.tensor_copy(prm[:, 1, :], PS[:, 0, P:2 * P]), "params_ready")
            for k in range(KD):
                dve.wait_ge(sem("x_turned"), k + 2)
                signal(dve.tensor_copy(xT[:, k, :], PS[:, 1 + k % 4, :]), "x_ready")
            dve.wait_ge(sem("setup_exp"), 1)
            sigmoid_tail(cond)
            signal(tt(cond, cond, prm_col("c", 0, 8), ALU.mult), "setup_step")
            dve.wait_ge(sem("params_loaded"), 16 * 9)
            for par in range(2):
                pp = slice(64 * par, 64 * par + 64)
                link(dve.tensor_copy(skipc[pp, :], rs[pp, par:8:2]))
            link(tsc(negw0, prm_col("a_w0", 0, 4), -1.0, ALU.mult))
            link(tsc(nega0, prm_col("a_a0", 0, 4), -1.0, ALU.mult))
            link(tsc(omu, prm_col("a_mu", 0, 14), -1.0, ALU.mult, 1.0, ALU.add))

            def modulation(l):
                dve.wait_ge(sem("ada_summed"), 12 * (l + 1))
                link(tt(mod[:, l, :], PS[:, 7, 0:48], prm_col("b_ada", 48 * l, 48), ALU.add))
                for place in range(2):
                    c = 8 + 24 * place
                    ins = stt(amul[:, l, place, :], mod[:, l, c:c + 8], 1.0,
                              prm_col("norm_gain", (2 * l + place) * 8, 8), ALU.add, ALU.mult)
                    if place == 0:
                        link(ins)
                signal(ins, "amul_ready")

            def norm(n):
                dve.wait_ge(sem("rstd_ready"), n + 1)
                for k in range(KD):
                    tt(h[:, k, :], xT[:, k, :], rs, ALU.mult).then_inc(sem("xn_ready"), 1)

            def projections(l):
                for n, (c, c0, w, kind, j) in enumerate(BLOCKS[l]):
                    ps = PS[:, n % 4, :]
                    if kind in WITH_ACT:
                        dve.wait_ge(sem("proj_act"), act_blocks(l, n + 1))
                    dve.wait_ge(sem("proj_done"), l * NB[0] + n + 1)
                    if kind == "shift":
                        o = shifted[j]
                        ins = stt(o[:, 1:T], ps[:, 0:T - 1], prm_col("a_mu", j), o[:, 1:T], ALU.mult, ALU.add)
                    elif kind == "q":
                        ins = tsc(lq[:, j, :], ps, 0.125 if l == 0 else 1.0, ALU.mult)
                    elif kind == "k":
                        ins = dve.tensor_copy(lk[:, j, :], ps)
                    elif kind == "v":
                        ins = dve.tensor_copy(lv[:, j, :], ps)
                    elif kind == "lora":
                        ins = dve.tensor_copy(le[0:16, 0:T], ps[0:16, :])
                    elif kind == "gate":
                        sigmoid_tail(lgate[:, j, :])
                        ins = tt(lgate[:, j, :], lgate[:, j, :], ps, ALU.mult)
                    elif kind == "z":
                        sigmoid_tail(zs[:, j, :])
                        ins = tt(zs[:, j, :], zs[:, j, :], ps, ALU.mult)
                    elif kind == "f":
                        sigmoid_tail(lg[:, j, :])
                        link(tsc(lg[:, j, :], lg[:, j, :], omlb[:, j:j + 1], ALU.mult, lb[:, j:j + 1], ALU.add))
                        ins = tsc(lk[:, j, :], lg[:, j, :], -1.0, ALU.mult, 1.0, ALU.add)
                    elif kind == "dt":
                        ins = tt(dt, ps[:, 0:32].rearrange("p (a b) -> p a b", b=8), bc(dtb, NT, 1), ALU.add)
                    elif kind == "conv":
                        cw = [prm_col("d_conv_w", 6 * i + j) for i in range(4)]
                        link(tsc(cva, ps, cw[3], ALU.mult, prm_col("d_conv_b", j), ALU.add))
                        for i in (2, 1):
                            s = 3 - i
                            link(stt(cva[:, s:T], ps[:, 0:T - s], cw[i], cva[:, s:T], ALU.mult, ALU.add))
                        signal(stt(cva[:, 3:T], ps[:, 0:T - 3], cw[0], cva[:, 3:T], ALU.mult, ALU.add), "conv_sum")
                        dve.wait_ge(sem("conv_exp"), j + 1)
                        sigmoid_tail(cve)
                        if j < 4:
                            ins = tt(xsF[:, j, :], cve, cva, ALU.mult)
                        elif j == 4:
                            ins = tt(Bf, cve, cva, ALU.mult)
                        else:
                            for g in range(2):
                                gp = slice(64 * g, 64 * g + 64)
                                ins = tt(Cp[gp, g, :], cve[gp, :], cva[gp, :], ALU.mult)
                                if g == 0:
                                    link(ins)
                    signal(ins, "proj_copied")

            def linear_attention(l):
                if l == 0:
                    dve.wait_ge(sem("alpha_ready"), 1)
                    for j in range(2):
                        link(tsc(lg[:, j, :], PS[:, 4 + j, :], prm_col("b_alpha_bias", j), ALU.add))
                    signal(stt(le, lgf, -1.0, lgf, ALU.mult, ALU.min), "log_pre")
                    dve.wait_ge(sem("log_done"), 1)
                    link(stt(lgf, lgf, 0.0, le, ALU.min, ALU.subtract))
                    link(tsc(lgf, lgf, 1.0 / 16, ALU.mult))
                else:
                    signal(dve.memset(f2(lqp), 0.0), "log_pre")
                    dve.wait_ge(sem("log_done"), 2)
                for j in range(2):
                    link(dve.tensor_tensor_scan(lg[:, j, :], reset128, lg[:, j, :], 0.0, ALU.mult, ALU.add))
                link(dve.memset(f2(lqp), 0.0))

                def diff(n):
                    hh = LV[n]
                    lo, hi = halves(lgf, hh)
                    ref = lo[:, :, hh - 1:hh]
                    m = 1024 // (2 * hh)
                    refb = ref.to_broadcast([P, m, hh])
                    eq = le[:, 0:512].rearrange("p (n h) -> p n h", h=hh)
                    ek = le[:, 512:1024].rearrange("p (n h) -> p n h", h=hh)
                    link(tt(eq, hi, refb, ALU.subtract))
                    signal(tt(ek, refb, lo, ALU.subtract), "lev_diff")

                def products(n):
                    hh = LV[n]
                    dve.wait_ge(sem("lev_exp"), lev_n * l + n + 1)
                    eq = le[:, 0:512].rearrange("p (t n h) -> p t n h", t=2, h=hh)
                    ek = le[:, 512:1024].rearrange("p (n h) -> p n h", h=hh)
                    for par in range(2):
                        pp = slice(64 * par, 64 * par + 64)
                        for t2 in range(2):
                            q_hi = halves(lq[pp, t2, :], hh)[1]
                            o_hi = halves(lqp[pp, 2 * t2 + par, :], hh)[1]
                            link(tt(o_hi, q_hi, eq[pp, t2], ALU.mult))
                    signal(tt(halves(f2(lkp), hh)[0], halves(f2(lk), hh)[0], ek, ALU.mult), "lev_ready")

                def merge(n, mask):
                    dve.wait_ge(sem("lev_scored"), (lev_n + 1) * l + n + 1)
                    ps = PS[:, 0:4, :].rearrange("p a (b c) -> p (a b) c", c=P)
                    if n == 0:
                        signal(tt(lA, ps, bc(ident, 16, 1), ALU.mult), "lev_merged")
                    else:
                        signal(dve.copy_predicated(lA, bc(mask, 16, 1).bitcast(I32), ps), "lev_merged")

                diff(0)
                for par in range(2):
                    pp = slice(64 * par, 64 * par + 64)
                    link(dve.tensor_copy(lqp[pp, par::2, :], lq[pp]))
                signal(dve.tensor_copy(lkp, lk), "lev_ready")
                for n in range(lev_n + 1):
                    merge(n, lev_up[LV[n - 1]] if n else None)
                    if n < lev_n:
                        products(n)
                        if n + 1 < lev_n:
                            diff(n + 1)
                dve.wait_ge(sem("start_decay"), l + 1)
                le2 = le.rearrange("p (a b) -> p a b", b=T)
                for par in range(2):
                    pp = slice(64 * par, 64 * par + 64)
                    link(tt(lqp[pp, par::2, :], lq[pp], le2[pp], ALU.mult))
                link(dve.tensor_copy(ebl, le.rearrange("p (a t s) -> p a t s", a=2, s=P)[:, :, :, P - 1]))
                b3 = lgf.rearrange("p (n s) -> p n s", s=P)
                signal(tt(le.rearrange("p (n s) -> p n s", s=P), b3[:, :, P - 1:P].to_broadcast([P, 8, P]), b3,
                          ALU.subtract), "kd_diff")
                dve.wait_ge(sem("end_decay"), l + 1)
                signal(tt(f2(lkp), f2(lk), le, ALU.mult), "kd_ready")
                dve.wait_ge(sem("kd_turned"), l + 1)
                signal(dve.tensor_copy(f2(lq), PS[:, 4:6, :].rearrange("p a b -> p (a b)")), "kdT_ready")
                for t in range(NT - 1):
                    dve.wait_ge(sem("ls_ps"), 3 * l + t + 1)
                    for j in range(2):
                        ps = PS[:, 6, j * P:(j + 1) * P]
                        if t == 0:
                            ins = dve.tensor_copy(lS[:, j, :], ps)
                        else:
                            ins = stt(lS[:, j, :], lS[:, j, :], ebl[:, j, t:t + 1], ps, ALU.mult, ALU.add)
                        if j == 0:
                            link(ins)
                    signal(ins, "ls_ready")
                gain = prm_col(("b_norm_gain", "c_norm_gain")[l])
                for hd in range(4):
                    dve.wait_ge(sem("o_rstd"), 4 * l + hd + 1)
                    link(stt(h[:, hd, :], PS[:, hd, :], gain, h[:, 4 + hd, :], ALU.mult, ALU.mult))
                    ins = tt(y[:, 4 * (1 - l) + hd, :], h[:, hd, :], lgate[:, hd, :], ALU.mult)
                    if hd < 3:
                        link(ins)
                signal(ins, "yhalf")

            def rwkv():
                dve.wait_ge(sem("setup_exp"), 3)
                link(tsc(gdp, gdp, 1.0, ALU.add))
                signal(dve.reciprocal(gdp, gdp), "setup_step")
                link(dve.memset(f2(alp), 0.0))
                link(dve.memset(f2(rho), 0.0))
                signal(dve.memset(f2(ST), 0.0), "st_done")

                def col(name):
                    return prm_col(name, 0, 4).unsqueeze(2).to_broadcast([P, 4, P])

                for t in range(NT):
                    ts = slice(t * P, (t + 1) * P)
                    r_t, k_t, v_t = rr[:, :, ts], kk_[:, :, ts], vv[:, :, ts]
                    dve.wait_ge(sem("lora_exp"), t + 1)
                    sigmoid_tail(t_sg)
                    link(dve.tensor_tensor_scan(f2(t_cs), reset64, f2(t_sg), 0.0, ALU.mult, ALU.add))
                    signal(tt(t_sg, t_cs, t_sg, ALU.subtract), "cs_ready")
                    link(tt(t_kk, k_t, col("a_k_k"), ALU.mult))
                    signal(tt(t_1, t_kk, t_kk, ALU.mult), "kk_sq")
                    sigmoid_tail(t_a)
                    link(stt(t_kt, t_a, -1.0, col("a_k_a"), ALU.add, ALU.mult))
                    link(stt(t_kt, t_kt, 1.0, k_t, ALU.add, ALU.mult))
                    dve.wait_ge(sem("kk_rn"), t + 1)
                    link(tt(t_kk, t_kk, t_1, ALU.mult))
                    dve.wait_ge(sem("decays_ready"), t + 1)
                    link(stt(t_sg, t_kk, -1.0, t_sg, ALU.mult, ALU.mult))
                    for par in range(2):
                        pp = slice(64 * par, 64 * par + 64)
                        link(dve.tensor_copy(alp[pp, par::2, :], t_sg[pp]))
                        link(tt(rho[pp, par::2, :], r_t[pp], t_eb[pp], ALU.mult))
                    link(tt(t_ka, t_kt, t_cs, ALU.mult))
                    link(tt(t_be, t_a, t_kk, ALU.mult))
                    link(tt(t_be, t_be, t_cs, ALU.mult))
                    link(tt(t_1, r_t, t_kt, ALU.mult))
                    signal(tt(t_1, t_1, col("a_r_k"), ALU.mult), "feat_ready")
                    dve.wait_ge(sem("bonus_sum"), t + 1)
                    signal(tt(t_1, PS[:, 3, :].rearrange("p (a b) -> p a b", b=P), v_t, ALU.mult), "bonus_used")
                    for n, (b, dst, mask) in enumerate(((5, XT, strict_up), (0, X, strict_lo), (2, LKT, strict_up),
                                                        (5, PKT, incl_up), (0, PBT, incl_up))):
                        dve.wait_ge(sem("score_ready"), 5 * t + n + 1)
                        ps = PS[:, b:b + 2, :].rearrange("p a (b c) -> p (a b) c", c=P)
                        signal(tt(dst, ps, bc(mask, 8, 1), ALU.mult), "score_copied")
                    for dst, src, mask in ((Tm, X, lev_lo[1]), (TT, XT, lev_up[1])):
                        link(dve.tensor_copy(dst, bc(ident, 8, 1)))
                        link(dve.copy_predicated(dst, bc(mask, 8, 1).bitcast(I32), src))
                    signal(dve.tensor_copy(Tm[:, 0:1, 0:1], Tm[:, 0:1, 0:1]), "inv_ready")
                    for n in range(5):
                        for o in range(2):
                            if n == 4 and o == 0:
                                continue
                            dve.wait_ge(sem("p_ready"), 9 * t + (2 * n + 2 if n < 4 else 9))
                            b, dst, mask = ((4, Tm, lev_lo), (0, TT, lev_up))[o]
                            ps = PS[:, b:b + 2, :].rearrange("p a (b c) -> p (a b) c", c=P)
                            signal(dve.copy_predicated(dst, bc(mask[LV[n + 1]], 8, 1).bitcast(I32), ps), "inv_ready")
                    for c in range(2):
                        po = 64 * c
                        dve.wait_ge(sem("un_ready"), 2 * t + c + 1)
                        dve.wait_ge(sem("rw_copied"), 2 * t + 2)
                        signal(tt(Un[po:po + 64, :], PS[po:po + 64, 3, :], U0[po:po + 64, :], ALU.add), "un_done")
                        dve.wait_ge(sem("st_ps"), 2 * t + c + 1)
                        for par in range(2):
                            pp = slice(64 * par, 64 * par + 64)
                            s_par = ST[pp, par::2, :]
                            link(tt(s_par, PS[pp, 4, 0:256].rearrange("p (a b) -> p a b", b=64), s_par, ALU.add))
                            ins = tt(s_par, s_par, t_eb[pp, :, po + 63:po + 64].to_broadcast([64, 4, 64]), ALU.mult)
                            if par == 0:
                                link(ins)
                        signal(ins, "st_done")
                    dve.wait_ge(sem("ys_copied"), t + 1)
                    signal(tt(f2(t_cs), PS[:, 5, :], f2(t_sg), ALU.add), "gn_in")
                    dve.wait_ge(sem("gn_sum"), 2 * t + 1)
                    link(stt(f2(t_cs), PS[:, 0, :], -1.0 / 64, f2(t_cs), ALU.mult, ALU.add))
                    signal(tt(t_eb, t_cs, t_cs, ALU.mult), "gn_in")
                    dve.wait_ge(sem("gn_rstd"), t + 1)
                    link(tt(t_cs, t_cs, t_eb, ALU.mult))
                    link(tt(t_cs, t_cs, col("a_ln_gain"), ALU.mult))
                    link(tt(t_cs, t_cs, col("a_ln_bias"), ALU.add))
                    link(tt(t_cs, t_cs, t_1, ALU.add))
                    signal(tt(y[:, 0:4, ts], y[:, 0:4, ts], t_cs, ALU.mult), "rwkv_done")

            def lower_bounds():
                c0, c1 = prm_col("c_lb", 0, 2), prm_col("c_lb", 2, 2)
                link(tt(lbt[:, 0:2], c0, c1, ALU.max))
                link(tt(lbt[:, 4:6], c0, lbt[:, 0:2], ALU.subtract))
                signal(tt(lbt[:, 6:8], c1, lbt[:, 0:2], ALU.subtract), "setup_step")

            def lower_bounds_end():
                e0, e1 = lbt[:, 4:6], lbt[:, 6:8]
                dve.wait_ge(sem("setup_exp"), 2)
                link(tt(lbt[:, 0:2], e0, e1, ALU.add))
                link(dve.reciprocal(lbt[:, 0:2], lbt[:, 0:2]))
                link(tt(e0, e0, lbt[:, 0:2], ALU.mult))
                link(tt(e1, e1, lbt[:, 0:2], ALU.mult))
                link(tt(lbt[:, 0:2], e0, e1, ALU.add))
                link(tt(lb, lbt[:, 0:2], e0, ALU.subtract))
                link(tsc(omlb, lb, -1.0, ALU.mult, 1.0, ALU.add))

            def ssd():
                signal(stt(f2(dz), f2(dt), -1.0, f2(dt), ALU.mult, ALU.min), "setup_step")
                dve.wait_ge(sem("setup_exp"), 4)
                link(tsc(f2(dz2), f2(dz), 2.0, ALU.add))
                link(dve.reciprocal(f2(dz2), f2(dz2)))
                link(tt(f2(dz), f2(dz), f2(dz2), ALU.mult))
                link(tt(f2(dz2), f2(dz), f2(dz), ALU.mult))
                terms = [2.0 / (2 * i + 1) for i in range(9)]
                link(tsc(f2(dpl), f2(dz2), terms[8], ALU.mult, terms[7], ALU.add))
                for i in range(6, -1, -1):
                    link(tt(f2(dpl), f2(dpl), f2(dz2), ALU.mult))
                    link(tsc(f2(dpl), f2(dpl), terms[i], ALU.add))
                link(tt(f2(dpl), f2(dpl), f2(dz), ALU.mult))
                link(stt(f2(dt), f2(dt), 0.0, f2(dpl), ALU.max, ALU.add))
                signal(stt(da, dt, -1.0, bc(alog, NT, 1), ALU.mult, ALU.mult), "da_ready")
                dve.wait_ge(sem("xs_turned"), 1)
                link(dve.tensor_copy(xsT, PS[:, 0:4, :]))
                signal(dve.tensor_copy(f2(Bt), PS[:, 4, :]), "xs_copied")
                dve.wait_ge(sem("xs_turned"), 2)
                link(dve.tensor_copy(f2(cumc), PS[:, 5, 0:32]))
                link(dve.memset(f2(Csp), 0.0))
                for t in range(NT):
                    ts = slice(t * P, (t + 1) * P)
                    dve.wait_ge(sem("cb_ready"), t + 1)
                    for hd in range(8):
                        link(tsc(Es[:, hd, :], PS[:, 2 + hd // 4, (hd % 4) * P:(hd % 4 + 1) * P],
                                 cumc[:, t, hd:hd + 1], ALU.subtract, 0.0, ALU.min))
                    last = PS[:, 2:4, :].rearrange("p a (b c) -> p (a b) c", c=P)[:, :, P - 1]
                    signal(tt(dte, last, cumc[:, t, :], ALU.subtract), "seg_diff")
                    link(tt(CBm, PS[:, 4, 0:256].rearrange("p (a b) -> p a b", b=P), bc(upper, 2, 1), ALU.mult))
                    xv = xsT[:, t, :].rearrange("p (a b) -> p a b", b=64)
                    xdv = xdt.rearrange("p (a b) -> p a b", b=64)
                    link(tt(xdv, xv, dt[:, t, :].unsqueeze(2).to_broadcast([P, 8, 64]), ALU.mult))
                    dve.wait_ge(sem("seg_exp"), 2 * t + 1)
                    link(tt(MT.rearrange("p (g q) c -> p g q c", g=2), Es.rearrange("p (g q) c -> p g q c", g=2),
                            bc(CBm, 4, 2), ALU.mult))
                    dve.wait_ge(sem("seg_exp"), 2 * t + 2)
                    link(tt(xdd.rearrange("p (a b) -> p a b", b=64), xdv,
                            dte.unsqueeze(2).to_broadcast([P, 8, 64]), ALU.mult))
                    for g in range(2):
                        gp = slice(64 * g, 64 * g + 64)
                        ins = tt(Csp[gp, 4 * g:4 * g + 4, :], ec[gp, 4 * g:4 * g + 4, :], bc(Cp[gp, g, ts], 4, 1), ALU.mult)
                        if g == 0:
                            link(ins)
                    signal(ins, "ssd_in")
                    if t < NT - 1:
                        dve.wait_ge(sem("ssd_st_ps"), t + 1)
                        ps = PS[:, 1, 0:256].rearrange("p (a b) -> p a b", b=64)
                        if t == 0:
                            link(dve.tensor_copy(Sst, ps))
                        else:
                            for g in range(2):
                                gp = slice(64 * g, 64 * g + 64)
                                link(tt(Stm[gp], Sst[gp], ec[gp, 4 * g:4 * g + 4, P - 1:P].to_broadcast([64, 4, 64]),
                                        ALU.mult))
                            link(tt(Sst, Stm, ps, ALU.add))
                    dve.wait_ge(sem("ssd_y_ready"), t + 1)
                    for j in range(4):
                        ins = stt(yF[:, j, ts], xsF[:, j, ts], skipc[:, j:j + 1], PS[:, 0, j * P:(j + 1) * P],
                                  ALU.mult, ALU.add)
                        if j < 3:
                            link(ins)
                    signal(ins, "ssd_y_copied")
                signal(tt(yF, yF, zs, ALU.mult), "yz_ready")
                for j in range(4):
                    if j % 2 == 0:
                        dve.wait_ge(sem("o_rstd"), 8 + j // 2 + 1)
                    rstd = f2(Es if j < 2 else MT)[:, 0:512]
                    link(stt(y[:, 4 + j, :], yF[:, j, :], prm_col("d_norm_gain", j), rstd, ALU.mult, ALU.mult))

            def outproj(l):
                signal(dve.tensor_copy(lsum[:, 0:1], lsum[:, 1:2]), "mix_done")
                for n in range(KD):
                    dve.wait_ge(sem("outproj_done"), 8 * l + n + 1)
                    signal(stt(xT[:, n, :], PS[:, n % 4, :], mod[:, l, 16 + n:17 + n], xT[:, n, :], ALU.mult, ALU.add),
                           "x_ready")

            def choose(l):
                dve.wait_ge(sem("logits_exp"), l + 1)
                sigmoid_tail(sc)
                link(tt(sel, sc, bc(rbias, NT, 1), ALU.add))
                v = sel.rearrange("p t (n two) -> p t n two", two=2)
                link(tt(r1, v[:, :, :, 0], v[:, :, :, 1], ALU.max))
                link(tt(r2, v[:, :, :, 0], v[:, :, :, 1], ALU.min))
                mx = r1.rearrange("p t (g two) -> p t g two", two=2)
                mn = r2.rearrange("p t (g two) -> p t g two", two=2)
                link(tt(gs, mx[:, :, :, 0], mx[:, :, :, 1], ALU.min))
                link(tt(gm, mn[:, :, :, 0], mn[:, :, :, 1], ALU.max))
                link(tt(gm, gm, gs, ALU.max))
                link(tt(gs, mx[:, :, :, 0], mx[:, :, :, 1], ALU.max))
                link(tt(gs, gs, gm, ALU.add))

                def first_max(vals, n, onehot):
                    link(dve.tensor_reduce(m1, vals, AX_X, ALU.max))
                    m1b = m1.unsqueeze(2).to_broadcast([P, NT, n])
                    t_ = idc[:, :, 0:n]
                    link(tt(t_, vals, m1b, ALU.is_lt))
                    link(stt(t_, t_, BIG, bc(iota16[:, 0:n], NT, 1), ALU.mult, ALU.add))
                    link(dve.tensor_reduce(m1, t_, AX_X, ALU.min))
                    link(tt(onehot, bc(iota16[:, 0:n], NT, 1), m1b, ALU.is_equal))

                first_max(gs, GRP, gm)
                link(tsc(gs, gm, -1.0, ALU.add, BIG, ALU.mult))
                s4 = sel.rearrange("p t (g i) -> p t g i", i=4)
                link(tt(s4, s4, gs.unsqueeze(3).to_broadcast([P, NT, GRP, 4]), ALU.add))
                ohv = [oh[:, k, :].rearrange("p (t e) -> p t e", e=E) for k in range(2)]
                first_max(sel, E, ohv[0])
                link(stt(sel, ohv[0], -4 * BIG, sel, ALU.mult, ALU.add))
                first_max(sel, E, ohv[1])
                signal(tt(both, ohv[0], ohv[1], ALU.add), "choices_ready")
                for k in range(2):
                    link(tt(idc, sc, ohv[k], ALU.mult))
                    link(dve.tensor_reduce(gk[:, k, :], idc, AX_X, ALU.add))
                link(tt(gsum, gk[:, 0, :], gk[:, 1, :], ALU.add))
                link(dve.reciprocal(gsum, gsum))
                link(tt(gk, gk, bc(gsum, 2, 1), ALU.mult))

                dve.wait_ge(sem("rank_ready"), l + 1)
                link(tt(rank, PS[:, 5, 0:NT * E].rearrange("p (a b) -> p a b", b=E), both, ALU.subtract))
                link(dve.tensor_copy(cnt, PS[:, 5, NT * E:(NT + 1) * E]))

                def thresholds(out, src, lo, op, tmp):
                    link(tsc(out, src, lo, op))
                    for m in (2, 3):
                        link(tsc(tmp, src, lo + P * (m - 1), op))
                        link(tt(out, out, tmp, ALU.add))

                thresholds(nov, cnt, float(P), ALU.is_gt, over)
                link(dve.tensor_tensor_scan(ove, ones[:, 0:E], nov, 0.0, ALU.mult, ALU.add))
                link(tt(over, ove, nov, ALU.subtract))
                link(tt(over, over, iota16, ALU.subtract))
                thresholds(qq, rank, float(P), ALU.is_ge, q0)
                link(tsc(q0, qq, 0.0, ALU.is_gt))
                link(stt(blk, qq, 15.0, bc(over, NT, 1), ALU.add, ALU.add))
                link(tt(blk, blk, q0, ALU.mult))
                link(tt(blk, blk, bc(iota16, NT, 1), ALU.add))
                link(stt(rin, qq, -float(P), rank, ALU.mult, ALU.add))
                for k in range(2):
                    for src, dst in ((blk, selb), (rin, selr)):
                        link(tt(idc, src, ohv[k], ALU.mult))
                        link(dve.tensor_reduce(dst[:, k, :], idc, AX_X, ALU.add))
                link(stt(destf, selb, float(P), selr, ALU.mult, ALU.add))
                link(dve.tensor_copy(idx_dest[:, :], f2(destf)))

                link(dve.tensor_copy(tabf[:, 0:E], iota16))
                w3 = rank.rearrange("p a b -> p (a b)")
                for b in range(8):
                    link(tsc(idc[:, 0, :], ove, float(b), ALU.is_le))
                    link(dve.tensor_reduce(tabf[:, E + b:E + b + 1], idc[:, 0, :], AX_X, ALU.add))
                link(tsc(tabf[:, E:E + 8], tabf[:, E:E + 8], float(E - 1), ALU.min))
                link(tsc(tabf[:, 24:25], ove[:, E - 1:E], 0.0, ALU.is_gt, 8.0, ALU.add))
                for m in (2.0, 4.0, 6.0):
                    link(tsc(tabf[:, 25:26], ove[:, E - 1:E], m, ALU.is_gt))
                    link(tt(tabf[:, 24:25], tabf[:, 24:25], tabf[:, 25:26], ALU.add))
                link(dve.tensor_copy(table[:, 0:24], tabf[:, 0:24]))
                link(dve.tensor_copy(table[:, 30 + l:31 + l], tabf[:, 24:25]))
                link(tsc(tabf[:, 24:25], tabf[:, 24:25], -1.0, ALU.add))
                link(dve.tensor_copy(table[:, 26 + l:27 + l], tabf[:, 24:25]))

                for n in range(2 * NT):
                    k, t = n // NT, n % NT
                    if n or l:
                        dve.wait_ge(sem("place_used"), 2 * NT * l + n)
                    link(tsc(ohb, iota24, selb[:, k, t:t + 1], ALU.is_equal, tokid[:, t:t + 1], ALU.mult))
                    signal(tsc(ohr, iota128, selr[:, k, t:t + 1], ALU.is_equal), "place_ready")
                dve.wait_ge(sem("place_used"), 2 * NT * (l + 1))
                signal(dve.tensor_copy(idx_tok[:, 0:MAX_BLOCKS], PS[:, 6, 0:MAX_BLOCKS]), "table_ready")

            def experts(l):
                choose(l)
                pairs = pairs_of(dve, l)
                so = sem(f"l{l}_silu_order")
                with dve.Fori(0, pairs) as it:
                    for j in range(2):
                        b1 = it * 2 + (j + 1)
                        dve.wait_ge(sem(f"l{l}_gate_exp"), b1)
                        tsc(sgt, sgt, 1.0, ALU.add).then_inc(so, 1)
                        dve.wait_ge(so, it * 6 + (3 * j + 1))
                        dve.reciprocal(sgt, sgt).then_inc(so, 1)
                        dve.wait_ge(so, it * 6 + (3 * j + 2))
                        tt(sgt, sgt, PS[:, 0, :], ALU.mult).then_inc(so, 1)
                        dve.wait_ge(so, it * 6 + (3 * j + 3))
                        dve.wait_ge(sem(f"l{l}_up_done"), b1)
                        tt(actb, sgt, PS[:, 1, :], ALU.mult).then_inc(sem(f"l{l}_act_done"), 1)
                        dve.wait_ge(sem(f"l{l}_at_turned"), b1)
                        dve.tensor_copy(aT, PS[:, 4, :].rearrange("p (a b) -> p a b", b=P))\
                           .then_inc(sem(f"l{l}_at_copied"), 1)
                for t in range(NT):
                    dve.wait_ge(sem(f"expert_rows{t % 2}"), 32 * (2 * l + t // 2 + 1))
                    c0, c1 = cg[:, (t % 2) * 2, :], cg[:, (t % 2) * 2 + 1, :]
                    link(tsc(c0, c0, gk[:, 0, t:t + 1], ALU.mult))
                    signal(stt(c0, c1, gk[:, 1, t:t + 1], c0, ALU.mult, ALU.add), "combined")
                    dve.wait_ge(sem("comb_turned"), NT * l + t + 1)
                    for k in range(KD):
                        xs = xT[:, k, t * P:(t + 1) * P]
                        ps = PS[:, 2 * (t % 2) + k // 4, (k % 4) * P:(k % 4 + 1) * P]
                        ins = stt(xs, ps, mod[:, l, 40 + k:41 + k], xs, ALU.mult, ALU.add)
                        if k < KD - 1:
                            link(ins)
                    signal(ins, "comb_added")
                signal(dve.tensor_copy(lsum[:, 0:1], lsum[:, 1:2]), "x_ready")

            link(dve.memset(lsum, 0.0))
            lower_bounds()
            lower_bounds_end()
            dve.wait_ge(sem("pool_const"), 2)
            ada_chunks(dve, link, 0)
            modulation(0)
            norm(0)
            projections(0)
            linear_attention(0)
            rwkv()
            modulation(1)
            outproj(0)
            norm(1)
            experts(0)
            link(dve.memset(f2(Cp), 0.0))
            norm(2)
            projections(1)
            linear_attention(1)
            ssd()
            outproj(1)
            norm(3)
            experts(1)
            norm(4)


_INS = ['x', 'c', 'norm_gain', 'w_ada', 'b_ada', 'w_in_even', 'w_in_odd', 'w_out', 'a_mu', 'a_w0', 'a_w_up', 'a_a0',
        'a_a_up', 'a_g_up', 'a_k_k', 'a_k_a', 'a_r_k', 'a_ln_gain', 'a_ln_bias', 'b_alpha_up', 'b_alpha_bias',
        'b_norm_gain', 'c_lb', 'c_norm_gain', 'd_conv_w', 'd_conv_b', 'd_dt_bias', 'd_a_log', 'd_skip', 'd_norm_gain',
        'w_router', 'router_bias', 'w_gate', 'w_up', 'w_down', 'final_gain']


def kernel(**inputs):
    import numpy as np
    import concourse.bacc as bacc
    from concourse.bass_utils import run_bass_kernel_spmd

    nc = bacc.Bacc("TRN2", target_bir_lowering=False, num_devices=1)
    arrays, aps = {}, {}
    for name in _INS:
        a = np.ascontiguousarray(inputs[name])
        arrays[f"in_{name}_dram"] = a
        aps[name] = nc.dram_tensor(f"in_{name}_dram", a.shape, mybir.dt.from_np(a.dtype), kind="ExternalInput").ap()
    out = nc.dram_tensor("out_0_dram", (1, T, D), F32, kind="ExternalOutput").ap()
    trunk(nc, aps, out)
    r = run_bass_kernel_spmd(nc, [arrays], core_ids=[0])
    return r.results[0]["out_0_dram"]
```

```python
from contextlib import ExitStack

import concourse.bass as bass
from concourse import mybir

F32 = mybir.dt.float32
I32 = mybir.dt.int32
ALU = mybir.AluOpType
ACT = mybir.ActivationFunctionType
AX_X = mybir.AxisListType.X

P = 128
D = 1024
T = 512
KD = D // P
NT = T // P
DEPTH = 2
EPS = 1e-6
HALF = D // 2
RW = 0.6065306597126334
RW_CHUNK = 64
GN_EPS = 64e-5
E = 16
GRP = 4
FE = 512
MAX_BLOCKS = 24
BIG = 1e30
RING = 3
SLOT = 8 * 512

ROWS1 = [("a_mu", 14), ("a_w0", 4), ("a_a0", 4), ("a_k_k", 4), ("a_k_a", 4), ("a_r_k", 4), ("a_ln_gain", 4),
         ("a_ln_bias", 4), ("b_alpha_bias", 2), ("b_norm_gain", 1), ("c_lb", 4), ("c_norm_gain", 1),
         ("d_conv_w", 24), ("d_conv_b", 6), ("d_norm_gain", 4), ("final_gain", 8)]
ROWS2 = [("b_ada", 96), ("norm_gain", 32)]


def columns():
    at = {}
    for tile, rows in enumerate((ROWS1, ROWS2)):
        c = 0
        for name, n in rows:
            at[name] = (tile, c)
            c += n
    return at


def chunk_plan():
    plan = [("ada", 0, i) for i in range(12)] + [("in", 0, i) for i in range(7)]
    plan += [None] + [("out", 0, i) for i in range(2)]
    plan += [("in", 1, i) for i in range(6)] + [("out", 1, i) for i in range(2)]
    return plan


IN_PIECES = [
    [[(1536, 512)], [(2048, 256), (2816, 16)], [(2304, 512)], [(2832, 512)], [(0, 512)], [(512, 512)], [(1024, 512)]],
    [[(0, 512)], [(512, 512)], [(1024, 512)], [(1536, 512)], [(2048, 512)], [(2560, 264)]],
]


def zone(tensor, start, end):
    place = [start]

    def take(*shape):
        n = 1
        for size in shape:
            n *= size
        ap = tensor[:, place[0]:place[0] + n]
        place[0] += n
        assert place[0] <= end
        if len(shape) == 2:
            ap = ap.rearrange("p (a b) -> p a b", b=shape[1])
        if len(shape) == 3:
            ap = ap.rearrange("p (a b c) -> p a b c", b=shape[1], c=shape[2])
        return ap

    return take, place


def bc(ap, n, at):
    u = ap.unsqueeze(at)
    shape = list(u.shape)
    shape[at] = n
    return u.to_broadcast(shape)


def trunk(nc, A, out):
    h_dram = nc.dram_tensor("h_rows", [T, D], F32, kind="Internal").ap()
    y_dram = nc.dram_tensor("expert_rows", [MAX_BLOCKS * P, D], F32, kind="Internal").ap()
    COL = columns()
    PLAN = chunk_plan()

    with ExitStack() as ctx:
        def sb(name, cols, dt=F32):
            return ctx.enter_context(nc.sbuf_tensor(name, [P, cols], dt))

        made = {}

        def sem(name):
            if name not in made:
                made[name] = ctx.enter_context(nc.semaphore(name))
            return made[name]

        PS = ctx.enter_context(nc.psum_tensor("banks", [P, 8, 512], F32))

        ring = sb("ring", RING * SLOT)
        xT_ = sb("x_features", KD * T)
        xT = xT_[:, :].rearrange("p (k t) -> p k t", t=T)
        h_ = sb("h_features", KD * T)
        h = h_[:, :].rearrange("p (k t) -> p k t", t=T)
        y_ = sb("y_features", KD * T)
        y = y_[:, :].rearrange("p (k t) -> p k t", t=T)
        work = sb("work", 20992)
        KEEP = 7168

        cst, _ = zone(sb("constants", 128 * 19 + 1024), 0, 128 * 19 + 1024)
        ident = cst(P)
        ones = cst(P)
        upper = cst(P)
        headones = cst(P)
        strict_up = cst(P)
        strict_lo = cst(P)
        incl_up = cst(P)
        LV = [1, 2, 4, 8, 16, 32, 64]
        lev_up = {hh: cst(P) for hh in LV}
        lev_lo = {hh: cst(P) for hh in LV[:5]}
        reset64 = cst(T)
        reset128 = cst(T)

        small, _ = zone(sb("small", 3608), 0, 3608)
        prm = small(2, P)
        mod = small(2, 48)
        amul = small(2, 2, 8)
        cond = small(8)

        wup = small(512)
        gup = small(512)
        alup = small(256)
        wr = small(8, E)
        rs = work[:, 20480:20992]
        rs_skip = work[:, 8192:8200]
        cexp = work[:, 8200:8208]
        acc = small(2, 512)
        negw0 = small(4)
        nega0 = small(4)
        nabias = small(2)
        omu = small(14)
        lb = small(2)
        omlb = small(2)
        lbt = small(12)
        dtb = small(8)
        alog = small(8)
        skipc = small(4)
        rbias = small(E)
        iota16 = small(E)
        iota24 = small(MAX_BLOCKS)
        iota128 = small(P)
        tokid = small(NT)
        pidx = small(1)
        epsc = small(4)
        ebl = small(2, NT)
        lsum = small(8)
        idx_tok = sb("idx_tok", MAX_BLOCKS + 2, I32)
        scratch_i = sb("scratch_ints", P, I32)
        idx_cur = sb("idx_cur", 2, I32)
        idx_dest = sb("idx_dest", 2 * NT, I32)
        table = sb("block_experts", 32, I32)

        def prm_col(name, i=0, n=1):
            tile, c = COL[name]
            return prm[:, tile, c + i:c + i + n]

        def slot(n, cols):
            s = n % RING
            return ring[:, s * SLOT:s * SLOT + 8 * cols].rearrange("p (k n) -> p k n", n=cols)

        def slot_w(kind, l, i):
            if kind == "in":
                return sum(w for _, w in IN_PIECES[l][i])
            return 512

        where = {c: n for n, c in enumerate(PLAN) if c is not None}

        slot_loaded = [sem(f"slot{i}_loaded") for i in range(RING)]

        def arrived(eng, key):
            n = where[key]
            eng.wait_ge(slot_loaded[n % RING], 16 * sum(key is not None for key in PLAN[n % RING:n + 1:RING]))

        def ring_ap(key):
            n = where[key]
            return slot(n, slot_w(*key))

        def w_src(key):
            kind, l, i = key
            if kind == "ada":
                return A["w_ada"][l].rearrange("(k p) n -> p k n", p=P)[:, :, i * 512:(i + 1) * 512]
            if kind == "out":
                return A["w_out"][l].rearrange("(k p) n -> p k n", p=P)[:, :, i * 512:(i + 1) * 512]
            w = (A["w_in_even"], A["w_in_odd"])[l][0].rearrange("(k p) n -> p k n", p=P)
            c, n = IN_PIECES[l][i][0]
            return w[:, :, c:c + n]

        ring2 = [work[:, 4096 * i:4096 * (i + 1)] for i in range(3)]
        mo, mo_at = zone(work, 3 * 4096, 20992)
        xg = mo(2, D)
        xTb = mo(8, P)
        sgt = mo(FE)
        actb = mo(FE)
        aT = mo(4, P)
        yb = mo(D)
        ro, _ = zone(work, mo_at[0], 20480)
        moe_w = []
        for j in range(2):
            base = [ring[:, s * SLOT:s * SLOT + 4096] for s in range(3)] if j == 0 else ring2
            moe_w.append((base[0].rearrange("p (k n) -> p k n", n=512), base[1].rearrange("p (k n) -> p k n", n=512),
                          base[2].rearrange("p (k n) -> p k n", n=1024)))

        cg = zone(work, 0, 3 * 4096)[0](4, D)

        sc = ro(NT, E)
        sel = ro(NT, E)
        r1 = ro(NT, 8)
        r2 = ro(NT, 8)
        gs = ro(NT, GRP)
        gm = ro(NT, GRP)
        m1 = ro(NT)
        idc = ro(NT, E)
        oh = ro(2, NT * E)
        both = ro(NT, E)
        gk = ro(2, NT)
        gsum = ro(NT)
        rank = ro(NT, E)
        cnt = ro(E)
        nov = ro(E)
        ove = ro(E)
        over = ro(E)
        qq = ro(NT, E)
        q0 = ro(NT, E)
        blk = ro(NT, E)
        rin = ro(NT, E)
        selb = ro(2, NT)
        selr = ro(2, NT)
        destf = ro(2, NT)
        ohb = ro(MAX_BLOCKS)
        ohr = ro(P)
        tabf = ro(32)

        la, la_at = zone(work, KEEP, 20992)
        lq = la(2, T)
        lk = la(2, T)
        lg = la(2, T)
        lv = la(NT, 512)
        lgate = la(4, T)
        lqp = la(4, T)
        lkp = la(2, T)
        lA = la(16, P)
        le = la(1024)
        lS = la(2, P)
        lsq = lqp
        lrms = work[:, KEEP:KEEP + 4 * T].rearrange("p (a b) -> p a b", b=T)

        kz, _ = zone(work, 0, KEEP)
        rr = kz(4, T)
        kk_ = kz(4, T)
        vv = kz(4, T)
        wad = kz(T)
        gdp = kz(T)
        rz, rz_at = zone(work, KEEP, 20992)
        LKT = rz(8, P)
        PKT = rz(8, P)
        PBT = rz(8, P)
        Gm = rz(8, P)
        G2 = rz(8, P)
        uz, _ = zone(work, rz_at[0] - 2048, rz_at[0])
        R0 = uz(512)
        Un = uz(512)
        U0 = uz(512)
        WnT = uz(4, P)
        ez, _ = zone(ring, 0, 2 * SLOT)
        SGA, CS, EB, KK, KT, KA, BE, B1, ALP, RHO = [[take(m, P) for take in (ez, rz)]
                                                     for m in (8, 4, 4, 4, 4, 4, 4, 4, 8, 8)]
        SG = [ap[:, 0:4, :] for ap in SGA]
        AA = [ap[:, 4:8, :] for ap in SGA]
        Vt = rz(512)
        kaT = rz(512)
        beT = rz(512)
        alT = rz(512)
        XT = h_[:, 0:1024].rearrange("p (a b) -> p a b", b=P)
        X = h_[:, 1024:2048].rearrange("p (a b) -> p a b", b=P)
        Tm = h_[:, 2048:3072].rearrange("p (a b) -> p a b", b=P)
        TT = h_[:, 3072:4096].rearrange("p (a b) -> p a b", b=P)
        ST = small(8, 64)

        sz, _ = zone(work, 0, KEEP)
        zs = sz(4, T)
        xsF = sz(4, T)
        Bf = sz(T)
        Cp = sz(2, T)
        dt = sz(NT, 8)
        da = sz(NT, 8)
        dz = sz(NT, 8)
        dz2 = sz(NT, 8)
        dpl = sz(NT, 8)
        cumc = sz(NT, 8)
        dte = sz(8)
        sw, _ = zone(work, KEEP, 20992)
        cva = acc[:, 0, :]
        cve = acc[:, 1, :]
        xsT = sw(NT, 512)
        Bt = sw(NT, P)
        Es = sw(8, P)
        MT = sw(8, P)
        ec = sw(8, P)
        Csp = sw(8, P)
        xdt = sw(512)
        xdd = sw(512)
        CBm = sw(2, P)
        Sst = sw(4, 64)
        Stm = sw(4, 64)
        yF = sw(4, T)

        def pairs_of(eng, l):
            return eng.value_load(table[0:1, 30 + l:31 + l], min_val=8, max_val=MAX_BLOCKS // 2)

        def further_pairs(eng, l):
            return eng.value_load(table[0:1, 26 + l:27 + l], min_val=7, max_val=MAX_BLOCKS // 2 - 1)

        PARTS = ("gate", "up", "down")
        w_loaded = [[sem(f"l{l}_{w}_{j}_loaded") for j in ("even", "odd") for w in PARTS]
                    for l in range(DEPTH)]
        gathered = [[sem(f"l{l}_{j}_rows_gathered") for j in ("even", "odd")] for l in range(DEPTH)]

        BLOCKS = [
            [(0, 256, 128, "q", 0), (0, 384, 128, "q", 1), (0, 0, 128, "shift", 12), (0, 128, 128, "shift", 13)]
            + [(1, 0, 128, "k", 0), (1, 128, 128, "k", 1), (1, 256, 16, "lora", 0)]
            + [(2, 0, 512, "v", t) for t in range(NT)] + [(3, 128 * j, 128, "gate", j) for j in range(4)]
            + [(4 + i, 128 * j, 128, "shift", 4 * i + j) for i in range(3) for j in range(4)],
            [(0, 0, 128, "q", 0), (0, 128, 128, "q", 1), (0, 256, 128, "f", 0), (0, 384, 128, "f", 1)]
            + [(1, 0, 512, "v", t) for t in range(NT)] + [(2, 128 * j, 128, "gate", j) for j in range(4)]
            + [(3, 128 * j, 128, "z", j) for j in range(4)] + [(4, 128 * j, 128, "conv", j) for j in range(4)]
            + [(5, 0, 128, "conv", 4), (5, 128, 128, "conv", 5), (5, 256, 8, "dt", 0)],
        ]
        NB = [len(b) for b in BLOCKS]
        WITH_ACT = ("shift", "gate", "f", "z")
        LOGS, SUMS, LEVELS = 0, 1, 2
        TILE_DECAYS = LEVELS + len(LV) + 1
        KEYS_TURNED = TILE_DECAYS + 1
        OUTPUTS = KEYS_TURNED + 1
        GATED = OUTPUTS + NT
        AFTER = [dict(zip((6, 7, 9, 10, 12, 13, 15, 16, 18, 19, 20, 21, 22, 23, 24, 25, 26), range(GATED + 1))),
                 dict(zip((3, 4, 6, 7, 8, 10, 11, 13, 14, 15, 16, 17, 18, 19, 20, 21, 22), range(GATED + 1)))]
        AB = 2

        def act_blocks(l, n):
            return sum(b[3] in WITH_ACT for b in BLOCKS[0][:NB[0] if l else n]) + \
                (sum(b[3] in WITH_ACT for b in BLOCKS[1][:n]) if l else 0)

        def chunk_blocks(l, i):
            return l * NB[0] + sum(b[0] <= i for b in BLOCKS[l])

        shifted = [rr[:, j, :] for j in range(4)] + [kk_[:, j, :] for j in range(4)] \
            + [vv[:, j, :] for j in range(4)] + [wad, gdp]
        lgf = lg.rearrange("p t s -> p (t s)")
        lev_n = len(LV)

        def halves(ap, hh):
            v = ap.rearrange("p (n two h) -> p n two h", two=2, h=hh)
            return v[:, :, 0, :], v[:, :, 1, :]

        def x_at(n, k):
            return [k + 1, k + 1, 9, 9 + k + 1, 18][n]

        HALVES = 24
        half_place = [y_[:, 2048 * i:2048 * (i + 1)].rearrange("p (k n) -> p k n", n=256) for i in range(2)]
        half_acc = [acc.rearrange("p a b -> p (a b)")[:, 256 * i:256 * (i + 1)] for i in range(4)]

        block = ctx.enter_context(nc.Block())

        @block.sync
        def _(sp):
            def load_half(i):
                if i < 2:
                    sp.wait_ge(sem("rows_cleared"), 16)
                else:
                    sp.wait_ge(sem("half_used"), i - 1)
                sp.dma_start(half_place[i % 2], A["w_ada"][1].rearrange("(k p) n -> p k n", p=P)
                             [:, :, 256 * i:256 * (i + 1)]).then_inc(sem(f"half_loaded{i % 2}"), 16)

            def load(n):
                if PLAN[n] == ("out", 0, 1):
                    sp.wait_ge(sem("rwkv_done"), NT - 1)
                if n >= RING and PLAN[n - RING] is not None:
                    kind, l, i = PLAN[n - RING]
                    if kind == "ada":
                        sp.wait_ge(sem("ada_used"), 12 * l + i + 1)
                    elif kind == "in":
                        sp.wait_ge(sem("proj_done"), chunk_blocks(l, i))
                    else:
                        sp.wait_ge(sem("outproj_done"), 8 * l + 4 * (i + 1))
                kind, l, i = PLAN[n]
                dst, src = ring_ap(PLAN[n]), w_src(PLAN[n])
                if kind == "in" and len(IN_PIECES[l][i]) == 2:
                    (_, w), (c2, w2) = IN_PIECES[l][i]
                    sp.dma_start(dst[:, :, w:w + w2], A["w_in_even"][0].rearrange("(k p) n -> p k n", p=P)
                                 [:, :, c2:c2 + w2]).then_inc(sem("second_piece_loaded"), 16)
                    dst = dst[:, :, 0:w]
                sp.dma_start(dst, src).then_inc(slot_loaded[n % RING], 16)

            ws = [A["w_gate"], A["w_up"], A["w_down"]]
            n = 0
            for l in range(DEPTH):
                while n < len(PLAN) and (PLAN[n] is None or PLAN[n][1] <= l):
                    if PLAN[n] is not None:
                        load(n)
                    if l == 0 and 14 <= n < 18:
                        for i in range(4 * (n - 14), 4 * (n - 13)):
                            load_half(i)
                    if n == 18:
                        for i in range(16, HALVES):
                            load_half(i)
                    n += 1
                sp.wait_ge(sem("outproj_done"), 8 * (l + 1))
                sp.wait_ge(sem("x_ready"), 9 * l + 1)
                for j in range(2):
                    for i in range(3):
                        sp.dma_start(moe_w[j][i], ws[i][l, j].rearrange("(k p) n -> p k n", p=P))\
                          .then_inc(w_loaded[l][3 * j + i], 16)
                sp.wait_ge(sem("table_ready"), l + 1)
                further = further_pairs(sp, l)
                with sp.Fori(0, further) as it:
                    for j in range(2):
                        e = sp.value_load(table[0:1, bass.ds(it * 2 + (j + 2), 1)], min_val=0, max_val=E - 1)
                        for i in range(3):
                            sp.wait_ge(sem(f"l{l}_{PARTS[i]}_done"), it * 2 + (j + 1))
                            src = ws[i][l][bass.ds(e, 1)].rearrange("o (k p) n -> p (o k) n", p=P)
                            sp.dma_start(moe_w[j][i], src).then_inc(w_loaded[l][3 * j + i], 16)
                sp.wait_ge(sem(f"l{l}_down_done"), further * 2 + 2)
                sp.sem_inc(sem("passed"), 1)

        @block.gpsimd
        def _(pool):
            steps = [0]

            def link(ins):
                steps[0] += 1
                ins.then_inc(sem("pool_order"), 1)
                pool.wait_ge(sem("pool_order"), steps[0])

            def fill(ap, value):
                link(pool.memset(ap, value))

            def keep_where(ap, base, pattern, mult, cmp=ALU.is_ge, fill_value=0.0):
                link(pool.affine_select(out=ap, in_=ap, compare_op=cmp, fill=fill_value, base=base,
                                        pattern=pattern, channel_multiplier=mult))

            fill(ident, 0.0)
            keep_where(ident, 0, [[-1, P]], 1, ALU.not_equal, 1.0)
            fill(epsc[:, 0:1], EPS)
            fill(epsc[:, 1:2], GN_EPS)
            fill(epsc[:, 2:3], 1e-12)
            fill(epsc[:, 3:4], 1.0)
            pool.memset(ones, 1.0).then_inc(sem("pool_const"), 1)
            fill(upper, 1.0)
            keep_where(upper, 0, [[1, P]], -1)
            fill(headones, 1.0)
            hv = headones.rearrange("p (n h) -> p n h", h=64)
            keep_where(hv, 0, [[-64, 2], [0, 64]], 1)
            keep_where(hv, 63, [[64, 2], [0, 64]], -1)
            for m, base, step, mult in ((strict_up, -1, 1, -1), (incl_up, 0, 1, -1), (strict_lo, -1, -1, 1)):
                link(pool.tensor_copy(m, headones))
                keep_where(m, base, [[step, P]], mult)
            for hh in LV:
                for m, half, lo in ((lev_up.get(hh), 1, 0), (lev_lo.get(hh), 0, hh)):
                    if m is None:
                        continue
                    fill(m, 0.0)
                    v = m.rearrange("p (n two h) -> p n two h", two=2, h=hh)[:, :, half, :]
                    nb = P // (2 * hh)
                    fill(v, 1.0)
                    keep_where(v, -lo, [[-2 * hh, nb], [0, hh]], 1)
                    keep_where(v, lo + hh - 1, [[2 * hh, nb], [0, hh]], -1)
            for m, c in ((reset64, 64), (reset128, 128)):
                fill(m, 1.0)
                fill(m.rearrange("p (n c) -> p n c", c=c)[:, :, 0:1], 0.0)
            for ap, n, mult in ((iota16, E, 0), (iota24, MAX_BLOCKS, 0), (iota128, P, 0), (pidx, 1, 1)):
                link(pool.iota(scratch_i[:, 0:n], pattern=[[1, n]], base=0, channel_multiplier=mult))
                link(pool.tensor_copy(ap, scratch_i[:, 0:n]))
            link(pool.iota(scratch_i[:, 0:NT], pattern=[[P, NT]], base=0, channel_multiplier=1))
            link(pool.tensor_copy(tokid, scratch_i[:, 0:NT]))
            pool.memset(idx_tok[:, :], 0).then_inc(sem("pool_const"), 1)

            pool.wait_ge(sem("setup_step"), 2)
            pool.wait_ge(sem("ada_summed"), 12)
            for i in range(HALVES):
                pool.wait_ge(sem(f"half_loaded{i % 2}"), 16 * (i // 2 + 1))
                if i >= 4:
                    pool.wait_ge(sem("half_summed"), i - 3)
                w = half_place[i % 2]
                link(pool.tensor_tensor(w, w, cond.unsqueeze(2).to_broadcast([P, KD, 256]), ALU.mult))
                link(pool.tensor_tensor(w[:, 0:4, :], w[:, 0:4, :], w[:, 4:8, :], ALU.add))
                link(pool.tensor_tensor(w[:, 0:2, :], w[:, 0:2, :], w[:, 2:4, :], ALU.add))
                pool.tensor_tensor(half_acc[i % 4], w[:, 0, :], w[:, 1, :], ALU.add).then_inc(sem("half_used"), 1)

            for l in range(DEPTH):
                pool.wait_ge(sem("table_ready"), l + 1)
                pool.wait_ge(sem(f"l{l}_rows_stored"), 16)
                further = further_pairs(pool, l)
                sg, sc_ = sem(f"l{l}_xt_turned"), sem(f"l{l}_idx_copied")

                def gather(b, j, it_wait, n):
                    if it_wait is not None:
                        pool.wait_ge(sg, it_wait)
                    pool.tensor_copy(idx_cur[:, j:j + 1], idx_tok[:, b]).then_inc(sc_, 1)
                    pool.wait_ge(sc_, n)
                    pool.sem_inc(sem("passed"), 1)
                    pool.indirect_dma_start(
                        xg[:, j, :], None, h_dram, bass.IndirectOffsetOnAxis(ap=idx_cur[:, j:j + 1], axis=0))\
                        .then_inc(gathered[l][j], 16)

                gather(bass.ds(0, 1), 0, None, 1)
                gather(bass.ds(1, 1), 1, None, 2)
                with pool.Fori(0, further) as it:
                    for j in range(2):
                        gather(bass.ds(it * 2 + (j + 2), 1), j, it * 2 + (j + 1), it * 2 + (j + 3))
                gather(bass.ds(further * 2 + 2, 1), 0, further * 2 + 1, further * 2 + 3)

                pool.wait_ge(sem(f"l{l}_rows_stored"), (further * 2 + 3) * 16)
                pool.sem_inc(sem("passed"), 1)
                for t in range(NT):
                    if t >= 2:
                        pool.wait_ge(sem("comb_turned"), NT * l + t - 1)
                    for k in range(2):
                        pool.indirect_dma_start(
                            cg[:, (t % 2) * 2 + k, :], None, y_dram,
                            bass.IndirectOffsetOnAxis(ap=idx_dest[:, k * NT + t:k * NT + t + 1], axis=0))\
                            .then_inc(sem(f"expert_rows{t % 2}"), 16)

        @block.scalar
        def _(act):
            steps = [0]

            def link(ins):
                steps[0] += 1
                ins.then_inc(sem("act_order"), 1)
                act.wait_ge(sem("act_order"), steps[0])

            def sigmoid(ap, src):
                link(act.activation(ap, src, ACT.Exp, scale=-1.0))
                link(act.activation(ap, ap, ACT.Ln, bias=epsc[:, 3:4]))
                return act.activation(ap, ap, ACT.Exp, scale=-1.0)

            act.dma_start(work[0:KD, 4096 + 2 * P:4096 + 3 * P], A["c"][0].rearrange("(k p) -> k p", p=P)).then_inc(sem("c_loaded"), 16)
            act.dma_start(work[:, 0:4096].rearrange("p (a d) -> p a d", d=D),
                         A["x"][0].rearrange("(a p) d -> p a d", p=P)).then_inc(sem("x_loaded"), 16)

            def rows_of(name):
                a = A[name]
                names = "a b c d"[:2 * len(a.shape) - 1]
                flat = a.rearrange(f"{names} -> ({names})") if len(a.shape) > 1 else a
                return flat.rearrange("(r c) -> r c", c=P)

            for tile, rows in enumerate((ROWS1, ROWS2)):
                c = 0
                for name, k in rows:
                    act.dma_start(work[c:c + k, 4096 + tile * P:4096 + (tile + 1) * P],
                                 rows_of(name)).then_inc(sem("rows_loaded"), 16)
                    c += k

            act.wait_ge(sem("pool_const"), 1)
            act.wait_ge(sem("x_turned"), 1)
            sigmoid(cexp, PS[:, 5, 0:KD]).then_inc(sem("setup_exp"), 1)

            act.dma_start(wup[0:64, :], A["a_w_up"][0]).then_inc(sem("params_loaded"), 16)
            act.dma_start(wup[64:128, :], A["a_a_up"][0]).then_inc(sem("params_loaded"), 16)
            act.dma_start(gup, A["a_g_up"][0]).then_inc(sem("params_loaded"), 16)
            act.dma_start(alup[0:16, :], A["b_alpha_up"][0]).then_inc(sem("params_loaded"), 16)
            act.dma_start(wr, A["w_router"].rearrange("(k p) e -> p k e", p=P)).then_inc(sem("params_loaded"), 16)
            act.dma_start(dtb, A["d_dt_bias"].to_broadcast([P, 8])).then_inc(sem("params_loaded"), 16)
            act.dma_start(alog, A["d_a_log"].to_broadcast([P, 8])).then_inc(sem("params_loaded"), 16)
            act.dma_start(rbias, A["router_bias"].unsqueeze(0).to_broadcast([P, E])).then_inc(sem("params_loaded"), 16)
            act.dma_start(rs_skip, A["d_skip"].to_broadcast([P, 8])).then_inc(sem("params_loaded"), 16)

            act.wait_ge(sem("setup_step"), 1)
            act.dma_start(y_dram[E * P:, :].rearrange("(b p) d -> p b d", p=P), bc(y_[:, 0:D], MAX_BLOCKS - E, 1))\
               .then_inc(sem("rows_cleared"), 16)

            for k in range(KD):
                act.wait_ge(sem("x_turned"), k + 2)
                act.activation(xT[:, k, :], PS[:, k % 4, :], ACT.Copy).then_inc(sem("x_copied"), 1)

            act.wait_ge(sem("setup_step"), 3)
            act.activation(lbt[:, 4:8], lbt[:, 4:8], ACT.Exp).then_inc(sem("setup_exp"), 1)

            def norm(n):
                l, place = n // 2, n % 2
                for k in range(KD):
                    act.wait_ge(sem("x_ready" if n else "x_copied"), x_at(n, k))
                    act.activation(h[:, k, :], xT[:, k, :], ACT.Square).then_inc(sem("sq_ready"), 1)
                act.wait_ge(sem("ms_ready"), n + 1)
                link(act.activation(rs, PS[:, 6, :], ACT.Ln, bias=epsc[:, 0:1], scale=1.0 / D))
                act.activation(rs, rs, ACT.Exp, scale=-0.5).then_inc(sem("rstd_ready"), 1)
                if n < 4:
                    act.wait_ge(sem("amul_ready"), l + 1)
                for k in range(KD):
                    act.wait_ge(sem("xn_ready"), KD * n + k + 1)
                    if n < 4:
                        act.activation(h[:, k, :], h[:, k, :], ACT.Identity, scale=amul[:, l, place, k:k + 1],
                                       bias=mod[:, l, 24 * place + k:24 * place + k + 1]).then_inc(sem("h_ready"), 1)
                    else:
                        act.activation(h[:, k, :], h[:, k, :], ACT.Copy, scale=prm_col("final_gain", k))\
                           .then_inc(sem("h_ready"), 1)

            def projections(l):
                for n, (c, c0, w, kind, j) in enumerate(BLOCKS[l]):
                    ps = PS[:, n % 2, :]
                    if kind in WITH_ACT:
                        act.wait_ge(sem("proj_done"), l * NB[0] + n + 1)
                        if kind == "shift":
                            ins = act.activation(shifted[j], ps, ACT.Copy, scale=omu[:, j:j + 1])
                        else:
                            ins = sigmoid({"gate": lgate, "f": lg, "z": zs if l else None}[kind][:, j, :], ps)
                        ins.then_inc(sem("proj_act"), 1)
                    if kind == "conv":
                        act.wait_ge(sem("proj_copied"), NB[0] + n + 1)
                        sigmoid(cve, cva).then_inc(sem("conv_act"), 1)
                    if l == 0 and n == 5:
                        act.wait_ge(sem("proj_copied"), 4)
                        link(act.activation(wad[0:64, :], wad[0:64, :], ACT.Tanh))
                        sigmoid(gdp, gdp).then_inc(sem("setup_exp"), 1)
                    if n in AFTER[l]:
                        attention(l, AFTER[l][n])

            def attention(l, step):
                level = step - LEVELS
                if step == LOGS and l == 0:
                    act.wait_ge(sem("log_pre"), 1)
                    link(act.activation(le, le, ACT.Exp))
                    act.activation(le, le, ACT.Ln, bias=epsc[:, 3:4]).then_inc(sem("log_done"), 1)
                elif step == LOGS:
                    act.wait_ge(sem("log_pre"), 2)
                    act.activation(lgf, lgf, ACT.Ln).then_inc(sem("log_done"), 1)
                elif step == SUMS or 0 <= level < lev_n - 1:
                    n = 0 if step == SUMS else level + 1
                    act.wait_ge(sem("lev_diff"), lev_n * l + n + 1)
                    act.activation(le, le, ACT.Exp).then_inc(sem("lev_exp"), 1)
                elif step == TILE_DECAYS:
                    act.wait_ge(sem("lev_ready"), (lev_n + 1) * (l + 1))
                    act.activation(le, lgf, ACT.Exp).then_inc(sem("tile_decay"), 1)
                    act.wait_ge(sem("end_keys"), 2 * l + 1)
                    act.activation(le, le, ACT.Exp).then_inc(sem("tile_decay"), 1)
                elif step == GATED:
                    act.wait_ge(sem("o_ready"), l + 1)
                    for hd in range(4):
                        act.activation(lsq[:, hd, :], PS[:, AB + hd, :], ACT.Square).then_inc(sem("o_sq"), 1)
                    for hd in range(4):
                        act.wait_ge(sem("o_ms"), 4 * l + hd + 1)
                        link(act.activation(lrms[:, hd, :], PS[:, hd % 2, :], ACT.Ln, bias=epsc[:, 0:1],
                                            scale=1.0 / P))
                        act.activation(lrms[:, hd, :], lrms[:, hd, :], ACT.Exp, scale=-0.5).then_inc(sem("o_rstd"), 1)

            def f2(ap):
                return ap.rearrange("p a b -> p (a b)")

            def front(t, piece):
                sga, sg, aa, cs, eb, b1 = (buffer[t % 2] for buffer in (SGA, SG, AA, CS, EB, B1))
                if piece == 0:
                    if t >= 2:
                        act.wait_ge(sem("rwkv_done"), t - 1)
                    act.wait_ge(sem("lora_done"), 2 * t + 1)
                    for j in range(4):
                        act.activation(sg[:, j, :], PS[:, 6, j * P:(j + 1) * P], ACT.Exp, scale=-1.0,
                                       bias=negw0[:, j:j + 1])
                        ins = act.activation(aa[:, j, :], PS[:, 7, j * P:(j + 1) * P], ACT.Exp, scale=-1.0,
                                             bias=nega0[:, j:j + 1])
                    link(ins)
                    link(act.activation(sga, sga, ACT.Ln, bias=epsc[:, 3:4]))
                    act.activation(sga, sga, ACT.Exp, scale=-1.0).then_inc(sem("lora_exp"), 1)
                elif piece == 1:
                    act.wait_ge(sem("lora_done"), 2 * t + 2)
                    act.activation(y[:, 0:4, t * P:(t + 1) * P], PS[:, 6, :].rearrange("p (a b) -> p a b", b=P),
                                   ACT.Copy).then_inc(sem("gate_copied"), 1)
                    act.wait_ge(sem("cs_ready"), t + 1)
                    act.activation(eb, cs, ACT.Exp, scale=-RW)
                    link(act.activation(sg, sg, ACT.Exp, scale=-RW))
                    act.activation(cs, cs, ACT.Exp, scale=RW).then_inc(sem("decays_ready"), 1)
                elif piece == 2:
                    act.wait_ge(sem("kk_ss"), t + 1)
                    link(act.activation(f2(b1), PS[:, 7, :], ACT.Ln, bias=epsc[:, 2:3]))
                    act.activation(b1, b1, ACT.Exp, scale=-0.5).then_inc(sem("kk_rn"), 1)

            def turned(t):
                act.wait_ge(sem("turns"), t + 1)
                for i, dst in enumerate((Vt, kaT, beT)):
                    act.activation(dst, PS[:, i, :], ACT.Copy)
                act.activation(alT, PS[:, 4, :], ACT.Copy).then_inc(sem("turned"), 1)

            def rwkv():
                act.wait_ge(sem("half_used"), HALVES)
                for piece in range(3):
                    front(0, piece)
                turned(0)
                for t in range(NT):
                    for n in range(5):
                        if n < 4:
                            act.wait_ge(sem("g_ready"), 9 * t + 2 * n + 1)
                            act.activation(Gm, PS[:, 0:2, :].rearrange("p a (b c) -> p (a b) c", c=P), ACT.Copy)\
                               .then_inc(sem("g_copied"), 1)
                        act.wait_ge(sem("g_ready"), 9 * t + (2 * n + 2 if n < 4 else 9))
                        act.activation(G2, PS[:, 2:4, :].rearrange("p a (b c) -> p (a b) c", c=P), ACT.Copy)\
                           .then_inc(sem("g_copied"), 1)
                        if t + 1 < NT:
                            front(t + 1, n)
                    act.wait_ge(sem("rw_ready"), 2 * t + 1)
                    act.activation(R0, PS[:, 2, :], ACT.Copy)
                    act.activation(f2(WnT), PS[:, 3, :], ACT.Copy).then_inc(sem("rw_copied"), 1)
                    act.wait_ge(sem("rw_ready"), 2 * t + 2)
                    act.activation(U0, PS[:, 4, :], ACT.Copy).then_inc(sem("rw_copied"), 1)
                    act.wait_ge(sem("y1_ready"), t + 1)
                    act.activation(f2(SG[t % 2]), PS[:, 6, :], ACT.Copy).then_inc(sem("ys_copied"), 1)
                    if t + 1 < NT:
                        turned(t + 1)
                    eb = EB[t % 2]
                    act.wait_ge(sem("gn_sum"), 2 * t + 2)
                    link(act.activation(f2(eb), PS[:, 7, :], ACT.Ln, bias=epsc[:, 1:2], scale=1.0 / 64))
                    act.activation(eb, eb, ACT.Exp, scale=-0.5).then_inc(sem("gn_rstd"), 1)

            def ssd():
                act.wait_ge(sem("setup_step"), 4)
                act.activation(dz, dz, ACT.Exp)
                act.activation(alog, alog, ACT.Exp).then_inc(sem("setup_exp"), 1)
                for t in range(NT):
                    act.wait_ge(sem("seg_diff"), t + 1)
                    act.activation(Es, Es, ACT.Exp).then_inc(sem("seg_exp"), 1)
                    act.activation(ec, PS[:, 2:4, :].rearrange("p a (b c) -> p (a b) c", c=P), ACT.Exp)
                    act.activation(dte, dte, ACT.Exp).then_inc(sem("seg_exp"), 1)
                act.wait_ge(sem("yz_ready"), 1)
                for j in range(4):
                    act.activation(xsT[:, j, :], yF[:, j, :], ACT.Square).then_inc(sem("o_sq"), 1)
                for g in range(2):
                    act.wait_ge(sem("o_ms"), 8 + g + 1)
                    dst = Es if g == 0 else MT
                    half = f2(dst)[:, 0:512]
                    link(act.activation(half, PS[:, g, :], ACT.Ln, bias=epsc[:, 0:1], scale=1.0 / 256))
                    act.activation(half, half, ACT.Exp, scale=-0.5).then_inc(sem("o_rstd"), 1)

            def experts(l):
                for t in range(NT):
                    act.wait_ge(sem("rows_turned"), NT * l + t + 1)
                    b = 2 * (t % 2)
                    act.activation(y_[:, t * D:(t + 1) * D], PS[:, b:b + 2, :].rearrange("p a b -> p (a b)"), ACT.Copy)\
                       .then_inc(sem("rows_copied"), 1)
                act.wait_ge(sem("rows_copied"), NT * (l + 1))
                row_dma = sem(f"l{l}_rows_stored")
                act.dma_start(h_dram.rearrange("(a p) d -> p a d", p=P),
                              y_[:, :].rearrange("p (a d) -> p a d", d=D)).then_inc(row_dma, 16)
                act.wait_ge(sem("logits_ready"), l + 1)
                act.activation(sc, PS[:, 4, 0:NT * E].rearrange("p (a b) -> p a b", b=E), ACT.Exp, scale=-1.0)\
                   .then_inc(sem("logits_exp"), 1)

                def x_copy(n):
                    act.wait_ge(sem(f"l{l}_xt_turned"), n)
                    act.activation(xTb, PS[:, 2:4, :].rearrange("p a (b c) -> p (a b) c", c=P), ACT.Copy)\
                       .then_inc(sem(f"l{l}_xt_copied"), 1)

                act.wait_ge(sem("table_ready"), l + 1)
                pairs = pairs_of(act, l)
                x_copy(1)
                with act.Fori(0, pairs) as it:
                    for j in range(2):
                        b1 = it * 2 + (j + 1)
                        act.wait_ge(sem(f"l{l}_gate_done"), b1)
                        act.activation(sgt, PS[:, 0, :], ACT.Exp, scale=-1.0).then_inc(sem(f"l{l}_gate_exp"), 1)
                        x_copy(b1 + 1)
                        act.wait_ge(sem(f"l{l}_down_done"), b1)
                        act.wait_ge(row_dma, b1 * 16)
                        act.activation(yb, PS[:, 5:7, :].rearrange("p a b -> p (a b)"), ACT.Copy)\
                           .then_inc(sem(f"l{l}_y_copied"), 1)
                        act.wait_ge(sem(f"l{l}_y_copied"), b1)
                        act.dma_start(y_dram[bass.ds((it * 2 + j) * P, P), :], yb).then_inc(row_dma, 16)

            norm(0)
            projections(0)
            rwkv()
            norm(1)
            experts(0)
            norm(2)
            projections(1)
            ssd()
            norm(3)
            experts(1)
            norm(4)
            for t in range(NT):
                act.wait_ge(sem("rows_turned"), NT * DEPTH + t + 1)
                b = 2 * (t % 2)
                act.activation(y_[:, t * D:(t + 1) * D], PS[:, b:b + 2, :].rearrange("p a b -> p (a b)"), ACT.Copy)\
                   .then_inc(sem("rows_copied"), 1)
                act.wait_ge(sem("rows_copied"), NT * DEPTH + t + 1)
                act.dma_start(out[0, t * P:(t + 1) * P, :], y_[:, t * D:(t + 1) * D]).then_inc(sem("out_stored"), 16)
            act.wait_ge(sem("out_stored"), 16 * NT)

        @block.tensor
        def _(pe):
            mm = nc.tensor.matmul
            tr = nc.tensor.transpose

            pe.wait_ge(sem("pool_const"), 1)
            pe.wait_ge(sem("c_loaded"), 16)
            tr(PS[:, 5, 0:KD], work[0:KD, 4096 + 2 * P:4096 + 3 * P], ident[0:KD, 0:KD]).then_inc(sem("x_turned"), 1)
            pe.wait_ge(sem("x_loaded"), 16)
            for k in range(KD):
                if k >= 4:
                    pe.wait_ge(sem("x_copied"), k - 3)
                for t in range(NT):
                    ins = tr(PS[:, k % 4, t * P:(t + 1) * P], work[:, t * D + k * P:t * D + (k + 1) * P], ident)
                ins.then_inc(sem("x_turned"), 1)
            pe.wait_ge(sem("rows_loaded"), 16 * (len(ROWS1) + len(ROWS2)))
            n1 = sum(n for _, n in ROWS1)
            tr(PS[:, 4, 0:n1], work[0:n1, 4096:4096 + P], ident[0:n1, 0:n1])
            tr(PS[:, 4, P:2 * P], work[:, 4096 + P:4096 + 2 * P], ident).then_inc(sem("x_turned"), 1)

            def ada_sums(i):
                pe.wait_ge(sem("ada_used"), i + 1)
                for j in range(4):
                    ins = mm(PS[:, 7, 4 * i + j:4 * i + j + 1], lhsT=acc[:, i % 2, j * P:(j + 1) * P],
                             rhs=ones[:, 0:1], start=True, stop=True)
                ins.then_inc(sem("ada_summed"), 1)

            def half_sums(i):
                pe.wait_ge(sem("half_used"), i + 1)
                for j in range(2):
                    ins = mm(PS[:, 7, 2 * i + j:2 * i + j + 1], lhsT=half_acc[i % 4][:, j * P:(j + 1) * P],
                             rhs=ones[:, 0:1], start=True, stop=True)
                ins.then_inc(sem("half_summed"), 1)

            def norm(n):
                for k in range(KD):
                    pe.wait_ge(sem("sq_ready"), KD * n + k + 1)
                    ins = mm(PS[:, 6, :], lhsT=ones, rhs=h[:, k, :], start=(k == 0), stop=(k == KD - 1))
                ins.then_inc(sem("ms_ready"), 1)

            def projections(l):
                last = -1
                for n, (c, c0, w, kind, j) in enumerate(BLOCKS[l]):
                    if c != last:
                        arrived(pe, ("in", l, c))
                        last = c
                    if kind == "lora":
                        pe.wait_ge(sem("second_piece_loaded"), 16)
                    if n >= 2:
                        pe.wait_ge(sem("proj_copied"), l * NB[0] + n - 1)
                    W = ring_ap(("in", l, c))
                    b = n % 2
                    if kind == "v":
                        for k in range(KD):
                            ins = mm(PS[:, b, :], lhsT=h[:, k, j * P:(j + 1) * P], rhs=W[:, k, 0:512],
                                     start=(k == 0), stop=(k == KD - 1))
                    elif kind == "dt":
                        for t in range(NT):
                            for k in range(KD):
                                ins = mm(PS[:, b, 8 * t:8 * t + 8], lhsT=h[:, k, t * P:(t + 1) * P],
                                         rhs=W[:, k, c0:c0 + 8], start=(k == 0), stop=(k == KD - 1))
                    else:
                        for k in range(KD):
                            if n == 0:
                                pe.wait_ge(sem("h_ready"), KD * 2 * l + k + 1)
                            ins = mm(PS[0:w, b, :], lhsT=W[:, k, c0:c0 + w], rhs=h[:, k, :],
                                     start=(k == 0), stop=(k == KD - 1))
                    ins.then_inc(sem("proj_done"), 1)
                    if l == 0 and 1 <= n <= HALVES:
                        half_sums(n - 1)
                    if n in AFTER[l]:
                        attention(l, AFTER[l][n])

            def attention(l, step):
                kdT = lq.rearrange("p a b -> p (a b)").rearrange("p (t c) -> p t c", c=256)
                if step == LOGS and l == 0:
                    pe.wait_ge(sem("proj_copied"), 7)
                    for j in range(2):
                        ins = mm(PS[:, AB + j, :], lhsT=alup[0:16, j * P:(j + 1) * P], rhs=le[0:16, 0:T],
                                 start=True, stop=True)
                    ins.then_inc(sem("alpha_ready"), 1)
                elif LEVELS <= step < TILE_DECAYS:
                    at = (lev_n + 1) * l + step - LEVELS
                    pe.wait_ge(sem("lev_ready"), at + 1)
                    if at:
                        pe.wait_ge(sem("lev_merged"), at)
                    for t in range(NT):
                        for hd in range(4):
                            ins = mm(PS[:, AB + t, hd * P:(hd + 1) * P], lhsT=lkp[:, hd // 2, t * P:(t + 1) * P],
                                     rhs=lqp[:, hd, t * P:(t + 1) * P], start=True, stop=True)
                    ins.then_inc(sem("lev_scored"), 1)
                elif step == KEYS_TURNED:
                    pe.wait_ge(sem("end_keys"), 2 * l + 2)
                    for t in range(2):
                        for j in range(2):
                            ins = tr(PS[:, 6, (2 * t + j) * P:(2 * t + j + 1) * P], lkp[:, j, t * P:(t + 1) * P], ident)
                    ins.then_inc(sem("kd_turned"), 1)
                elif OUTPUTS <= step < GATED:
                    t = step - OUTPUTS
                    if t == 0:
                        pe.wait_ge(sem("lev_merged"), (lev_n + 1) * (l + 1))
                    else:
                        pe.wait_ge(sem("ls_ready"), 3 * l + t)
                    for hd in range(4):
                        o = PS[:, AB + hd, t * P:(t + 1) * P]
                        ins = mm(o, lhsT=lv[:, t, hd * P:(hd + 1) * P], rhs=lA[:, 4 * t + hd, :],
                                 start=True, stop=(t == 0))
                        if t:
                            ins = mm(o, lhsT=lS[:, hd // 2, :], rhs=lqp[:, hd, t * P:(t + 1) * P],
                                     start=False, stop=True)
                    if t == NT - 1:
                        ins.then_inc(sem("o_ready"), 1)
                        return
                    if t == 0:
                        pe.wait_ge(sem("kdT_ready"), l + 1)
                    for hd in range(4):
                        p0 = 64 * (hd % 2)
                        ins = mm(PS[p0:p0 + 64, 6, (hd // 2) * P:(hd // 2 + 1) * P], lhsT=kdT[:, t, hd * 64:hd * 64 + 64],
                                 rhs=lv[:, t, hd * P:(hd + 1) * P], start=True, stop=True)
                    if t == 0:
                        for j in range(2):
                            ins = tr(PS[:, 6, (2 + j) * P:(3 + j) * P], lkp[:, j, 2 * P:3 * P], ident)
                    ins.then_inc(sem("ls_ps"), 1)
                elif step == GATED:
                    pe.wait_ge(sem("proj_copied"), NB[0] + l * NB[1])
                    for hd in range(4):
                        pe.wait_ge(sem("o_sq"), 4 * l + hd + 1)
                        if hd >= 2:
                            pe.wait_ge(sem("o_rstd"), 4 * l + hd - 1)
                        mm(PS[:, hd % 2, :], lhsT=ones, rhs=lsq[:, hd, :], start=True, stop=True)\
                            .then_inc(sem("o_ms"), 1)

            def f2(ap):
                return ap.rearrange("p a b -> p (a b)")

            def front(t, piece):
                ts = slice(t * P, (t + 1) * P)
                if piece == 0:
                    if t >= 2:
                        pe.wait_ge(sem("rwkv_done"), t - 1)
                    for j in range(4):
                        js = slice(j * P, (j + 1) * P)
                        mm(PS[:, 6, js], lhsT=wup[0:64, js], rhs=wad[0:64, ts], start=True, stop=True)
                    for j in range(4):
                        js = slice(j * P, (j + 1) * P)
                        ins = mm(PS[:, 7, js], lhsT=wup[64:128, js], rhs=wad[64:128, ts], start=True, stop=True)
                    ins.then_inc(sem("lora_done"), 1)
                elif piece == 1:
                    pe.wait_ge(sem("lora_exp"), t + 1)
                    for j in range(4):
                        js = slice(j * P, (j + 1) * P)
                        ins = mm(PS[:, 6, js], lhsT=gup[:, js], rhs=gdp[:, ts], start=True, stop=True)
                    ins.then_inc(sem("lora_done"), 1)
                elif piece == 2:
                    pe.wait_ge(sem("kk_sq"), t + 1)
                    mm(PS[:, 7, :], lhsT=headones, rhs=f2(B1[t % 2]), start=True, stop=True).then_inc(sem("kk_ss"), 1)
                elif piece == 5:
                    pe.wait_ge(sem("feat_ready"), t + 1)
                    pe.wait_ge(sem("gate_copied"), t + 1)
                    mm(PS[:, 7, :], lhsT=headones, rhs=f2(B1[t % 2]), start=True, stop=True)\
                        .then_inc(sem("bonus_sum"), 1)

            def turns(t):
                pe.wait_ge(sem("st_done"), 2 * t + 1)
                for b, src in ((0, vv[:, :, t * P:(t + 1) * P]), (1, KA[t % 2]), (2, BE[t % 2]), (4, SG[t % 2])):
                    for j in range(4):
                        ins = tr(PS[:, b, j * P:(j + 1) * P], src[:, j, :], ident)
                ins.then_inc(sem("turns"), 1)

            def score(t, n):
                ka, be, alp, rho = (buffer[t % 2] for buffer in (KA, BE, ALP, RHO))
                b, lhs, rhs, flip = ((5, be, alp, 0), (0, be, alp, 1), (2, ka, alp, 0), (5, ka, rho, 0),
                                     (0, be, rho, 0))[n]
                if n == 0 and t:
                    pe.wait_ge(sem("gn_in"), 2 * t - 1)
                if n == 1:
                    pe.wait_ge(sem("turned"), t + 1)
                if n >= 3:
                    pe.wait_ge(sem("score_copied"), 5 * t + n - 2)
                for hd in range(8):
                    o = PS[:, b + hd // 4, (hd % 4) * P:(hd % 4 + 1) * P]
                    left, right = lhs[:, hd // 2, :], rhs[:, hd, :]
                    if flip:
                        left, right = right, left
                    ins = mm(o, lhsT=left, rhs=right, start=True, stop=True)
                ins.then_inc(sem("score_ready"), 1)

            def heads(bank, lhs, rhs, name):
                for hd in range(8):
                    o = PS[:, bank + hd // 4, (hd % 4) * P:(hd % 4 + 1) * P]
                    ins = mm(o, lhsT=lhs[:, hd, :], rhs=rhs[:, hd, :], start=True, stop=True)
                ins.then_inc(sem(name), 1)

            def inversion(t):
                pe.wait_ge(sem("score_copied"), 5 * t + 5)
                for n in range(5):
                    pe.wait_ge(sem("inv_ready"), 10 * t + 2 * n + 1)
                    if n < 4:
                        heads(0, XT, Tm, "g_ready")
                    heads(2, X, TT, "g_ready")
                    if n < 4:
                        pe.wait_ge(sem("g_copied"), 9 * t + 2 * n + 1)
                        heads(4, TT, Gm, "p_ready")
                    pe.wait_ge(sem("g_copied"), 9 * t + (2 * n + 2 if n < 4 else 9))
                    heads(0, Tm, G2, "p_ready")
                    if t + 1 < NT:
                        front(t + 1, n)
                if t + 1 < NT:
                    front(t + 1, 5)
                pe.wait_ge(sem("inv_ready"), 10 * (t + 1))

            def solve(t):
                for hd in range(8):
                    mm(PS[:, 2, hd * 64:hd * 64 + 64], lhsT=LKT[:, hd, :], rhs=Vt[:, hd * 64:hd * 64 + 64],
                       start=True, stop=True)
                for hd in range(8):
                    p0 = 64 * (hd % 2)
                    ins = mm(PS[p0:p0 + 64, 3, (hd // 2) * P:(hd // 2 + 1) * P], lhsT=alT[:, hd * 64:hd * 64 + 64],
                             rhs=TT[:, hd, :], start=True, stop=True)
                ins.then_inc(sem("rw_ready"), 1)
                pe.wait_ge(sem("rw_copied"), 2 * t + 1)
                for hd in range(8):
                    ins = mm(PS[:, 4, hd * 64:hd * 64 + 64], lhsT=TT[:, hd, :], rhs=R0[:, hd * 64:hd * 64 + 64],
                             start=True, stop=True)
                ins.then_inc(sem("rw_ready"), 1)
                pe.wait_ge(sem("rw_copied"), 2 * t + 2)
                for c in range(2):
                    po = 64 * c
                    pe.wait_ge(sem("st_done"), 2 * t + c + 1)
                    for hd in range(8):
                        mm(PS[po:po + 64, 3, hd * 64:hd * 64 + 64], lhsT=WnT[:, hd // 2, po:po + 64],
                           rhs=ST[:, hd, :], start=True, stop=True)
                    for hd in range(8):
                        p0 = 64 * (hd % 2)
                        at = (hd // 2) * P + po
                        ins = mm(PS[p0:p0 + 64, 6, at:at + 64], lhsT=ST[:, hd, :], rhs=RHO[t % 2][:, hd, po:po + 64],
                                 start=True, stop=True)
                    ins.then_inc(sem("un_ready"), 1)
                    pe.wait_ge(sem("un_done"), 2 * t + c + 1)
                    for hd in range(8):
                        p0 = 64 * (hd % 2)
                        hs = slice(hd * 64, hd * 64 + 64)
                        o = PS[p0:p0 + 64, 4, (hd // 2) * 64:(hd // 2) * 64 + 64]
                        mm(o, lhsT=kaT[po:po + 64, hs], rhs=Vt[po:po + 64, hs], start=True, stop=False)
                        ins = mm(o, lhsT=beT[po:po + 64, hs], rhs=Un[po:po + 64, hs], start=False, stop=True)
                    ins.then_inc(sem("st_ps"), 1)
                for hd in range(8):
                    p0 = 64 * (hd % 2)
                    hs = slice(hd * 64, hd * 64 + 64)
                    o = PS[p0:p0 + 64, 5, (hd // 2) * P:(hd // 2 + 1) * P]
                    mm(o, lhsT=Vt[:, hs], rhs=PKT[:, hd, :], start=True, stop=False)
                    ins = mm(o, lhsT=Un[:, hs], rhs=PBT[:, hd, :], start=False, stop=True)
                ins.then_inc(sem("y1_ready"), 1)

            def head_sums(t, n):
                if n == 0 and t + 1 < NT:
                    pe.wait_ge(sem("bonus_used"), t + 2)
                pe.wait_ge(sem("gn_in"), 2 * t + n + 1)
                mm(PS[:, 7, :], lhsT=headones, rhs=f2((CS, EB)[n][t % 2]), start=True, stop=True)\
                    .then_inc(sem("gn_sum"), 1)

            def rwkv():
                pe.wait_ge(sem("yhalf"), 1)
                pe.wait_ge(sem("setup_exp"), 3)
                pe.wait_ge(sem("amul_ready"), 2)
                for piece in range(6):
                    front(0, piece)
                turns(0)
                for n in range(5):
                    score(0, n)
                for t in range(NT):
                    inversion(t)
                    solve(t)
                    if t + 1 < NT:
                        turns(t + 1)
                    head_sums(t, 0)
                    if t + 1 < NT:
                        score(t + 1, 0)
                    head_sums(t, 1)
                    if t + 1 < NT:
                        for n in range(1, 5):
                            score(t + 1, n)

            def ssd():
                pe.wait_ge(sem("yhalf"), 2)
                for t in range(NT):
                    for j in range(4):
                        tr(PS[:, t, j * P:(j + 1) * P], xsF[:, j, t * P:(t + 1) * P], ident)
                for t in range(NT):
                    ins = tr(PS[:, 4, t * P:(t + 1) * P], Bf[:, t * P:(t + 1) * P], ident)
                ins.then_inc(sem("xs_turned"), 1)
                pe.wait_ge(sem("ssd_inputs"), 1)
                mm(PS[:, 5, 0:32], lhsT=upper, rhs=da.rearrange("p a b -> p (a b)"), start=True, stop=True)\
                    .then_inc(sem("xs_turned"), 1)
                pe.wait_ge(sem("ssd_inputs"), 2)
                for t in range(NT):
                    ts = slice(t * P, (t + 1) * P)
                    if t:
                        pe.wait_ge(sem("ssd_y_copied"), t)
                    for hd in range(8):
                        mm(PS[:, 2 + hd // 4, (hd % 4) * P:(hd % 4 + 1) * P],
                           lhsT=da[:, t, hd:hd + 1].to_broadcast([P, P]), rhs=upper, start=True, stop=True)
                    for g in range(2):
                        ins = mm(PS[:, 4, g * P:(g + 1) * P], lhsT=Bf[:, ts], rhs=Cp[:, g, ts], start=True, stop=True)
                    ins.then_inc(sem("cb_ready"), 1)
                    pe.wait_ge(sem("ssd_in"), t + 1)
                    for hd in range(8):
                        p0 = 64 * (hd % 2)
                        o = PS[p0:p0 + 64, 0, (hd // 2) * P:(hd // 2 + 1) * P]
                        ins = mm(o, lhsT=xdt[:, hd * 64:hd * 64 + 64], rhs=MT[:, hd, :], start=True, stop=(t == 0))
                        if t:
                            ins = mm(o, lhsT=Sst[:, hd % 4, :], rhs=Csp[:, hd, :], start=False, stop=True)
                    ins.then_inc(sem("ssd_y_ready"), 1)
                    if t < NT - 1:
                        for g in range(2):
                            ins = mm(PS[64 * g:64 * g + 64, 1, 0:256], lhsT=Bt[:, t, 64 * g:64 * g + 64],
                                     rhs=xdd[:, 256 * g:256 * g + 256], start=True, stop=True)
                        ins.then_inc(sem("ssd_st_ps"), 1)
                for j in range(4):
                    pe.wait_ge(sem("o_sq"), 8 + j + 1)
                    ins = mm(PS[:, j // 2, :], lhsT=ones, rhs=xsT[:, j, :], start=(j % 2 == 0), stop=(j % 2 == 1))
                    if j % 2:
                        ins.then_inc(sem("o_ms"), 1)

            def outproj(l):
                pe.wait_ge(sem("mix_done"), l + 1)
                for n in range(KD):
                    if n % 4 == 0:
                        arrived(pe, ("out", l, n // 4))
                    if n >= 4:
                        pe.wait_ge(sem("x_ready"), 9 * l + n - 3)
                    W = ring_ap(("out", l, n // 4))
                    for k in range(KD):
                        ins = mm(PS[:, n % 4, :], lhsT=W[:, k, (n % 4) * P:(n % 4 + 1) * P], rhs=y[:, k, :],
                                 start=(k == 0), stop=(k == KD - 1))
                    ins.then_inc(sem("outproj_done"), 1)

            def experts(l):
                pe.wait_ge(sem("h_ready"), KD * (2 * l + 2))
                for t in range(NT):
                    for k in range(KD):
                        ins = mm(PS[:, 4, t * E:(t + 1) * E], lhsT=h[:, k, t * P:(t + 1) * P], rhs=wr[:, k, :],
                                 start=(k == 0), stop=(k == KD - 1))
                ins.then_inc(sem("logits_ready"), 1)
                for t in range(NT):
                    if t >= 2:
                        pe.wait_ge(sem("rows_copied"), NT * l + t - 1)
                    for k in range(KD):
                        ins = tr(PS[:, 2 * (t % 2) + k // 4, (k % 4) * P:(k % 4 + 1) * P], h[:, k, t * P:(t + 1) * P], ident)
                    ins.then_inc(sem("rows_turned"), 1)
                pe.wait_ge(sem("choices_ready"), l + 1)
                for t in range(NT):
                    for s in range(t + 1):
                        mm(PS[:, 5, t * E:(t + 1) * E], lhsT=(upper if s == t else ones), rhs=both[:, s, :],
                           start=(s == 0), stop=(s == t))
                for s in range(NT):
                    ins = mm(PS[:, 5, NT * E:(NT + 1) * E], lhsT=ones, rhs=both[:, s, :], start=(s == 0), stop=(s == NT - 1))
                ins.then_inc(sem("rank_ready"), 1)
                for n in range(2 * NT):
                    pe.wait_ge(sem("place_ready"), 2 * NT * l + n + 1)
                    mm(PS[:, 6, 0:MAX_BLOCKS], lhsT=ohr, rhs=ohb, start=(n == 0), stop=(n == 2 * NT - 1))\
                        .then_inc(sem("place_used"), 1)
                pe.wait_ge(sem("table_ready"), l + 1)
                pairs = pairs_of(pe, l)

                def turn_x(j, loads):
                    pe.wait_ge(gathered[l][j], loads)
                    for k in range(KD):
                        ins = tr(PS[:, 2 + k // 4, (k % 4) * P:(k % 4 + 1) * P], xg[:, j, k * P:(k + 1) * P], ident)
                    ins.then_inc(sem(f"l{l}_xt_turned"), 1)

                turn_x(0, 16)
                with pe.Fori(0, pairs) as it:
                    for j in range(2):
                        b1 = it * 2 + (j + 1)
                        wg, wu, wd = moe_w[j]
                        pe.wait_ge(sem(f"l{l}_xt_copied"), b1)
                        pe.wait_ge(w_loaded[l][3 * j], (it + 1) * 16)
                        for k in range(KD):
                            ins = mm(PS[:, 0, :], lhsT=xTb[:, k, :], rhs=wg[:, k, :], start=(k == 0), stop=(k == KD - 1))
                        ins.then_inc(sem(f"l{l}_gate_done"), 1)
                        pe.wait_ge(w_loaded[l][3 * j + 1], (it + 1) * 16)
                        for k in range(KD):
                            ins = mm(PS[:, 1, :], lhsT=xTb[:, k, :], rhs=wu[:, k, :], start=(k == 0), stop=(k == KD - 1))
                        ins.then_inc(sem(f"l{l}_up_done"), 1)
                        turn_x(1 - j, (it + 1) * 16 if j == 0 else (it + 2) * 16)
                        pe.wait_ge(sem(f"l{l}_act_done"), b1)
                        for k in range(4):
                            ins = tr(PS[:, 4, k * P:(k + 1) * P], actb[:, k * P:(k + 1) * P], ident)
                        ins.then_inc(sem(f"l{l}_at_turned"), 1)
                        pe.wait_ge(sem(f"l{l}_at_copied"), b1)
                        pe.wait_ge(w_loaded[l][3 * j + 2], (it + 1) * 16)
                        for n in range(2):
                            for k in range(4):
                                ins = mm(PS[:, 5 + n, :], lhsT=aT[:, k, :], rhs=wd[:, k, n * 512:(n + 1) * 512],
                                         start=(k == 0), stop=(k == 3))
                        ins.then_inc(sem(f"l{l}_down_done"), 1)
                for t in range(NT):
                    pe.wait_ge(sem("combined"), NT * l + t + 1)
                    if t >= 2:
                        pe.wait_ge(sem("comb_added"), NT * l + t - 1)
                    for k in range(KD):
                        ins = tr(PS[:, 2 * (t % 2) + k // 4, (k % 4) * P:(k % 4 + 1) * P],
                                 cg[:, (t % 2) * 2, k * P:(k + 1) * P], ident)
                    ins.then_inc(sem("comb_turned"), 1)

            pe.wait_ge(sem("pool_const"), 2)
            pe.wait_ge(sem("params_loaded"), 16 * 9)
            for i in range(12):
                if i == 8:
                    norm(0)
                ada_sums(i)
            projections(0)
            rwkv()
            outproj(0)
            norm(1)
            experts(0)
            norm(2)
            projections(1)
            ssd()
            outproj(1)
            norm(3)
            experts(1)
            norm(4)
            pe.wait_ge(sem("h_ready"), KD * 5)
            for t in range(NT):
                if t >= 2:
                    pe.wait_ge(sem("rows_copied"), NT * DEPTH + t - 1)
                for k in range(KD):
                    ins = tr(PS[:, 2 * (t % 2) + k // 4, (k % 4) * P:(k % 4 + 1) * P], h[:, k, t * P:(t + 1) * P], ident)
                ins.then_inc(sem("rows_turned"), 1)

        @block.vector
        def _(dve):
            steps = {}

            def link(ins):
                signal(ins, "dve_order")

            def signal(ins, name):
                steps[name] = steps.get(name, 0) + 1
                ins.then_inc(sem(name), 1)
                dve.wait_ge(sem(name), steps[name])

            def tt(out, a, b, op):
                return dve.tensor_tensor(out, a, b, op)

            def tsc(out, a, s1, op0, s2=None, op1=None):
                return dve.tensor_scalar(out, a, s1, s2, op0, op1) if op1 else dve.tensor_scalar(out, a, s1, None, op0)

            def stt(out, a, s, b, op0, op1):
                return dve.scalar_tensor_tensor(out=out, in0=a, scalar=s, in1=b, op0=op0, op1=op1)

            def f2(ap):
                return ap.rearrange("p a b -> p (a b)")

            def sigmoid_tail(ap):
                link(tsc(ap, ap, 1.0, ALU.add))
                link(dve.reciprocal(ap, ap))

            signal(dve.memset(y_[:, 0:D], 0.0), "setup_step")
            dve.wait_ge(sem("setup_exp"), 1)
            signal(tt(cond, cexp, PS[:, 5, 0:KD], ALU.mult), "setup_step")

            def ada_chunk(i):
                arrived(dve, ("ada", 0, i))
                if i >= 2:
                    dve.wait_ge(sem("ada_summed"), i - 1)
                w = ring_ap(("ada", 0, i))
                a = acc[:, i % 2, :]
                link(tsc(a, w[:, 0, :], cond[:, 0:1], ALU.mult))
                for k in range(1, KD - 1):
                    link(stt(a, w[:, k, :], cond[:, k:k + 1], a, ALU.mult, ALU.add))
                signal(stt(a, w[:, KD - 1, :], cond[:, KD - 1:KD], a, ALU.mult, ALU.add), "ada_used")

            def parameters():
                dve.wait_ge(sem("x_turned"), KD + 2)
                n1 = sum(n for _, n in ROWS1)
                link(dve.tensor_copy(prm[:, 0, 0:n1], PS[:, 4, 0:n1]))
                link(dve.tensor_copy(prm[:, 1, :], PS[:, 4, P:2 * P]))
                dve.wait_ge(sem("params_loaded"), 16 * 9)
                for par in range(2):
                    pp = slice(64 * par, 64 * par + 64)
                    link(dve.tensor_copy(skipc[pp, :], rs_skip[pp, par:8:2]))
                link(tsc(negw0, prm_col("a_w0", 0, 4), -1.0, ALU.mult))
                link(tsc(nega0, prm_col("a_a0", 0, 4), -1.0, ALU.mult))
                link(tsc(omu, prm_col("a_mu", 0, 14), -1.0, ALU.mult, 1.0, ALU.add))

            def modulation(l):
                if l == 0:
                    dve.wait_ge(sem("ada_summed"), 12)
                else:
                    dve.wait_ge(sem("half_summed"), HALVES)
                link(tt(mod[:, l, :], PS[:, 7, 0:48], prm_col("b_ada", 48 * l, 48), ALU.add))
                for place in range(2):
                    c = 8 + 24 * place
                    ins = stt(amul[:, l, place, :], mod[:, l, c:c + 8], 1.0,
                              prm_col("norm_gain", (2 * l + place) * 8, 8), ALU.add, ALU.mult)
                    if place == 0:
                        link(ins)
                signal(ins, "amul_ready")

            def norm(n):
                dve.wait_ge(sem("rstd_ready"), n + 1)
                for k in range(KD):
                    tt(h[:, k, :], xT[:, k, :], rs, ALU.mult).then_inc(sem("xn_ready"), 1)

            def projections(l):
                for n, (c, c0, w, kind, j) in enumerate(BLOCKS[l]):
                    ps = PS[:, n % 2, :]
                    if kind in WITH_ACT:
                        dve.wait_ge(sem("proj_act"), act_blocks(l, n + 1))
                    dve.wait_ge(sem("proj_done"), l * NB[0] + n + 1)
                    if kind == "shift":
                        o = shifted[j]
                        ins = stt(o[:, 1:T], ps[:, 0:T - 1], prm_col("a_mu", j), o[:, 1:T], ALU.mult, ALU.add)
                    elif kind == "q":
                        ins = tsc(lq[:, j, :], ps, 0.125 if l == 0 else 1.0, ALU.mult)
                    elif kind == "k":
                        ins = dve.tensor_copy(lk[:, j, :], ps)
                    elif kind == "v":
                        ins = dve.tensor_copy(lv[:, j, :], ps)
                    elif kind == "lora":
                        ins = dve.tensor_copy(le[0:16, 0:T], ps[0:16, :])
                    elif kind == "gate":
                        ins = tt(lgate[:, j, :], lgate[:, j, :], ps, ALU.mult)
                    elif kind == "z":
                        ins = tt(zs[:, j, :], zs[:, j, :], ps, ALU.mult)
                    elif kind == "f":
                        link(tsc(lg[:, j, :], lg[:, j, :], omlb[:, j:j + 1], ALU.mult, lb[:, j:j + 1], ALU.add))
                        ins = tsc(lk[:, j, :], lg[:, j, :], -1.0, ALU.mult, 1.0, ALU.add)
                    elif kind == "dt":
                        ins = tt(dt, ps[:, 0:32].rearrange("p (a b) -> p a b", b=8), bc(dtb, NT, 1), ALU.add)
                    elif kind == "conv":
                        cw = [prm_col("d_conv_w", 6 * i + j) for i in range(4)]
                        link(tsc(cva, ps, cw[3], ALU.mult, prm_col("d_conv_b", j), ALU.add))
                        for i in (2, 1):
                            s = 3 - i
                            link(stt(cva[:, s:T], ps[:, 0:T - s], cw[i], cva[:, s:T], ALU.mult, ALU.add))
                        signal(stt(cva[:, 3:T], ps[:, 0:T - 3], cw[0], cva[:, 3:T], ALU.mult, ALU.add), "proj_copied")
                        dve.wait_ge(sem("conv_act"), j + 1)
                        if j < 4:
                            link(tt(xsF[:, j, :], cve, cva, ALU.mult))
                        elif j == 4:
                            link(tt(Bf, cve, cva, ALU.mult))
                        else:
                            for g in range(2):
                                gp = slice(64 * g, 64 * g + 64)
                                link(tt(Cp[gp, g, :], cve[gp, :], cva[gp, :], ALU.mult))
                    if kind != "conv":
                        signal(ins, "proj_copied")
                    if n in AFTER[l]:
                        attention(l, AFTER[l][n])

            def attention(l, step):
                if step == LOGS and l == 0:
                    dve.wait_ge(sem("alpha_ready"), 1)
                    for j in range(2):
                        link(tsc(lg[:, j, :], PS[:, AB + j, :], prm_col("b_alpha_bias", j), ALU.add))
                    signal(stt(le, lgf, -1.0, lgf, ALU.mult, ALU.min), "log_pre")
                elif step == LOGS:
                    signal(dve.memset(f2(lqp), 0.0), "log_pre")
                elif step == SUMS:
                    decay_sums(l)
                elif step < TILE_DECAYS:
                    level(l, step - LEVELS)
                elif step == TILE_DECAYS:
                    tile_decays(l)
                elif step == KEYS_TURNED:
                    dve.wait_ge(sem("kd_turned"), l + 1)
                    signal(dve.tensor_copy(f2(lq)[:, 0:512], PS[:, 6, :]), "kdT_ready")
                elif step < OUTPUTS + NT - 1:
                    state(l, step - OUTPUTS)
                elif step == GATED:
                    gated(l)

            def diff(l, n):
                hh = LV[n]
                lo, hi = halves(lgf, hh)
                ref = lo[:, :, hh - 1:hh]
                m = 1024 // (2 * hh)
                refb = ref.to_broadcast([P, m, hh])
                eq = le[:, 0:512].rearrange("p (n h) -> p n h", h=hh)
                ek = le[:, 512:1024].rearrange("p (n h) -> p n h", h=hh)
                link(tt(eq, hi, refb, ALU.subtract))
                signal(tt(ek, refb, lo, ALU.subtract), "lev_diff")

            def products(l, n):
                hh = LV[n]
                dve.wait_ge(sem("lev_exp"), lev_n * l + n + 1)
                eq = le[:, 0:512].rearrange("p (t n h) -> p t n h", t=2, h=hh)
                ek = le[:, 512:1024].rearrange("p (n h) -> p n h", h=hh)
                for par in range(2):
                    pp = slice(64 * par, 64 * par + 64)
                    for t2 in range(2):
                        q_hi = halves(lq[pp, t2, :], hh)[1]
                        o_hi = halves(lqp[pp, 2 * t2 + par, :], hh)[1]
                        link(tt(o_hi, q_hi, eq[pp, t2], ALU.mult))
                signal(tt(halves(f2(lkp), hh)[0], halves(f2(lk), hh)[0], ek, ALU.mult), "lev_ready")

            def merge(l, n, mask):
                dve.wait_ge(sem("lev_scored"), (lev_n + 1) * l + n + 1)
                ps = PS[:, AB:AB + NT, :].rearrange("p a (b c) -> p (a b) c", c=P)
                if n == 0:
                    signal(tt(lA, ps, bc(ident, 16, 1), ALU.mult), "lev_merged")
                else:
                    signal(dve.copy_predicated(lA, bc(mask, 16, 1).bitcast(I32), ps), "lev_merged")

            def decay_sums(l):
                dve.wait_ge(sem("log_done"), l + 1)
                if l == 0:
                    link(stt(lgf, lgf, 0.0, le, ALU.min, ALU.subtract))
                    link(tsc(lgf, lgf, 1.0 / 16, ALU.mult))
                for j in range(2):
                    link(dve.tensor_tensor_scan(lg[:, j, :], reset128, lg[:, j, :], 0.0, ALU.mult, ALU.add))
                link(dve.memset(f2(lqp), 0.0))

                diff(l, 0)
                for par in range(2):
                    pp = slice(64 * par, 64 * par + 64)
                    link(dve.tensor_copy(lqp[pp, par::2, :], lq[pp]))
                signal(dve.tensor_copy(lkp, lk), "lev_ready")

            def level(l, n):
                merge(l, n, lev_up[LV[n - 1]] if n else None)
                if n < lev_n:
                    products(l, n)
                if n + 1 < lev_n:
                    diff(l, n + 1)

            def tile_decays(l):
                dve.wait_ge(sem("tile_decay"), 2 * l + 1)
                le2 = le.rearrange("p (a b) -> p a b", b=T)
                for par in range(2):
                    pp = slice(64 * par, 64 * par + 64)
                    link(tt(lqp[pp, par::2, :], lq[pp], le2[pp], ALU.mult))
                link(dve.tensor_copy(ebl, le.rearrange("p (a t s) -> p a t s", a=2, s=P)[:, :, :, P - 1]))
                b3 = lgf.rearrange("p (n s) -> p n s", s=P)
                signal(tt(le.rearrange("p (n s) -> p n s", s=P), b3[:, :, P - 1:P].to_broadcast([P, 8, P]), b3,
                          ALU.subtract), "end_keys")
                dve.wait_ge(sem("tile_decay"), 2 * l + 2)
                signal(tt(f2(lkp), f2(lk), le, ALU.mult), "end_keys")

            def state(l, t):
                dve.wait_ge(sem("ls_ps"), 3 * l + t + 1)
                if t == 0:
                    link(dve.tensor_copy(f2(lq)[:, 512:768], PS[:, 6, 256:512]))
                for j in range(2):
                    ps = PS[:, 6, j * P:(j + 1) * P]
                    if t == 0:
                        ins = dve.tensor_copy(lS[:, j, :], ps)
                    else:
                        ins = stt(lS[:, j, :], lS[:, j, :], ebl[:, j, t:t + 1], ps, ALU.mult, ALU.add)
                    if j == 0:
                        link(ins)
                signal(ins, "ls_ready")

            def gated(l):
                if l == 0:
                    dve.wait_ge(sem("half_used"), HALVES)
                gain = prm_col(("b_norm_gain", "c_norm_gain")[l])
                for hd in range(4):
                    dve.wait_ge(sem("o_rstd"), 4 * l + hd + 1)
                    link(stt(lsq[:, hd, :], PS[:, AB + hd, :], gain, lrms[:, hd, :], ALU.mult, ALU.mult))
                    ins = tt(y[:, 4 * (1 - l) + hd, :], lsq[:, hd, :], lgate[:, hd, :], ALU.mult)
                    if hd < 3:
                        link(ins)
                signal(ins, "yhalf")

            def col(name):
                return prm_col(name, 0, 4).unsqueeze(2).to_broadcast([P, 4, P])

            def front(t, piece):
                ts = slice(t * P, (t + 1) * P)
                r_t, k_t, v_t = rr[:, :, ts], kk_[:, :, ts], vv[:, :, ts]
                sg, aa, cs, eb, kk, kt, ka, be, b1, alp, rho = (
                    buffer[t % 2] for buffer in (SG, AA, CS, EB, KK, KT, KA, BE, B1, ALP, RHO))
                if piece == 0:
                    link(tt(kk, k_t, col("a_k_k"), ALU.mult))
                    signal(tt(b1, kk, kk, ALU.mult), "kk_sq")
                elif piece == 1:
                    dve.wait_ge(sem("lora_exp"), t + 1)
                    link(dve.tensor_tensor_scan(f2(cs), reset64, f2(sg), 0.0, ALU.mult, ALU.add))
                    signal(tt(sg, cs, sg, ALU.subtract), "cs_ready")
                    link(stt(kt, aa, -1.0, col("a_k_a"), ALU.add, ALU.mult))
                    link(stt(kt, kt, 1.0, k_t, ALU.add, ALU.mult))
                elif piece == 2:
                    dve.wait_ge(sem("decays_ready"), t + 1)
                    link(tt(ka, kt, cs, ALU.mult))
                    link(tt(be, aa, cs, ALU.mult))
                    for par in range(2):
                        pp = slice(64 * par, 64 * par + 64)
                        link(tt(rho[pp, par::2, :], r_t[pp], eb[pp], ALU.mult))
                elif piece == 3:
                    dve.wait_ge(sem("kk_rn"), t + 1)
                    link(tt(kk, kk, b1, ALU.mult))
                    link(stt(sg, kk, -1.0, sg, ALU.mult, ALU.mult))
                    for par in range(2):
                        pp = slice(64 * par, 64 * par + 64)
                        link(dve.tensor_copy(alp[pp, par::2, :], sg[pp]))
                    link(tt(be, be, kk, ALU.mult))
                elif piece == 4:
                    link(tt(b1, r_t, kt, ALU.mult))
                    signal(tt(b1, b1, col("a_r_k"), ALU.mult), "feat_ready")
                elif piece == 5:
                    dve.wait_ge(sem("bonus_sum"), t + 1)
                    signal(tt(b1, PS[:, 7, :].rearrange("p (a b) -> p a b", b=P), v_t, ALU.mult), "bonus_used")

            def score_copy(t, n):
                b, dst, mask = ((5, XT, strict_up), (0, X, strict_lo), (2, LKT, strict_up), (5, PKT, incl_up),
                                (0, PBT, incl_up))[n]
                dve.wait_ge(sem("score_ready"), 5 * t + n + 1)
                ps = PS[:, b:b + 2, :].rearrange("p a (b c) -> p (a b) c", c=P)
                signal(tt(dst, ps, bc(mask, 8, 1), ALU.mult), "score_copied")

            def inversion(t):
                for dst, src, mask in ((Tm, X, lev_lo[1]), (TT, XT, lev_up[1])):
                    link(dve.tensor_copy(dst, bc(ident, 8, 1)))
                    link(dve.copy_predicated(dst, bc(mask, 8, 1).bitcast(I32), src))
                signal(dve.tensor_copy(Tm[:, 0:1, 0:1], Tm[:, 0:1, 0:1]), "inv_ready")
                for n in range(5):
                    for o in range(2):
                        if n == 4 and o == 0:
                            continue
                        dve.wait_ge(sem("p_ready"), 9 * t + (2 * n + 2 if n < 4 else 9))
                        b, dst, mask = ((4, Tm, lev_lo), (0, TT, lev_up))[o]
                        ps = PS[:, b:b + 2, :].rearrange("p a (b c) -> p (a b) c", c=P)
                        signal(dve.copy_predicated(dst, bc(mask[LV[n + 1]], 8, 1).bitcast(I32), ps), "inv_ready")
                    if t + 1 < NT:
                        front(t + 1, n)

            def states(t):
                for c in range(2):
                    po = 64 * c
                    dve.wait_ge(sem("un_ready"), 2 * t + c + 1)
                    dve.wait_ge(sem("rw_copied"), 2 * t + 2)
                    signal(tt(Un[po:po + 64, :], PS[po:po + 64, 3, :], U0[po:po + 64, :], ALU.add), "un_done")
                    dve.wait_ge(sem("st_ps"), 2 * t + c + 1)
                    for par in range(2):
                        pp = slice(64 * par, 64 * par + 64)
                        s_par = ST[pp, par::2, :]
                        link(tt(s_par, PS[pp, 4, 0:256].rearrange("p (a b) -> p a b", b=64), s_par, ALU.add))
                        ins = tt(s_par, s_par, EB[t % 2][pp, :, po + 63:po + 64].to_broadcast([64, 4, 64]), ALU.mult)
                        if par == 0:
                            link(ins)
                    signal(ins, "st_done")

            def head_norm(t, n):
                ts = slice(t * P, (t + 1) * P)
                sg, cs, eb, b1 = (buffer[t % 2] for buffer in (SG, CS, EB, B1))
                if n == 0:
                    dve.wait_ge(sem("ys_copied"), t + 1)
                    signal(tt(f2(cs), PS[:, 5, :], f2(sg), ALU.add), "gn_in")
                elif n == 1:
                    dve.wait_ge(sem("gn_sum"), 2 * t + 1)
                    link(stt(f2(cs), PS[:, 7, :], -1.0 / 64, f2(cs), ALU.mult, ALU.add))
                    signal(tt(eb, cs, cs, ALU.mult), "gn_in")
                else:
                    dve.wait_ge(sem("gn_rstd"), t + 1)
                    link(tt(cs, cs, eb, ALU.mult))
                    link(tt(cs, cs, col("a_ln_gain"), ALU.mult))
                    link(tt(cs, cs, col("a_ln_bias"), ALU.add))
                    link(tt(cs, cs, b1, ALU.add))
                    signal(tt(y[:, 0:4, ts], y[:, 0:4, ts], cs, ALU.mult), "rwkv_done")

            def rwkv():
                for ap in (*ALP, *RHO):
                    link(dve.memset(f2(ap), 0.0))
                signal(dve.memset(f2(ST), 0.0), "st_done")
                for piece in range(6):
                    front(0, piece)
                for n in range(5):
                    score_copy(0, n)
                for t in range(NT):
                    inversion(t)
                    states(t)
                    if t + 1 < NT:
                        front(t + 1, 5)
                    head_norm(t, 0)
                    head_norm(t, 1)
                    if t + 1 < NT:
                        score_copy(t + 1, 0)
                        score_copy(t + 1, 1)
                    head_norm(t, 2)
                    if t + 1 < NT:
                        for n in range(2, 5):
                            score_copy(t + 1, n)

            def lower_bounds():
                c0, c1 = prm_col("c_lb", 0, 2), prm_col("c_lb", 2, 2)
                link(tt(lbt[:, 0:2], c0, c1, ALU.max))
                link(tt(lbt[:, 4:6], c0, lbt[:, 0:2], ALU.subtract))
                signal(tt(lbt[:, 6:8], c1, lbt[:, 0:2], ALU.subtract), "setup_step")

            def lower_bounds_end():
                e0, e1 = lbt[:, 4:6], lbt[:, 6:8]
                dve.wait_ge(sem("setup_exp"), 2)
                link(tt(lbt[:, 0:2], e0, e1, ALU.add))
                link(dve.reciprocal(lbt[:, 0:2], lbt[:, 0:2]))
                link(tt(e0, e0, lbt[:, 0:2], ALU.mult))
                link(tt(e1, e1, lbt[:, 0:2], ALU.mult))
                link(tt(lbt[:, 0:2], e0, e1, ALU.add))
                link(tt(lb, lbt[:, 0:2], e0, ALU.subtract))
                link(tsc(omlb, lb, -1.0, ALU.mult, 1.0, ALU.add))

            def ssd():
                signal(stt(f2(dz), f2(dt), -1.0, f2(dt), ALU.mult, ALU.min), "setup_step")
                dve.wait_ge(sem("setup_exp"), 4)
                link(tsc(f2(dz2), f2(dz), 2.0, ALU.add))
                link(dve.reciprocal(f2(dz2), f2(dz2)))
                link(tt(f2(dz), f2(dz), f2(dz2), ALU.mult))
                link(tt(f2(dz2), f2(dz), f2(dz), ALU.mult))
                terms = [2.0 / (2 * i + 1) for i in range(9)]
                link(tsc(f2(dpl), f2(dz2), terms[8], ALU.mult, terms[7], ALU.add))
                for i in range(6, -1, -1):
                    link(tt(f2(dpl), f2(dpl), f2(dz2), ALU.mult))
                    link(tsc(f2(dpl), f2(dpl), terms[i], ALU.add))
                link(tt(f2(dpl), f2(dpl), f2(dz), ALU.mult))
                link(stt(f2(dt), f2(dt), 0.0, f2(dpl), ALU.max, ALU.add))
                signal(stt(da, dt, -1.0, bc(alog, NT, 1), ALU.mult, ALU.mult), "ssd_inputs")
                dve.wait_ge(sem("xs_turned"), 1)
                link(dve.tensor_copy(xsT, PS[:, 0:4, :]))
                signal(dve.tensor_copy(f2(Bt), PS[:, 4, :]), "ssd_inputs")
                dve.wait_ge(sem("xs_turned"), 2)
                link(dve.tensor_copy(f2(cumc), PS[:, 5, 0:32]))
                link(dve.memset(f2(Csp), 0.0))
                for t in range(NT):
                    ts = slice(t * P, (t + 1) * P)
                    dve.wait_ge(sem("cb_ready"), t + 1)
                    for hd in range(8):
                        link(tsc(Es[:, hd, :], PS[:, 2 + hd // 4, (hd % 4) * P:(hd % 4 + 1) * P],
                                 cumc[:, t, hd:hd + 1], ALU.subtract, 0.0, ALU.min))
                    last = PS[:, 2:4, :].rearrange("p a (b c) -> p (a b) c", c=P)[:, :, P - 1]
                    signal(tt(dte, last, cumc[:, t, :], ALU.subtract), "seg_diff")
                    link(tt(CBm, PS[:, 4, 0:256].rearrange("p (a b) -> p a b", b=P), bc(upper, 2, 1), ALU.mult))
                    xv = xsT[:, t, :].rearrange("p (a b) -> p a b", b=64)
                    xdv = xdt.rearrange("p (a b) -> p a b", b=64)
                    link(tt(xdv, xv, dt[:, t, :].unsqueeze(2).to_broadcast([P, 8, 64]), ALU.mult))
                    dve.wait_ge(sem("seg_exp"), 2 * t + 1)
                    link(tt(MT.rearrange("p (g q) c -> p g q c", g=2), Es.rearrange("p (g q) c -> p g q c", g=2),
                            bc(CBm, 4, 2), ALU.mult))
                    dve.wait_ge(sem("seg_exp"), 2 * t + 2)
                    link(tt(xdd.rearrange("p (a b) -> p a b", b=64), xdv,
                            dte.unsqueeze(2).to_broadcast([P, 8, 64]), ALU.mult))
                    for g in range(2):
                        gp = slice(64 * g, 64 * g + 64)
                        ins = tt(Csp[gp, 4 * g:4 * g + 4, :], ec[gp, 4 * g:4 * g + 4, :], bc(Cp[gp, g, ts], 4, 1), ALU.mult)
                        if g == 0:
                            link(ins)
                    signal(ins, "ssd_in")
                    if t < NT - 1:
                        dve.wait_ge(sem("ssd_st_ps"), t + 1)
                        ps = PS[:, 1, 0:256].rearrange("p (a b) -> p a b", b=64)
                        if t == 0:
                            link(dve.tensor_copy(Sst, ps))
                        else:
                            for g in range(2):
                                gp = slice(64 * g, 64 * g + 64)
                                link(tt(Stm[gp], Sst[gp], ec[gp, 4 * g:4 * g + 4, P - 1:P].to_broadcast([64, 4, 64]),
                                        ALU.mult))
                            link(tt(Sst, Stm, ps, ALU.add))
                    dve.wait_ge(sem("ssd_y_ready"), t + 1)
                    for j in range(4):
                        ins = stt(yF[:, j, ts], xsF[:, j, ts], skipc[:, j:j + 1], PS[:, 0, j * P:(j + 1) * P],
                                  ALU.mult, ALU.add)
                        if j < 3:
                            link(ins)
                    signal(ins, "ssd_y_copied")
                signal(tt(yF, yF, zs, ALU.mult), "yz_ready")
                for j in range(4):
                    if j % 2 == 0:
                        dve.wait_ge(sem("o_rstd"), 8 + j // 2 + 1)
                    rstd = f2(Es if j < 2 else MT)[:, 0:512]
                    link(stt(y[:, 4 + j, :], yF[:, j, :], prm_col("d_norm_gain", j), rstd, ALU.mult, ALU.mult))

            def outproj(l):
                signal(dve.tensor_copy(lsum[:, 0:1], lsum[:, 1:2]), "mix_done")
                for n in range(KD):
                    dve.wait_ge(sem("outproj_done"), 8 * l + n + 1)
                    signal(stt(xT[:, n, :], PS[:, n % 4, :], mod[:, l, 16 + n:17 + n], xT[:, n, :], ALU.mult, ALU.add),
                           "x_ready")

            def choose(l):
                dve.wait_ge(sem("logits_exp"), l + 1)
                sigmoid_tail(sc)
                link(tt(sel, sc, bc(rbias, NT, 1), ALU.add))
                v = sel.rearrange("p t (n two) -> p t n two", two=2)
                link(tt(r1, v[:, :, :, 0], v[:, :, :, 1], ALU.max))
                link(tt(r2, v[:, :, :, 0], v[:, :, :, 1], ALU.min))
                mx = r1.rearrange("p t (g two) -> p t g two", two=2)
                mn = r2.rearrange("p t (g two) -> p t g two", two=2)
                link(tt(gs, mx[:, :, :, 0], mx[:, :, :, 1], ALU.min))
                link(tt(gm, mn[:, :, :, 0], mn[:, :, :, 1], ALU.max))
                link(tt(gm, gm, gs, ALU.max))
                link(tt(gs, mx[:, :, :, 0], mx[:, :, :, 1], ALU.max))
                link(tt(gs, gs, gm, ALU.add))

                def first_max(vals, n, onehot):
                    link(dve.tensor_reduce(m1, vals, AX_X, ALU.max))
                    m1b = m1.unsqueeze(2).to_broadcast([P, NT, n])
                    t_ = idc[:, :, 0:n]
                    link(tt(t_, vals, m1b, ALU.is_lt))
                    link(stt(t_, t_, BIG, bc(iota16[:, 0:n], NT, 1), ALU.mult, ALU.add))
                    link(dve.tensor_reduce(m1, t_, AX_X, ALU.min))
                    link(tt(onehot, bc(iota16[:, 0:n], NT, 1), m1b, ALU.is_equal))

                first_max(gs, GRP, gm)
                link(tsc(gs, gm, -1.0, ALU.add, BIG, ALU.mult))
                s4 = sel.rearrange("p t (g i) -> p t g i", i=4)
                link(tt(s4, s4, gs.unsqueeze(3).to_broadcast([P, NT, GRP, 4]), ALU.add))
                ohv = [oh[:, k, :].rearrange("p (t e) -> p t e", e=E) for k in range(2)]
                first_max(sel, E, ohv[0])
                link(stt(sel, ohv[0], -4 * BIG, sel, ALU.mult, ALU.add))
                first_max(sel, E, ohv[1])
                signal(tt(both, ohv[0], ohv[1], ALU.add), "choices_ready")
                for k in range(2):
                    link(tt(idc, sc, ohv[k], ALU.mult))
                    link(dve.tensor_reduce(gk[:, k, :], idc, AX_X, ALU.add))
                link(tt(gsum, gk[:, 0, :], gk[:, 1, :], ALU.add))
                link(dve.reciprocal(gsum, gsum))
                link(tt(gk, gk, bc(gsum, 2, 1), ALU.mult))

                dve.wait_ge(sem("rank_ready"), l + 1)
                link(tt(rank, PS[:, 5, 0:NT * E].rearrange("p (a b) -> p a b", b=E), both, ALU.subtract))
                link(dve.tensor_copy(cnt, PS[:, 5, NT * E:(NT + 1) * E]))

                def thresholds(out, src, lo, op, tmp):
                    link(tsc(out, src, lo, op))
                    for m in (2, 3):
                        link(tsc(tmp, src, lo + P * (m - 1), op))
                        link(tt(out, out, tmp, ALU.add))

                thresholds(nov, cnt, float(P), ALU.is_gt, over)
                link(dve.tensor_tensor_scan(ove, ones[:, 0:E], nov, 0.0, ALU.mult, ALU.add))
                link(tt(over, ove, nov, ALU.subtract))
                link(tt(over, over, iota16, ALU.subtract))
                thresholds(qq, rank, float(P), ALU.is_ge, q0)
                link(tsc(q0, qq, 0.0, ALU.is_gt))
                link(stt(blk, qq, 15.0, bc(over, NT, 1), ALU.add, ALU.add))
                link(tt(blk, blk, q0, ALU.mult))
                link(tt(blk, blk, bc(iota16, NT, 1), ALU.add))
                link(stt(rin, qq, -float(P), rank, ALU.mult, ALU.add))
                for k in range(2):
                    for src, dst in ((blk, selb), (rin, selr)):
                        link(tt(idc, src, ohv[k], ALU.mult))
                        link(dve.tensor_reduce(dst[:, k, :], idc, AX_X, ALU.add))
                link(stt(destf, selb, float(P), selr, ALU.mult, ALU.add))
                link(dve.tensor_copy(idx_dest[:, :], f2(destf)))

                link(dve.tensor_copy(tabf[:, 0:E], iota16))
                w3 = rank.rearrange("p a b -> p (a b)")
                for b in range(8):
                    link(tsc(idc[:, 0, :], ove, float(b), ALU.is_le))
                    link(dve.tensor_reduce(tabf[:, E + b:E + b + 1], idc[:, 0, :], AX_X, ALU.add))
                link(tsc(tabf[:, E:E + 8], tabf[:, E:E + 8], float(E - 1), ALU.min))
                link(tsc(tabf[:, 24:25], ove[:, E - 1:E], 0.0, ALU.is_gt, 8.0, ALU.add))
                for m in (2.0, 4.0, 6.0):
                    link(tsc(tabf[:, 25:26], ove[:, E - 1:E], m, ALU.is_gt))
                    link(tt(tabf[:, 24:25], tabf[:, 24:25], tabf[:, 25:26], ALU.add))
                link(dve.tensor_copy(table[:, 0:24], tabf[:, 0:24]))
                link(dve.tensor_copy(table[:, 30 + l:31 + l], tabf[:, 24:25]))
                link(tsc(tabf[:, 24:25], tabf[:, 24:25], -1.0, ALU.add))
                link(dve.tensor_copy(table[:, 26 + l:27 + l], tabf[:, 24:25]))

                for n in range(2 * NT):
                    k, t = n // NT, n % NT
                    if n or l:
                        dve.wait_ge(sem("place_used"), 2 * NT * l + n)
                    link(tsc(ohb, iota24, selb[:, k, t:t + 1], ALU.is_equal, tokid[:, t:t + 1], ALU.mult))
                    signal(tsc(ohr, iota128, selr[:, k, t:t + 1], ALU.is_equal), "place_ready")
                dve.wait_ge(sem("place_used"), 2 * NT * (l + 1))
                signal(dve.tensor_copy(idx_tok[:, 0:MAX_BLOCKS], PS[:, 6, 0:MAX_BLOCKS]), "table_ready")

            def experts(l):
                choose(l)
                pairs = pairs_of(dve, l)
                so = sem(f"l{l}_silu_order")
                with dve.Fori(0, pairs) as it:
                    for j in range(2):
                        b1 = it * 2 + (j + 1)
                        dve.wait_ge(sem(f"l{l}_gate_exp"), b1)
                        tsc(sgt, sgt, 1.0, ALU.add).then_inc(so, 1)
                        dve.wait_ge(so, it * 6 + (3 * j + 1))
                        dve.reciprocal(sgt, sgt).then_inc(so, 1)
                        dve.wait_ge(so, it * 6 + (3 * j + 2))
                        tt(sgt, sgt, PS[:, 0, :], ALU.mult).then_inc(so, 1)
                        dve.wait_ge(so, it * 6 + (3 * j + 3))
                        dve.wait_ge(sem(f"l{l}_up_done"), b1)
                        tt(actb, sgt, PS[:, 1, :], ALU.mult).then_inc(sem(f"l{l}_act_done"), 1)
                        dve.wait_ge(sem(f"l{l}_at_turned"), b1)
                        dve.tensor_copy(aT, PS[:, 4, :].rearrange("p (a b) -> p a b", b=P))\
                           .then_inc(sem(f"l{l}_at_copied"), 1)
                for t in range(NT):
                    dve.wait_ge(sem(f"expert_rows{t % 2}"), 32 * (2 * l + t // 2 + 1))
                    c0, c1 = cg[:, (t % 2) * 2, :], cg[:, (t % 2) * 2 + 1, :]
                    link(tsc(c0, c0, gk[:, 0, t:t + 1], ALU.mult))
                    signal(stt(c0, c1, gk[:, 1, t:t + 1], c0, ALU.mult, ALU.add), "combined")
                    dve.wait_ge(sem("comb_turned"), NT * l + t + 1)
                    for k in range(KD):
                        xs = xT[:, k, t * P:(t + 1) * P]
                        ps = PS[:, 2 * (t % 2) + k // 4, (k % 4) * P:(k % 4 + 1) * P]
                        ins = stt(xs, ps, mod[:, l, 40 + k:41 + k], xs, ALU.mult, ALU.add)
                        if k < KD - 1:
                            link(ins)
                    signal(ins, "comb_added")
                signal(dve.tensor_copy(lsum[:, 0:1], lsum[:, 1:2]), "x_ready")

            link(dve.memset(lsum, 0.0))
            for i in range(12):
                ada_chunk(i)
                if i == 6:
                    parameters()
                    lower_bounds()
                if i == 8:
                    lower_bounds_end()
                if i == 9:
                    norm(0)
            dve.wait_ge(sem("pool_const"), 2)
            modulation(0)
            projections(0)
            modulation(1)
            rwkv()
            outproj(0)
            norm(1)
            experts(0)
            link(dve.memset(f2(Cp), 0.0))
            norm(2)
            projections(1)
            ssd()
            outproj(1)
            norm(3)
            experts(1)
            norm(4)


_INS = ['x', 'c', 'norm_gain', 'w_ada', 'b_ada', 'w_in_even', 'w_in_odd', 'w_out', 'a_mu', 'a_w0', 'a_w_up', 'a_a0',
        'a_a_up', 'a_g_up', 'a_k_k', 'a_k_a', 'a_r_k', 'a_ln_gain', 'a_ln_bias', 'b_alpha_up', 'b_alpha_bias',
        'b_norm_gain', 'c_lb', 'c_norm_gain', 'd_conv_w', 'd_conv_b', 'd_dt_bias', 'd_a_log', 'd_skip', 'd_norm_gain',
        'w_router', 'router_bias', 'w_gate', 'w_up', 'w_down', 'final_gain']


def kernel(**inputs):
    import numpy as np
    import concourse.bacc as bacc
    from concourse.bass_utils import run_bass_kernel_spmd

    nc = bacc.Bacc("TRN2", target_bir_lowering=False, num_devices=1)
    arrays, aps = {}, {}
    for name in _INS:
        a = np.ascontiguousarray(inputs[name])
        arrays[f"in_{name}_dram"] = a
        aps[name] = nc.dram_tensor(f"in_{name}_dram", a.shape, mybir.dt.from_np(a.dtype), kind="ExternalInput").ap()
    out = nc.dram_tensor("out_0_dram", (1, T, D), F32, kind="ExternalOutput").ap()
    trunk(nc, aps, out)
    r = run_bass_kernel_spmd(nc, [arrays], core_ids=[0])
    return r.results[0]["out_0_dram"]
```

```python
from contextlib import ExitStack

import concourse.bass as bass
from concourse import mybir

F32 = mybir.dt.float32
I32 = mybir.dt.int32
ALU = mybir.AluOpType
ACT = mybir.ActivationFunctionType
AX_X = mybir.AxisListType.X

P = 128
D = 1024
T = 512
KD = D // P
NT = T // P
DEPTH = 2
EPS = 1e-6
HALF = D // 2
RW = 0.6065306597126334
RW_CHUNK = 64
GN_EPS = 64e-5
E = 16
GRP = 4
FE = 512
MAX_BLOCKS = 24
BIG = 1e30
RING = 3
SLOT = 8 * 512

ROWS1 = [("a_mu", 14), ("a_w0", 4), ("a_a0", 4), ("a_k_k", 4), ("a_k_a", 4), ("a_r_k", 4), ("a_ln_gain", 4),
         ("a_ln_bias", 4), ("b_alpha_bias", 2), ("b_norm_gain", 1), ("c_lb", 4), ("c_norm_gain", 1),
         ("d_conv_w", 24), ("d_conv_b", 6), ("d_norm_gain", 4), ("final_gain", 8)]
ROWS2 = [("b_ada", 96), ("norm_gain", 32)]


def columns():
    at = {}
    for tile, rows in enumerate((ROWS1, ROWS2)):
        c = 0
        for name, n in rows:
            at[name] = (tile, c)
            c += n
    return at


def chunk_plan():
    plan = [("ada", 0, i) for i in range(12)] + [("in", 0, i) for i in range(7)]
    plan += [None] + [("out", 0, i) for i in range(2)]
    plan += [("in", 1, i) for i in range(6)] + [("out", 1, i) for i in range(2)]
    return plan


IN_PIECES = [
    [[(1536, 512)], [(2048, 256), (2816, 16)], [(2304, 512)], [(2832, 512)], [(0, 512)], [(512, 512)], [(1024, 512)]],
    [[(0, 512)], [(512, 512)], [(1024, 512)], [(1536, 512)], [(2560, 264)], [(2048, 512)]],
]


def zone(tensor, start, end):
    place = [start]

    def take(*shape):
        n = 1
        for size in shape:
            n *= size
        ap = tensor[:, place[0]:place[0] + n]
        place[0] += n
        assert place[0] <= end
        if len(shape) == 2:
            ap = ap.rearrange("p (a b) -> p a b", b=shape[1])
        if len(shape) == 3:
            ap = ap.rearrange("p (a b c) -> p a b c", b=shape[1], c=shape[2])
        return ap

    return take, place


def bc(ap, n, at):
    u = ap.unsqueeze(at)
    shape = list(u.shape)
    shape[at] = n
    return u.to_broadcast(shape)


def trunk(nc, A, out):
    h_dram = nc.dram_tensor("h_rows", [T, D], F32, kind="Internal").ap()
    y_dram = nc.dram_tensor("expert_rows", [MAX_BLOCKS * P, D], F32, kind="Internal").ap()
    COL = columns()
    PLAN = chunk_plan()

    with ExitStack() as ctx:
        def sb(name, cols, dt=F32):
            return ctx.enter_context(nc.sbuf_tensor(name, [P, cols], dt))

        made = {}

        def sem(name):
            if name not in made:
                made[name] = ctx.enter_context(nc.semaphore(name))
            return made[name]

        PS = ctx.enter_context(nc.psum_tensor("banks", [P, 8, 512], F32))

        ring = sb("ring", RING * SLOT)
        xT_ = sb("x_features", KD * T)
        xT = xT_[:, :].rearrange("p (k t) -> p k t", t=T)
        h_ = sb("h_features", KD * T)
        h = h_[:, :].rearrange("p (k t) -> p k t", t=T)
        y_ = sb("y_features", KD * T)
        y = y_[:, :].rearrange("p (k t) -> p k t", t=T)
        work = sb("work", 20992)
        KEEP = 7168

        cst, _ = zone(sb("constants", 128 * 19 + 1024), 0, 128 * 19 + 1024)
        ident = cst(P)
        ones = cst(P)
        upper = cst(P)
        headones = cst(P)
        strict_up = cst(P)
        strict_lo = cst(P)
        incl_up = cst(P)
        LV = [1, 2, 4, 8, 16, 32, 64]
        lev_up = {hh: cst(P) for hh in LV}
        lev_lo = {1: cst(P)}
        reset64 = cst(T)
        reset128 = cst(T)

        small, _ = zone(sb("small", 3608), 0, 3608)
        prm = small(2, P)
        mod = small(2, 48)
        amul = small(2, 2, 8)
        cond = small(8)

        wup = small(512)
        gup = small(512)
        alup = small(256)
        wr = small(8, E)
        rs = work[:, 20480:20992]
        rs_skip = work[:, 8192:8200]
        cexp = work[:, 8200:8208]
        acc = small(2, 512)
        negw0 = small(4)
        nega0 = small(4)
        nabias = small(2)
        omu = small(14)
        lb = small(2)
        omlb = small(2)
        lbt = small(12)
        dtb = small(8)
        alog = small(8)
        skipc = small(4)
        rbias = small(E)
        iota16 = small(E)
        iota24 = small(MAX_BLOCKS)
        iota128 = small(P)
        tokid = small(NT)
        pidx = small(1)
        epsc = small(4)
        ebl = small(2, NT)
        lsum = small(8)
        idx_tok = sb("idx_tok", MAX_BLOCKS + 2, I32)
        scratch_i = sb("scratch_ints", P, I32)
        idx_cur = sb("idx_cur", 2, I32)
        idx_dest = sb("idx_dest", 2 * NT, I32)
        table = sb("block_experts", 32, I32)

        def prm_col(name, i=0, n=1):
            tile, c = COL[name]
            return prm[:, tile, c + i:c + i + n]

        def slot(n, cols):
            s = n % RING
            return ring[:, s * SLOT:s * SLOT + 8 * cols].rearrange("p (k n) -> p k n", n=cols)

        def slot_w(kind, l, i):
            if kind == "in":
                return sum(w for _, w in IN_PIECES[l][i])
            return 512

        where = {c: n for n, c in enumerate(PLAN) if c is not None}

        slot_loaded = [sem(f"slot{i}_loaded") for i in range(RING)]

        def arrived(eng, key):
            n = where[key]
            eng.wait_ge(slot_loaded[n % RING], 16 * sum(key is not None for key in PLAN[n % RING:n + 1:RING]))

        def ring_ap(key):
            n = where[key]
            return slot(n, slot_w(*key))

        def w_src(key):
            kind, l, i = key
            if kind == "ada":
                return A["w_ada"][l].rearrange("(k p) n -> p k n", p=P)[:, :, i * 512:(i + 1) * 512]
            if kind == "out":
                return A["w_out"][l].rearrange("(k p) n -> p k n", p=P)[:, :, i * 512:(i + 1) * 512]
            w = (A["w_in_even"], A["w_in_odd"])[l][0].rearrange("(k p) n -> p k n", p=P)
            c, n = IN_PIECES[l][i][0]
            return w[:, :, c:c + n]

        ring2 = [work[:, 4096 * i:4096 * (i + 1)] for i in range(3)]
        mo, mo_at = zone(work, 3 * 4096, 20992)
        xg = mo(2, D)
        xTb = mo(8, P)
        sgt = mo(FE)
        actb = mo(FE)
        aT = mo(4, P)
        yb = mo(D)
        ro, _ = zone(work, mo_at[0], 20480)
        moe_w = []
        for j in range(2):
            base = [ring[:, s * SLOT:s * SLOT + 4096] for s in range(3)] if j == 0 else ring2
            moe_w.append((base[0].rearrange("p (k n) -> p k n", n=512), base[1].rearrange("p (k n) -> p k n", n=512),
                          base[2].rearrange("p (k n) -> p k n", n=1024)))

        cg = zone(work, 0, 3 * 4096)[0](2 * NT, D)

        sc = ro(NT, E)
        sel = ro(NT, E)
        r1 = ro(NT, 8)
        r2 = ro(NT, 8)
        gs = ro(NT, GRP)
        gm = ro(NT, GRP)
        m1 = ro(NT)
        idc = ro(NT, E)
        oh = ro(2, NT * E)
        both = ro(NT, E)
        gk = ro(2, NT)
        gsum = ro(NT)
        rank = ro(NT, E)
        cnt = ro(E)
        nov = ro(E)
        ove = ro(E)
        over = ro(E)
        qq = ro(NT, E)
        q0 = ro(NT, E)
        blk = ro(NT, E)
        rin = ro(NT, E)
        selb = ro(2, NT)
        selr = ro(2, NT)
        destf = ro(2, NT)
        ohb = ro(2 * NT, MAX_BLOCKS)
        ohr = ro(2 * NT, P)
        cmp3 = ro(NT * E, 3)
        picked = ro(2, NT * E)
        mult3 = ro(3)
        tabf = ro(32)

        la, la_at = zone(work, KEEP, 20992)
        lq = la(2, T)
        lk = la(2, T)
        lg = la(2, T)
        lv = la(NT, 512)
        lgate = la(4, T)
        lqp = la(4, T)
        lkp = la(2, T)
        lA = la(16, P)
        le = la(1024)
        lS = la(2, P)
        lsq = lqp
        lrms = work[:, KEEP:KEEP + 4 * T].rearrange("p (a b) -> p a b", b=T)

        kz, _ = zone(work, 0, KEEP)
        rr = kz(4, T)
        kk_ = kz(4, T)
        vv = kz(4, T)
        wad = kz(T)
        gdp = kz(T)
        rz, rz_at = zone(work, KEEP, 20992)
        LKT = rz(8, P)
        PKT = rz(8, P)
        PBT = rz(8, P)
        Gm = rz(8, P)
        G2 = rz(8, P)
        uz, _ = zone(work, rz_at[0] - 2048, rz_at[0])
        R0 = uz(512)
        Un = uz(512)
        U0 = uz(512)
        WnT = uz(4, P)
        ez, _ = zone(ring, 0, 2 * SLOT)
        SGA, CS, EB, KK, KT, KA, BE, B1, ALP, RHO = [[take(m, P) for take in (ez, rz)]
                                                     for m in (8, 4, 4, 4, 4, 4, 4, 4, 8, 8)]
        SG = [ap[:, 0:4, :] for ap in SGA]
        AA = [ap[:, 4:8, :] for ap in SGA]
        Vt = rz(512)
        kaT = rz(512)
        beT = rz(512)
        alT = rz(512)
        X = h_[:, 1024:2048].rearrange("p (a b) -> p a b", b=P)
        Tm = h_[:, 2048:3072].rearrange("p (a b) -> p a b", b=P)
        TT = h_[:, 3072:4096].rearrange("p (a b) -> p a b", b=P)
        ST = small(8, 64)

        sz, _ = zone(work, 0, KEEP)
        zs = sz(4, T)
        xsF = sz(4, T)
        Bf = sz(T)
        Cp = sz(2, T)
        dt = sz(NT, 8)
        da = sz(NT, 8)
        dz = sz(NT, 8)
        dz2 = sz(NT, 8)
        dpl = sz(NT, 8)
        cumc = sz(NT, 8)
        dte = sz(8)
        sw, _ = zone(work, KEEP, 20992)
        cva = acc[:, 0, :]
        cve = acc[:, 1, :]
        xsT = sw(NT, 512)
        Bt = sw(NT, P)
        Es2, ec2, Csp2, xdt2, xdd2 = [[take(*shape) for take in (sw, zone(ring, int(1024 * i), SLOT)[0])]
                                      for i, shape in ((0, (8, P)), (1, (8, P)), (2, (8, P)), (3, (512,)), (3.5, (512,)))]
        CBm2 = [sw(2, P) for _ in range(2)]
        dte2 = [dte, sw(8)]
        Sst = sw(4, 64)
        Stm = sw(4, 64)
        yF = sw(4, T)

        def pairs_of(eng, l):
            return eng.value_load(table[0:1, 30 + l:31 + l], min_val=8, max_val=MAX_BLOCKS // 2)

        def further_pairs(eng, l):
            return eng.value_load(table[0:1, 26 + l:27 + l], min_val=7, max_val=MAX_BLOCKS // 2 - 1)

        PARTS = ("gate", "up", "down")
        w_loaded = [[sem(f"l{l}_{w}_{j}_loaded") for j in ("even", "odd") for w in PARTS]
                    for l in range(DEPTH)]
        gathered = [[sem(f"l{l}_{j}_rows_gathered") for j in ("even", "odd")] for l in range(DEPTH)]

        BLOCKS = [
            [(0, 256, 128, "q", 0), (0, 384, 128, "q", 1), (0, 0, 128, "shift", 12), (0, 128, 128, "shift", 13)]
            + [(1, 0, 128, "k", 0), (1, 128, 128, "k", 1), (1, 256, 16, "lora", 0)]
            + [(2, 0, 512, "v", t) for t in range(NT)] + [(3, 128 * j, 128, "gate", j) for j in range(4)]
            + [(4 + i, 128 * j, 128, "shift", 4 * i + j) for i in range(3) for j in range(4)],
            [(0, 0, 128, "q", 0), (0, 128, 128, "q", 1), (0, 256, 128, "f", 0), (0, 384, 128, "f", 1)]
            + [(1, 0, 512, "v", t) for t in range(NT)] + [(2, 128 * j, 128, "gate", j) for j in range(4)]
            + [(3, 128 * j, 128, "z", j) for j in range(4)]
            + [(4, 0, 128, "conv", 4), (4, 128, 128, "conv", 5), (4, 256, 8, "dt", 0)]
            + [(5, 128 * j, 128, "conv", j) for j in range(4)],
        ]
        NB = [len(b) for b in BLOCKS]
        WITH_ACT = ("shift", "gate", "f", "z")
        LOGS, SUMS, LEVELS = 0, 1, 2
        TILE_DECAYS = LEVELS + len(LV) + 1
        KEYS_TURNED = TILE_DECAYS + 1
        OUTPUTS = KEYS_TURNED + 1
        GATED = OUTPUTS + NT
        AFTER = [(6, 7, 9, 10, 12, 13, 14, 16, 17, 18, 19, 20, 21, 22, 22, 23, 23, 24, 25, 26),
                 (3, 4, 6, 7, 8, 10, 11, 13, 14, 15, 16, 17, 18, 19, 20, 21, 22, 22, 22, 22)]

        def steps_after(l, n):
            return [step for step, block in enumerate(AFTER[l]) if block == n]

        AB = 2

        def act_blocks(l, n):
            return sum(b[3] in WITH_ACT for b in BLOCKS[0][:NB[0] if l else n]) + \
                (sum(b[3] in WITH_ACT for b in BLOCKS[1][:n]) if l else 0)

        def chunk_blocks(l, i):
            return l * NB[0] + sum(b[0] <= i for b in BLOCKS[l])

        shifted = [rr[:, j, :] for j in range(4)] + [kk_[:, j, :] for j in range(4)] \
            + [vv[:, j, :] for j in range(4)] + [wad, gdp]
        lgf = lg.rearrange("p t s -> p (t s)")
        lev_n = len(LV)

        def halves(ap, hh):
            v = ap.rearrange("p (n two h) -> p n two h", two=2, h=hh)
            return v[:, :, 0, :], v[:, :, 1, :]

        def x_at(n, k):
            return [k + 1, k + 1, 9, 9 + k + 1, 18][n]

        HALVES = 24
        half_place = [y_[:, 2048 * i:2048 * (i + 1)].rearrange("p (k n) -> p k n", n=256) for i in range(2)]
        half_acc = [acc.rearrange("p a b -> p (a b)")[:, 256 * i:256 * (i + 1)] for i in range(4)]

        block = ctx.enter_context(nc.Block())

        @block.sync
        def _(sp):
            def load_half(i):
                if i >= 2:
                    sp.wait_ge(sem("half_used"), i - 1)
                sp.dma_start(half_place[i % 2], A["w_ada"][1].rearrange("(k p) n -> p k n", p=P)
                             [:, :, 256 * i:256 * (i + 1)]).then_inc(sem(f"half_loaded{i % 2}"), 16)

            def load(n):
                if PLAN[n] == ("out", 0, 1):
                    sp.wait_ge(sem("rwkv_done"), NT - 1)
                if n >= RING and PLAN[n - RING] is not None:
                    kind, l, i = PLAN[n - RING]
                    if kind == "ada":
                        sp.wait_ge(sem("ada_used"), 12 * l + i + 1)
                    elif kind == "in":
                        sp.wait_ge(sem("proj_done"), chunk_blocks(l, i))
                    else:
                        sp.wait_ge(sem("outproj_done"), 8 * l + 4 * (i + 1))
                kind, l, i = PLAN[n]
                dst, src = ring_ap(PLAN[n]), w_src(PLAN[n])
                if kind == "in" and len(IN_PIECES[l][i]) == 2:
                    (_, w), (c2, w2) = IN_PIECES[l][i]
                    sp.dma_start(dst[:, :, w:w + w2], A["w_in_even"][0].rearrange("(k p) n -> p k n", p=P)
                                 [:, :, c2:c2 + w2]).then_inc(sem("second_piece_loaded"), 16)
                    dst = dst[:, :, 0:w]
                sp.dma_start(dst, src).then_inc(slot_loaded[n % RING], 16)

            ws = [A["w_gate"], A["w_up"], A["w_down"]]
            n = 0
            for l in range(DEPTH):
                while n < len(PLAN) and (PLAN[n] is None or PLAN[n][1] <= l):
                    if PLAN[n] is not None:
                        load(n)
                    if l == 0 and 14 <= n < 18:
                        for i in range(4 * (n - 14), 4 * (n - 13)):
                            load_half(i)
                    if n == 18:
                        for i in range(16, HALVES):
                            load_half(i)
                    n += 1
                sp.wait_ge(sem("outproj_done"), 8 * (l + 1))
                sp.wait_ge(sem("x_ready"), 9 * l + 1)
                for j in range(2):
                    for i in range(3):
                        sp.dma_start(moe_w[j][i], ws[i][l, j].rearrange("(k p) n -> p k n", p=P))\
                          .then_inc(w_loaded[l][3 * j + i], 16)
                sp.wait_ge(sem("table_ready"), l + 1)
                further = further_pairs(sp, l)
                with sp.Fori(0, further) as it:
                    for j in range(2):
                        e = sp.value_load(table[0:1, bass.ds(it * 2 + (j + 2), 1)], min_val=0, max_val=E - 1)
                        for i in range(3):
                            sp.wait_ge(sem(f"l{l}_{PARTS[i]}_done"), it * 2 + (j + 1))
                            src = ws[i][l][bass.ds(e, 1)].rearrange("o (k p) n -> p (o k) n", p=P)
                            sp.dma_start(moe_w[j][i], src).then_inc(w_loaded[l][3 * j + i], 16)
                sp.wait_ge(sem(f"l{l}_down_done"), further * 2 + 2)
                sp.sem_inc(sem("passed"), 1)
                sp.wait_ge(sem(f"expert_rows{NT - 1}"), 32 * (l + 1))

        @block.gpsimd
        def _(pool):
            steps = [0]

            def link(ins):
                steps[0] += 1
                ins.then_inc(sem("pool_order"), 1)
                pool.wait_ge(sem("pool_order"), steps[0])

            def fill(ap, value):
                link(pool.memset(ap, value))

            def keep_where(ap, base, pattern, mult, cmp=ALU.is_ge, fill_value=0.0):
                link(pool.affine_select(out=ap, in_=ap, compare_op=cmp, fill=fill_value, base=base,
                                        pattern=pattern, channel_multiplier=mult))

            fill(ident, 0.0)
            keep_where(ident, 0, [[-1, P]], 1, ALU.not_equal, 1.0)
            fill(epsc[:, 0:1], EPS)
            fill(epsc[:, 1:2], GN_EPS)
            fill(epsc[:, 2:3], 1e-12)
            fill(epsc[:, 3:4], 1.0)
            pool.memset(ones, 1.0).then_inc(sem("pool_const"), 1)
            fill(upper, 1.0)
            keep_where(upper, 0, [[1, P]], -1)
            fill(headones, 1.0)
            hv = headones.rearrange("p (n h) -> p n h", h=64)
            keep_where(hv, 0, [[-64, 2], [0, 64]], 1)
            keep_where(hv, 63, [[64, 2], [0, 64]], -1)
            for m, base, step, mult in ((strict_up, -1, 1, -1), (incl_up, 0, 1, -1), (strict_lo, -1, -1, 1)):
                link(pool.tensor_copy(m, headones))
                keep_where(m, base, [[step, P]], mult)
            for hh in LV:
                for m, half, lo in ((lev_up.get(hh), 1, 0), (lev_lo.get(hh), 0, hh)):
                    if m is None:
                        continue
                    fill(m, 0.0)
                    v = m.rearrange("p (n two h) -> p n two h", two=2, h=hh)[:, :, half, :]
                    nb = P // (2 * hh)
                    fill(v, 1.0)
                    keep_where(v, -lo, [[-2 * hh, nb], [0, hh]], 1)
                    keep_where(v, lo + hh - 1, [[2 * hh, nb], [0, hh]], -1)
            for m, c in ((reset64, 64), (reset128, 128)):
                fill(m, 1.0)
                fill(m.rearrange("p (n c) -> p n c", c=c)[:, :, 0:1], 0.0)
            for ap, n, mult in ((iota16, E, 0), (iota24, MAX_BLOCKS, 0), (iota128, P, 0), (pidx, 1, 1)):
                link(pool.iota(scratch_i[:, 0:n], pattern=[[1, n]], base=0, channel_multiplier=mult))
                link(pool.tensor_copy(ap, scratch_i[:, 0:n]))
            link(pool.iota(scratch_i[:, 0:NT], pattern=[[P, NT]], base=0, channel_multiplier=1))
            link(pool.tensor_copy(tokid, scratch_i[:, 0:NT]))
            pool.memset(idx_tok[:, :], 0).then_inc(sem("pool_const"), 1)

            pool.wait_ge(sem("setup_step"), 1)
            pool.wait_ge(sem("ada_summed"), 12)
            for i in range(HALVES):
                pool.wait_ge(sem(f"half_loaded{i % 2}"), 16 * (i // 2 + 1))
                if i >= 4:
                    pool.wait_ge(sem("half_summed"), i - 3)
                w = half_place[i % 2]
                link(pool.tensor_tensor(w, w, cond.unsqueeze(2).to_broadcast([P, KD, 256]), ALU.mult))
                link(pool.tensor_tensor(w[:, 0:4, :], w[:, 0:4, :], w[:, 4:8, :], ALU.add))
                link(pool.tensor_tensor(w[:, 0:2, :], w[:, 0:2, :], w[:, 2:4, :], ALU.add))
                pool.tensor_tensor(half_acc[i % 4], w[:, 0, :], w[:, 1, :], ALU.add).then_inc(sem("half_used"), 1)

            for l in range(DEPTH):
                pool.wait_ge(sem("table_ready"), l + 1)
                pool.wait_ge(sem(f"l{l}_rows_stored"), 16)
                further = further_pairs(pool, l)
                sg, sc_ = sem(f"l{l}_xt_turned"), sem(f"l{l}_idx_copied")

                def gather(b, j, it_wait, n):
                    if it_wait is not None:
                        pool.wait_ge(sg, it_wait)
                    pool.tensor_copy(idx_cur[:, j:j + 1], idx_tok[:, b]).then_inc(sc_, 1)
                    pool.wait_ge(sc_, n)
                    pool.sem_inc(sem("passed"), 1)
                    pool.indirect_dma_start(
                        xg[:, j, :], None, h_dram, bass.IndirectOffsetOnAxis(ap=idx_cur[:, j:j + 1], axis=0))\
                        .then_inc(gathered[l][j], 16)

                gather(bass.ds(0, 1), 0, None, 1)
                gather(bass.ds(1, 1), 1, None, 2)
                with pool.Fori(0, further) as it:
                    for j in range(2):
                        gather(bass.ds(it * 2 + (j + 2), 1), j, it * 2 + (j + 1), it * 2 + (j + 3))
                gather(bass.ds(further * 2 + 2, 1), 0, further * 2 + 1, further * 2 + 3)

                pool.wait_ge(sem(f"l{l}_rows_stored"), (further * 2 + 3) * 16)
                pool.sem_inc(sem("passed"), 1)
                for t in range(NT):
                    for k in range(2):
                        pool.indirect_dma_start(
                            cg[:, t * 2 + k, :], None, y_dram,
                            bass.IndirectOffsetOnAxis(ap=idx_dest[:, k * NT + t:k * NT + t + 1], axis=0))\
                            .then_inc(sem(f"expert_rows{t}"), 16)

        @block.scalar
        def _(act):
            steps = [0]

            def link(ins):
                steps[0] += 1
                ins.then_inc(sem("act_order"), 1)
                act.wait_ge(sem("act_order"), steps[0])

            def sigmoid(ap, src):
                link(act.activation(ap, src, ACT.Exp, scale=-1.0))
                link(act.activation(ap, ap, ACT.Ln, bias=epsc[:, 3:4]))
                return act.activation(ap, ap, ACT.Exp, scale=-1.0)

            act.dma_start(work[0:KD, 4096 + 2 * P:4096 + 3 * P], A["c"][0].rearrange("(k p) -> k p", p=P)).then_inc(sem("c_loaded"), 16)
            act.dma_start(work[:, 0:4096].rearrange("p (a d) -> p a d", d=D),
                         A["x"][0].rearrange("(a p) d -> p a d", p=P)).then_inc(sem("x_loaded"), 16)

            def rows_of(name):
                a = A[name]
                names = "a b c d"[:2 * len(a.shape) - 1]
                flat = a.rearrange(f"{names} -> ({names})") if len(a.shape) > 1 else a
                return flat.rearrange("(r c) -> r c", c=P)

            for tile, rows in enumerate((ROWS1, ROWS2)):
                c = 0
                for name, k in rows:
                    act.dma_start(work[c:c + k, 4096 + tile * P:4096 + (tile + 1) * P],
                                 rows_of(name)).then_inc(sem("rows_loaded"), 16)
                    c += k

            act.wait_ge(sem("pool_const"), 1)
            act.wait_ge(sem("x_turned"), 1)
            sigmoid(cexp, PS[:, 5, 0:KD]).then_inc(sem("setup_exp"), 1)

            act.dma_start(wup[0:64, :], A["a_w_up"][0]).then_inc(sem("params_loaded"), 16)
            act.dma_start(wup[64:128, :], A["a_a_up"][0]).then_inc(sem("params_loaded"), 16)
            act.dma_start(gup, A["a_g_up"][0]).then_inc(sem("params_loaded"), 16)
            act.dma_start(alup[0:16, :], A["b_alpha_up"][0]).then_inc(sem("params_loaded"), 16)
            act.dma_start(wr, A["w_router"].rearrange("(k p) e -> p k e", p=P)).then_inc(sem("params_loaded"), 16)
            act.dma_start(dtb, A["d_dt_bias"].to_broadcast([P, 8])).then_inc(sem("params_loaded"), 16)
            act.dma_start(alog, A["d_a_log"].to_broadcast([P, 8])).then_inc(sem("params_loaded"), 16)
            act.dma_start(rbias, A["router_bias"].unsqueeze(0).to_broadcast([P, E])).then_inc(sem("params_loaded"), 16)
            act.dma_start(rs_skip, A["d_skip"].to_broadcast([P, 8])).then_inc(sem("params_loaded"), 16)

            for k in range(KD):
                act.wait_ge(sem("x_turned"), k + 2)
                act.activation(xT[:, k, :], PS[:, k % 4, :], ACT.Copy).then_inc(sem("x_copied"), 1)


            def norm(n):
                l, place = n // 2, n % 2
                for k in range(KD):
                    act.wait_ge(sem("x_ready" if n else "x_copied"), x_at(n, k))
                    act.activation(h[:, k, :], xT[:, k, :], ACT.Square).then_inc(sem("sq_ready"), 1)
                act.wait_ge(sem("ms_ready"), n + 1)
                link(act.activation(rs, PS[:, 6, :], ACT.Ln, bias=epsc[:, 0:1], scale=1.0 / D))
                act.activation(rs, rs, ACT.Exp, scale=-0.5).then_inc(sem("rstd_ready"), 1)
                if n < 4:
                    act.wait_ge(sem("amul_ready"), l + 1)
                for k in range(KD):
                    act.wait_ge(sem("xn_ready"), KD * n + k + 1)
                    if n < 4:
                        act.activation(h[:, k, :], h[:, k, :], ACT.Identity, scale=amul[:, l, place, k:k + 1],
                                       bias=mod[:, l, 24 * place + k:24 * place + k + 1]).then_inc(sem("h_ready"), 1)
                    else:
                        act.activation(h[:, k, :], h[:, k, :], ACT.Copy, scale=prm_col("final_gain", k))\
                           .then_inc(sem("h_ready"), 1)

            def projections(l):
                for n, (c, c0, w, kind, j) in enumerate(BLOCKS[l]):
                    ps = PS[:, n % 2, :]
                    if kind in WITH_ACT:
                        act.wait_ge(sem("proj_done"), l * NB[0] + n + 1)
                        if kind == "shift":
                            ins = act.activation(shifted[j], ps, ACT.Copy, scale=omu[:, j:j + 1])
                        else:
                            ins = sigmoid({"gate": lgate, "f": lg, "z": zs if l else None}[kind][:, j, :], ps)
                        ins.then_inc(sem("proj_act"), 1)
                    if kind == "conv":
                        act.wait_ge(sem("proj_copied"), NB[0] + n + 1)
                        sigmoid(cve, cva).then_inc(sem("conv_act"), 1)
                    if l == 0 and n == 5:
                        act.wait_ge(sem("proj_copied"), 4)
                        link(act.activation(wad[0:64, :], wad[0:64, :], ACT.Tanh))
                        sigmoid(gdp, gdp).then_inc(sem("setup_exp"), 1)
                    for step in steps_after(l, n):
                        attention(l, step)
                    if l == 1 and n == 19:
                        act.wait_ge(sem("setup_step"), 3)
                        act.activation(dz, dz, ACT.Exp)
                        act.activation(alog, alog, ACT.Exp).then_inc(sem("setup_exp"), 1)

            def attention(l, step):
                level = step - LEVELS
                if step == LOGS and l == 0:
                    act.wait_ge(sem("log_pre"), 1)
                    link(act.activation(le, le, ACT.Exp))
                    act.activation(le, le, ACT.Ln, bias=epsc[:, 3:4]).then_inc(sem("log_done"), 1)
                elif step == LOGS:
                    act.wait_ge(sem("log_pre"), 2)
                    act.activation(lgf, lgf, ACT.Ln).then_inc(sem("log_done"), 1)
                elif step == SUMS or 0 <= level < lev_n - 1:
                    n = 0 if step == SUMS else level + 1
                    act.wait_ge(sem("lev_diff"), lev_n * l + n + 1)
                    act.activation(le, le, ACT.Exp).then_inc(sem("lev_exp"), 1)
                elif step == TILE_DECAYS:
                    act.wait_ge(sem("lev_ready"), (lev_n + 1) * (l + 1))
                    act.activation(le, lgf, ACT.Exp).then_inc(sem("tile_decay"), 1)
                    act.wait_ge(sem("end_keys"), 2 * l + 1)
                    act.activation(le, le, ACT.Exp).then_inc(sem("tile_decay"), 1)
                elif step >= GATED:
                    hd = step - GATED
                    act.wait_ge(sem("o_ready"), l + 1)
                    act.activation(lsq[:, hd, :], PS[:, AB + hd, :], ACT.Square).then_inc(sem("o_sq"), 1)
                    act.wait_ge(sem("o_ms"), 4 * l + hd + 1)
                    link(act.activation(lrms[:, hd, :], PS[:, 6, :], ACT.Ln, bias=epsc[:, 0:1], scale=1.0 / P))
                    act.activation(lrms[:, hd, :], lrms[:, hd, :], ACT.Exp, scale=-0.5).then_inc(sem("o_rstd"), 1)

            def f2(ap):
                return ap.rearrange("p a b -> p (a b)")

            def front(t, piece):
                sga, sg, aa, cs, eb, b1 = (buffer[t % 2] for buffer in (SGA, SG, AA, CS, EB, B1))
                if piece == 0:
                    if t >= 2:
                        act.wait_ge(sem("rwkv_done"), t - 1)
                    act.wait_ge(sem("lora_done"), 2 * t + 1)
                    for j in range(4):
                        act.activation(sg[:, j, :], PS[:, 6, j * P:(j + 1) * P], ACT.Exp, scale=-1.0,
                                       bias=negw0[:, j:j + 1])
                        ins = act.activation(aa[:, j, :], PS[:, 7, j * P:(j + 1) * P], ACT.Exp, scale=-1.0,
                                             bias=nega0[:, j:j + 1])
                    link(ins)
                    link(act.activation(sga, sga, ACT.Ln, bias=epsc[:, 3:4]))
                    act.activation(sga, sga, ACT.Exp, scale=-1.0).then_inc(sem("front_act"), 1)
                elif piece == 1:
                    act.wait_ge(sem("lora_done"), 2 * t + 2)
                    act.activation(y[:, 0:4, t * P:(t + 1) * P], PS[:, 6, :].rearrange("p (a b) -> p a b", b=P),
                                   ACT.Copy).then_inc(sem("gate_copied"), 1)
                    act.wait_ge(sem("cs_ready"), t + 1)
                    act.activation(eb, cs, ACT.Exp, scale=-RW)
                    link(act.activation(sg, sg, ACT.Exp, scale=-RW))
                    act.activation(cs, cs, ACT.Exp, scale=RW).then_inc(sem("front_act"), 1)
                elif piece == 2:
                    act.wait_ge(sem("kk_ss"), t + 1)
                    link(act.activation(f2(b1), PS[:, 7, :], ACT.Ln, bias=epsc[:, 2:3]))
                    act.activation(b1, b1, ACT.Exp, scale=-0.5).then_inc(sem("front_act"), 1)

            def turned(t):
                act.wait_ge(sem("turns"), t + 1)
                for i, dst in enumerate((Vt, kaT, beT)):
                    act.activation(dst, PS[:, i, :], ACT.Copy)
                act.activation(alT, PS[:, 4, :], ACT.Copy).then_inc(sem("turned"), 1)

            def inversion(t):
                def heads_copy(dst, bank, g, name):
                    act.activation(dst[:, 4 * g:4 * g + 4, :], PS[:, bank + g, :].rearrange("p (b c) -> p b c", c=P),
                                   ACT.Copy).then_inc(sem(name), 1)

                for g in range(2):
                    act.wait_ge(sem("inv_turned"), 10 * t + g + 1)
                    heads_copy(TT, 4, g, "inv_copied")
                for n in range(5):
                    for g in range(2):
                        act.wait_ge(sem("g_ready"), 10 * t + 2 * n + g + 1)
                        heads_copy(G2, 2, g, "g_copied")
                        if n:
                            act.wait_ge(sem("inv_turned"), 10 * t + 2 * n + g + 1)
                            heads_copy(Tm, 4, g, "inv_copied")
                    if t + 1 < NT:
                        for piece in ((), (), (0,), (), (1, 2))[n]:
                            front(t + 1, piece)

            def rwkv():
                act.wait_ge(sem("half_used"), HALVES)
                act.wait_ge(sem("st_done"), 1)
                act.dma_start(y_dram[E * P:, :].rearrange("(b p) d -> p b d", p=P), bc(f2(RHO[1]), MAX_BLOCKS - E, 1))\
                   .then_inc(sem("rows_cleared"), 16)
                for piece in range(3):
                    front(0, piece)
                turned(0)
                for t in range(NT):
                    inversion(t)
                    act.wait_ge(sem("rw_ready"), 2 * t + 1)
                    act.activation(R0, PS[:, 2, :], ACT.Copy)
                    act.activation(f2(WnT), PS[:, 3, :], ACT.Copy).then_inc(sem("rw_copied"), 1)
                    act.wait_ge(sem("rw_ready"), 2 * t + 2)
                    act.activation(U0, PS[:, 4, :], ACT.Copy).then_inc(sem("rw_copied"), 1)
                    act.wait_ge(sem("y1_ready"), t + 1)
                    act.activation(f2(SG[t % 2]), PS[:, 6, :], ACT.Copy).then_inc(sem("ys_copied"), 1)
                    if t + 1 < NT:
                        turned(t + 1)
                    eb = EB[t % 2]
                    act.wait_ge(sem("gn_sum"), 2 * t + 2)
                    link(act.activation(f2(eb), PS[:, 7, :], ACT.Ln, bias=epsc[:, 1:2], scale=1.0 / 64))
                    act.activation(eb, eb, ACT.Exp, scale=-0.5).then_inc(sem("gn_rstd"), 1)

            def ssd():
                for t in range(NT):
                    b, dte_t = 2 + 3 * (t % 2), dte2[t % 2]
                    act.wait_ge(sem("seg_diff"), t + 1)
                    act.activation(Es2[t % 2], Es2[t % 2], ACT.Exp).then_inc(sem("seg_exp"), 1)
                    act.activation(ec2[t % 2], PS[:, b:b + 2, :].rearrange("p a (b c) -> p (a b) c", c=P), ACT.Exp)
                    act.activation(dte_t, dte_t, ACT.Exp).then_inc(sem("seg_exp"), 1)
                act.wait_ge(sem("yz_ready"), 1)
                for j in range(4):
                    act.activation(xsT[:, j, :], yF[:, j, :], ACT.Square).then_inc(sem("o_sq"), 1)
                for g in range(2):
                    act.wait_ge(sem("o_ms"), 8 + g + 1)
                    half = f2(Es2[0])[:, 512 * g:512 * g + 512]
                    link(act.activation(half, PS[:, g, :], ACT.Ln, bias=epsc[:, 0:1], scale=1.0 / 256))
                    act.activation(half, half, ACT.Exp, scale=-0.5).then_inc(sem("o_rstd"), 1)

            def experts(l):
                act.wait_ge(sem("logits_ready"), l + 1)
                act.activation(sc, PS[:, 4, 0:NT * E].rearrange("p (a b) -> p a b", b=E), ACT.Exp, scale=-1.0)\
                   .then_inc(sem("logits_exp"), 1)
                for t in range(NT):
                    act.wait_ge(sem("rows_turned"), NT * l + t + 1)
                    b = 2 * (t % 2)
                    act.activation(y_[:, t * D:(t + 1) * D], PS[:, b:b + 2, :].rearrange("p a b -> p (a b)"), ACT.Copy)\
                       .then_inc(sem("rows_copied"), 1)
                act.wait_ge(sem("rows_copied"), NT * (l + 1))
                row_dma = sem(f"l{l}_rows_stored")
                act.dma_start(h_dram.rearrange("(a p) d -> p a d", p=P),
                              y_[:, :].rearrange("p (a d) -> p a d", d=D)).then_inc(row_dma, 16)

                def x_copy(n):
                    act.wait_ge(sem(f"l{l}_xt_turned"), n)
                    act.activation(xTb, PS[:, 2:4, :].rearrange("p a (b c) -> p (a b) c", c=P), ACT.Copy)\
                       .then_inc(sem(f"l{l}_xt_copied"), 1)

                act.wait_ge(sem("table_ready"), l + 1)
                pairs = pairs_of(act, l)
                x_copy(1)
                with act.Fori(0, pairs) as it:
                    for j in range(2):
                        b1 = it * 2 + (j + 1)
                        act.wait_ge(sem(f"l{l}_gate_done"), b1)
                        act.activation(sgt, PS[:, 0, :], ACT.Exp, scale=-1.0).then_inc(sem(f"l{l}_gate_exp"), 1)
                        x_copy(b1 + 1)
                        act.wait_ge(sem(f"l{l}_down_done"), b1)
                        act.wait_ge(row_dma, b1 * 16)
                        act.activation(yb, PS[:, 5:7, :].rearrange("p a b -> p (a b)"), ACT.Copy)\
                           .then_inc(sem(f"l{l}_y_copied"), 1)
                        act.wait_ge(sem(f"l{l}_y_copied"), b1)
                        act.dma_start(y_dram[bass.ds((it * 2 + j) * P, P), :], yb).then_inc(row_dma, 16)

            norm(0)
            act.wait_ge(sem("setup_step"), 2)
            act.activation(lbt[:, 4:8], lbt[:, 4:8], ACT.Exp).then_inc(sem("setup_exp"), 1)
            projections(0)
            rwkv()
            norm(1)
            experts(0)
            norm(2)
            projections(1)
            ssd()
            norm(3)
            experts(1)
            norm(4)
            for t in range(NT):
                act.wait_ge(sem("rows_turned"), NT * DEPTH + t + 1)
                b = 2 * (t % 2)
                act.activation(y_[:, t * D:(t + 1) * D], PS[:, b:b + 2, :].rearrange("p a b -> p (a b)"), ACT.Copy)\
                   .then_inc(sem("rows_copied"), 1)
                act.wait_ge(sem("rows_copied"), NT * DEPTH + t + 1)
                act.dma_start(out[0, t * P:(t + 1) * P, :], y_[:, t * D:(t + 1) * D]).then_inc(sem("out_stored"), 16)
            act.wait_ge(sem("out_stored"), 16 * NT)

        @block.tensor
        def _(pe):
            mm = nc.tensor.matmul
            tr = nc.tensor.transpose

            pe.wait_ge(sem("pool_const"), 1)
            pe.wait_ge(sem("c_loaded"), 16)
            tr(PS[:, 5, 0:KD], work[0:KD, 4096 + 2 * P:4096 + 3 * P], ident[0:KD, 0:KD]).then_inc(sem("x_turned"), 1)
            pe.wait_ge(sem("x_loaded"), 16)
            for k in range(KD):
                if k >= 4:
                    pe.wait_ge(sem("x_copied"), k - 3)
                for t in range(NT):
                    ins = tr(PS[:, k % 4, t * P:(t + 1) * P], work[:, t * D + k * P:t * D + (k + 1) * P], ident)
                ins.then_inc(sem("x_turned"), 1)
            def ada_sums(i):
                pe.wait_ge(sem("ada_used"), i + 1)
                for j in range(4):
                    ins = mm(PS[:, 7, 4 * i + j:4 * i + j + 1], lhsT=acc[:, i % 2, j * P:(j + 1) * P],
                             rhs=ones[:, 0:1], start=True, stop=True)
                ins.then_inc(sem("ada_summed"), 1)

            def half_sums(i):
                pe.wait_ge(sem("half_used"), i + 1)
                for j in range(2):
                    ins = mm(PS[:, 7, 2 * i + j:2 * i + j + 1], lhsT=half_acc[i % 4][:, j * P:(j + 1) * P],
                             rhs=ones[:, 0:1], start=True, stop=True)
                ins.then_inc(sem("half_summed"), 1)

            def norm(n):
                for k in range(KD):
                    pe.wait_ge(sem("sq_ready"), KD * n + k + 1)
                    ins = mm(PS[:, 6, :], lhsT=ones, rhs=h[:, k, :], start=(k == 0), stop=(k == KD - 1))
                ins.then_inc(sem("ms_ready"), 1)

            def projections(l):
                last = -1
                for n, (c, c0, w, kind, j) in enumerate(BLOCKS[l]):
                    if c != last:
                        arrived(pe, ("in", l, c))
                        last = c
                    if kind == "lora":
                        pe.wait_ge(sem("second_piece_loaded"), 16)
                    if n >= 2:
                        pe.wait_ge(sem("proj_copied"), l * NB[0] + n - 1)
                    W = ring_ap(("in", l, c))
                    b = n % 2
                    if kind == "v":
                        for k in range(KD):
                            ins = mm(PS[:, b, :], lhsT=h[:, k, j * P:(j + 1) * P], rhs=W[:, k, 0:512],
                                     start=(k == 0), stop=(k == KD - 1))
                    elif kind == "dt":
                        for t in range(NT):
                            for k in range(KD):
                                ins = mm(PS[:, b, 8 * t:8 * t + 8], lhsT=h[:, k, t * P:(t + 1) * P],
                                         rhs=W[:, k, c0:c0 + 8], start=(k == 0), stop=(k == KD - 1))
                    else:
                        for k in range(KD):
                            if n == 0:
                                pe.wait_ge(sem("h_ready"), KD * 2 * l + k + 1)
                            ins = mm(PS[0:w, b, :], lhsT=W[:, k, c0:c0 + w], rhs=h[:, k, :],
                                     start=(k == 0), stop=(k == KD - 1))
                    ins.then_inc(sem("proj_done"), 1)
                    if l == 0 and 1 <= n <= HALVES:
                        half_sums(n - 1)
                    for step in steps_after(l, n):
                        attention(l, step)

            def attention(l, step):
                kdT = lq.rearrange("p a b -> p (a b)").rearrange("p (t c) -> p t c", c=256)
                if step == LOGS and l == 0:
                    pe.wait_ge(sem("proj_copied"), 7)
                    for j in range(2):
                        ins = mm(PS[:, AB + j, :], lhsT=alup[0:16, j * P:(j + 1) * P], rhs=le[0:16, 0:T],
                                 start=True, stop=True)
                    ins.then_inc(sem("alpha_ready"), 1)
                elif LEVELS <= step < TILE_DECAYS:
                    at = (lev_n + 1) * l + step - LEVELS
                    pe.wait_ge(sem("lev_ready"), at + 1)
                    if at:
                        pe.wait_ge(sem("lev_merged"), at)
                    for t in range(NT):
                        for hd in range(4):
                            ins = mm(PS[:, AB + t, hd * P:(hd + 1) * P], lhsT=lkp[:, hd // 2, t * P:(t + 1) * P],
                                     rhs=lqp[:, hd, t * P:(t + 1) * P], start=True, stop=True)
                    ins.then_inc(sem("lev_scored"), 1)
                elif step == KEYS_TURNED:
                    pe.wait_ge(sem("end_keys"), 2 * l + 2)
                    for t in range(2):
                        for j in range(2):
                            ins = tr(PS[:, 6, (2 * t + j) * P:(2 * t + j + 1) * P], lkp[:, j, t * P:(t + 1) * P], ident)
                    ins.then_inc(sem("kd_turned"), 1)
                elif OUTPUTS <= step < GATED:
                    t = step - OUTPUTS
                    if t == 0:
                        pe.wait_ge(sem("lev_merged"), (lev_n + 1) * (l + 1))
                    else:
                        pe.wait_ge(sem("ls_ready"), 3 * l + t)
                    for hd in range(4):
                        o = PS[:, AB + hd, t * P:(t + 1) * P]
                        ins = mm(o, lhsT=lv[:, t, hd * P:(hd + 1) * P], rhs=lA[:, 4 * t + hd, :],
                                 start=True, stop=(t == 0))
                        if t:
                            ins = mm(o, lhsT=lS[:, hd // 2, :], rhs=lqp[:, hd, t * P:(t + 1) * P],
                                     start=False, stop=True)
                    if t == NT - 1:
                        ins.then_inc(sem("o_ready"), 1)
                        return
                    if t == 0:
                        pe.wait_ge(sem("kdT_ready"), l + 1)
                    for hd in range(4):
                        p0 = 64 * (hd % 2)
                        ins = mm(PS[p0:p0 + 64, 6, (hd // 2) * P:(hd // 2 + 1) * P], lhsT=kdT[:, t, hd * 64:hd * 64 + 64],
                                 rhs=lv[:, t, hd * P:(hd + 1) * P], start=True, stop=True)
                    if t == 0:
                        for j in range(2):
                            ins = tr(PS[:, 6, (2 + j) * P:(3 + j) * P], lkp[:, j, 2 * P:3 * P], ident)
                    ins.then_inc(sem("ls_ps"), 1)
                elif step >= GATED:
                    hd = step - GATED
                    pe.wait_ge(sem("o_sq"), 4 * l + hd + 1)
                    if hd:
                        pe.wait_ge(sem("o_rstd"), 4 * l + hd)
                    mm(PS[:, 6, :], lhsT=ones, rhs=lsq[:, hd, :], start=True, stop=True).then_inc(sem("o_ms"), 1)

            def f2(ap):
                return ap.rearrange("p a b -> p (a b)")

            def front(t, piece):
                ts = slice(t * P, (t + 1) * P)
                if piece == 0:
                    if t >= 2:
                        pe.wait_ge(sem("rwkv_done"), t - 1)
                    for j in range(4):
                        js = slice(j * P, (j + 1) * P)
                        mm(PS[:, 6, js], lhsT=wup[0:64, js], rhs=wad[0:64, ts], start=True, stop=True)
                    for j in range(4):
                        js = slice(j * P, (j + 1) * P)
                        ins = mm(PS[:, 7, js], lhsT=wup[64:128, js], rhs=wad[64:128, ts], start=True, stop=True)
                    ins.then_inc(sem("lora_done"), 1)
                elif piece == 1:
                    pe.wait_ge(sem("front_act"), 3 * t + 1)
                    for j in range(4):
                        js = slice(j * P, (j + 1) * P)
                        ins = mm(PS[:, 6, js], lhsT=gup[:, js], rhs=gdp[:, ts], start=True, stop=True)
                    ins.then_inc(sem("lora_done"), 1)
                elif piece == 2:
                    pe.wait_ge(sem("kk_sq"), t + 1)
                    mm(PS[:, 7, :], lhsT=headones, rhs=f2(B1[t % 2]), start=True, stop=True).then_inc(sem("kk_ss"), 1)
                elif piece == 5:
                    pe.wait_ge(sem("feat_ready"), t + 1)
                    mm(PS[:, 3, :], lhsT=headones, rhs=f2(B1[t % 2]), start=True, stop=True)\
                        .then_inc(sem("bonus_sum"), 1)

            def turns(t):
                pe.wait_ge(sem("st_done"), 2 * t + 1)
                for b, src in ((0, vv[:, :, t * P:(t + 1) * P]), (1, KA[t % 2]), (2, BE[t % 2]), (4, SG[t % 2])):
                    for j in range(4):
                        ins = tr(PS[:, b, j * P:(j + 1) * P], src[:, j, :], ident)
                ins.then_inc(sem("turns"), 1)

            def score(t, n):
                ka, be, alp, rho = (buffer[t % 2] for buffer in (KA, BE, ALP, RHO))
                b, lhs, rhs = ((5, alp, be), (0, ka, alp), (2, ka, rho), (5, be, rho))[n]
                if n == 0 and t:
                    pe.wait_ge(sem("gn_in"), 2 * t - 1)
                if n == 1:
                    pe.wait_ge(sem("turned"), t + 1)
                if n == 2:
                    pe.wait_ge(sem("bonus_used"), t + 1)
                if n == 3:
                    pe.wait_ge(sem("score_copied"), 4 * t + 1)
                for hd in range(8):
                    o = PS[:, b + hd // 4, (hd % 4) * P:(hd % 4 + 1) * P]
                    left = lhs[:, hd if n == 0 else hd // 2, :]
                    right = rhs[:, hd // 2 if n == 0 else hd, :]
                    ins = mm(o, lhsT=left, rhs=right, start=True, stop=True)
                ins.then_inc(sem("score_ready"), 1)

            def inversion(t):
                def heads(bank, lhs, rhs, g, name):
                    for hd in range(4):
                        ins = mm(PS[:, bank + g, hd * P:(hd + 1) * P], lhsT=lhs[:, 4 * g + hd, :],
                                 rhs=rhs[:, 4 * g + hd, :], start=True, stop=True)
                    ins.then_inc(sem(name), 1)

                def turn(src, g):
                    for hd in range(4):
                        ins = tr(PS[:, 4 + g, hd * P:(hd + 1) * P], src[:, 4 * g + hd, :], ident)
                    ins.then_inc(sem("inv_turned"), 1)

                pe.wait_ge(sem("score_copied"), 4 * t + 4)
                for g in range(2):
                    pe.wait_ge(sem("inv_ready"), 12 * t + g + 1)
                    turn(Tm, g)
                for g in range(2):
                    pe.wait_ge(sem("inv_copied"), 10 * t + g + 1)
                    heads(2, X, TT, g, "g_ready")
                for n in range(5):
                    for g in range(2):
                        if n:
                            pe.wait_ge(sem("inv_copied"), 10 * t + 2 * n + g + 1)
                        pe.wait_ge(sem("g_copied"), 10 * t + 2 * n + g + 1)
                        heads(0, Tm, G2, g, "p_ready")
                    if n < 4:
                        for g in range(2):
                            pe.wait_ge(sem("inv_ready"), 12 * t + 2 * n + g + 3)
                            heads(2, X, TT, g, "g_ready")
                            turn(TT, g)
                    if t + 1 < NT:
                        for piece in ((), (0,), (), (1,), (2,))[n]:
                            front(t + 1, piece)
                pe.wait_ge(sem("inv_ready"), 12 * (t + 1))

            def solve(t):
                for hd in range(8):
                    mm(PS[:, 2, hd * 64:hd * 64 + 64], lhsT=LKT[:, hd, :], rhs=Vt[:, hd * 64:hd * 64 + 64],
                       start=True, stop=True)
                for hd in range(8):
                    p0 = 64 * (hd % 2)
                    ins = mm(PS[p0:p0 + 64, 3, (hd // 2) * P:(hd // 2 + 1) * P], lhsT=alT[:, hd * 64:hd * 64 + 64],
                             rhs=TT[:, hd, :], start=True, stop=True)
                ins.then_inc(sem("rw_ready"), 1)
                pe.wait_ge(sem("rw_copied"), 2 * t + 1)
                for hd in range(8):
                    ins = mm(PS[:, 4, hd * 64:hd * 64 + 64], lhsT=TT[:, hd, :], rhs=R0[:, hd * 64:hd * 64 + 64],
                             start=True, stop=True)
                ins.then_inc(sem("rw_ready"), 1)
                pe.wait_ge(sem("rw_copied"), 2 * t + 2)
                if t + 1 < NT:
                    pe.wait_ge(sem("gate_copied"), t + 2)
                for c in range(2):
                    po = 64 * c
                    pe.wait_ge(sem("st_done"), 2 * t + c + 1)
                    for hd in range(8):
                        mm(PS[po:po + 64, 3, hd * 64:hd * 64 + 64], lhsT=WnT[:, hd // 2, po:po + 64],
                           rhs=ST[:, hd, :], start=True, stop=True)
                    for hd in range(8):
                        p0 = 64 * (hd % 2)
                        at = (hd // 2) * P + po
                        ins = mm(PS[p0:p0 + 64, 6, at:at + 64], lhsT=ST[:, hd, :], rhs=RHO[t % 2][:, hd, po:po + 64],
                                 start=True, stop=True)
                    ins.then_inc(sem("un_ready"), 1)
                    pe.wait_ge(sem("un_done"), 2 * t + c + 1)
                    for hd in range(8):
                        p0 = 64 * (hd % 2)
                        hs = slice(hd * 64, hd * 64 + 64)
                        o = PS[p0:p0 + 64, 4, (hd // 2) * 64:(hd // 2) * 64 + 64]
                        mm(o, lhsT=kaT[po:po + 64, hs], rhs=Vt[po:po + 64, hs], start=True, stop=False)
                        ins = mm(o, lhsT=beT[po:po + 64, hs], rhs=Un[po:po + 64, hs], start=False, stop=True)
                    ins.then_inc(sem("st_ps"), 1)
                for hd in range(8):
                    p0 = 64 * (hd % 2)
                    hs = slice(hd * 64, hd * 64 + 64)
                    o = PS[p0:p0 + 64, 5, (hd // 2) * P:(hd // 2 + 1) * P]
                    mm(o, lhsT=Vt[:, hs], rhs=PKT[:, hd, :], start=True, stop=False)
                    ins = mm(o, lhsT=Un[:, hs], rhs=PBT[:, hd, :], start=False, stop=True)
                ins.then_inc(sem("y1_ready"), 1)

            def head_sums(t, n):
                pe.wait_ge(sem("gn_in"), 2 * t + n + 1)
                mm(PS[:, 7, :], lhsT=headones, rhs=f2((CS, EB)[n][t % 2]), start=True, stop=True)\
                    .then_inc(sem("gn_sum"), 1)

            def rwkv():
                pe.wait_ge(sem("yhalf"), 1)
                pe.wait_ge(sem("setup_exp"), 3)
                pe.wait_ge(sem("amul_ready"), 2)
                for piece in range(6):
                    front(0, piece)
                turns(0)
                for n in range(4):
                    score(0, n)
                for t in range(NT):
                    inversion(t)
                    solve(t)
                    if t + 1 < NT:
                        front(t + 1, 5)
                        turns(t + 1)
                    head_sums(t, 0)
                    if t + 1 < NT:
                        score(t + 1, 0)
                    head_sums(t, 1)
                    if t + 1 < NT:
                        for n in range(1, 4):
                            score(t + 1, n)

            def products(t):
                ts = slice(t * P, (t + 1) * P)
                b = 2 + 3 * (t % 2)
                if t == 1:
                    pe.wait_ge(sem("ssd_inputs"), 3)
                for hd in range(8):
                    mm(PS[:, b + hd // 4, (hd % 4) * P:(hd % 4 + 1) * P],
                       lhsT=da[:, t, hd:hd + 1].to_broadcast([P, P]), rhs=upper, start=True, stop=True)
                for g in range(2):
                    ins = mm(PS[:, b + 2, g * P:(g + 1) * P], lhsT=Bf[:, ts], rhs=Cp[:, g, ts], start=True, stop=True)
                ins.then_inc(sem("cb_ready"), 1)

            def ssd():
                pe.wait_ge(sem("yhalf"), 2)
                for t in range(NT):
                    for j in range(4):
                        tr(PS[:, t, j * P:(j + 1) * P], xsF[:, j, t * P:(t + 1) * P], ident)
                for t in range(NT):
                    ins = tr(PS[:, 4, t * P:(t + 1) * P], Bf[:, t * P:(t + 1) * P], ident)
                ins.then_inc(sem("xs_turned"), 1)
                pe.wait_ge(sem("ssd_inputs"), 1)
                mm(PS[:, 5, 0:32], lhsT=upper, rhs=da.rearrange("p a b -> p (a b)"), start=True, stop=True)\
                    .then_inc(sem("xs_turned"), 1)
                pe.wait_ge(sem("ssd_inputs"), 2)
                products(0)
                for t in range(NT):
                    if t + 1 < NT:
                        products(t + 1)
                    pe.wait_ge(sem("ssd_in"), t + 1)
                    if t:
                        pe.wait_ge(sem("ssd_y_copied"), t)
                    for hd in range(8):
                        p0 = 64 * (hd % 2)
                        o = PS[p0:p0 + 64, 0, (hd // 2) * P:(hd // 2 + 1) * P]
                        ins = mm(o, lhsT=xdt2[t % 2][:, hd * 64:hd * 64 + 64], rhs=Es2[t % 2][:, hd, :], start=True,
                                 stop=(t == 0))
                        if t:
                            ins = mm(o, lhsT=Sst[:, hd % 4, :], rhs=Csp2[t % 2][:, hd, :], start=False, stop=True)
                    ins.then_inc(sem("ssd_y_ready"), 1)
                    if t < NT - 1:
                        for g in range(2):
                            ins = mm(PS[64 * g:64 * g + 64, 1, 0:256], lhsT=Bt[:, t, 64 * g:64 * g + 64],
                                     rhs=xdd2[t % 2][:, 256 * g:256 * g + 256], start=True, stop=True)
                        ins.then_inc(sem("ssd_st_ps"), 1)
                for j in range(4):
                    pe.wait_ge(sem("o_sq"), 8 + j + 1)
                    ins = mm(PS[:, j // 2, :], lhsT=ones, rhs=xsT[:, j, :], start=(j % 2 == 0), stop=(j % 2 == 1))
                    if j % 2:
                        ins.then_inc(sem("o_ms"), 1)

            def outproj(l):
                pe.wait_ge(sem("mix_done"), l + 1)
                for n in range(KD):
                    if n % 4 == 0:
                        arrived(pe, ("out", l, n // 4))
                    if n >= 4:
                        pe.wait_ge(sem("x_ready"), 9 * l + n - 3)
                    W = ring_ap(("out", l, n // 4))
                    for k in range(KD):
                        ins = mm(PS[:, n % 4, :], lhsT=W[:, k, (n % 4) * P:(n % 4 + 1) * P], rhs=y[:, k, :],
                                 start=(k == 0), stop=(k == KD - 1))
                    ins.then_inc(sem("outproj_done"), 1)

            def experts(l):
                for t in range(NT):
                    for k in range(KD):
                        if t == 0:
                            pe.wait_ge(sem("h_ready"), KD * (2 * l + 1) + k + 1)
                        ins = mm(PS[:, 4, t * E:(t + 1) * E], lhsT=h[:, k, t * P:(t + 1) * P], rhs=wr[:, k, :],
                                 start=(k == 0), stop=(k == KD - 1))
                ins.then_inc(sem("logits_ready"), 1)
                for t in range(NT):
                    if t >= 2:
                        pe.wait_ge(sem("rows_copied"), NT * l + t - 1)
                    for k in range(KD):
                        ins = tr(PS[:, 2 * (t % 2) + k // 4, (k % 4) * P:(k % 4 + 1) * P], h[:, k, t * P:(t + 1) * P], ident)
                    ins.then_inc(sem("rows_turned"), 1)
                pe.wait_ge(sem("choices_ready"), l + 1)
                for t in range(NT):
                    for s in range(t + 1):
                        mm(PS[:, 5, t * E:(t + 1) * E], lhsT=(upper if s == t else ones), rhs=both[:, s, :],
                           start=(s == 0), stop=(s == t))
                for s in range(NT):
                    ins = mm(PS[:, 5, NT * E:(NT + 1) * E], lhsT=ones, rhs=both[:, s, :], start=(s == 0), stop=(s == NT - 1))
                ins.then_inc(sem("rank_ready"), 1)
                pe.wait_ge(sem("place_ready"), l + 1)
                for n in range(2 * NT):
                    ins = mm(PS[:, 6, 0:MAX_BLOCKS], lhsT=ohr[:, n, :], rhs=ohb[:, n, :], start=(n == 0),
                             stop=(n == 2 * NT - 1))
                ins.then_inc(sem("place_used"), 1)
                pe.wait_ge(sem("table_ready"), l + 1)
                pairs = pairs_of(pe, l)

                def turn_x(j, loads):
                    pe.wait_ge(gathered[l][j], loads)
                    for k in range(KD):
                        ins = tr(PS[:, 2 + k // 4, (k % 4) * P:(k % 4 + 1) * P], xg[:, j, k * P:(k + 1) * P], ident)
                    ins.then_inc(sem(f"l{l}_xt_turned"), 1)

                turn_x(0, 16)
                with pe.Fori(0, pairs) as it:
                    for j in range(2):
                        b1 = it * 2 + (j + 1)
                        wg, wu, wd = moe_w[j]
                        pe.wait_ge(sem(f"l{l}_xt_copied"), b1)
                        pe.wait_ge(w_loaded[l][3 * j], (it + 1) * 16)
                        for k in range(KD):
                            ins = mm(PS[:, 0, :], lhsT=xTb[:, k, :], rhs=wg[:, k, :], start=(k == 0), stop=(k == KD - 1))
                        ins.then_inc(sem(f"l{l}_gate_done"), 1)
                        pe.wait_ge(w_loaded[l][3 * j + 1], (it + 1) * 16)
                        for k in range(KD):
                            ins = mm(PS[:, 1, :], lhsT=xTb[:, k, :], rhs=wu[:, k, :], start=(k == 0), stop=(k == KD - 1))
                        ins.then_inc(sem(f"l{l}_up_done"), 1)
                        turn_x(1 - j, (it + 1) * 16 if j == 0 else (it + 2) * 16)
                        for s in range(2):
                            pe.wait_ge(sem(f"l{l}_act_done"), it * 4 + (2 * j + s + 1))
                            for k in (2 * s, 2 * s + 1):
                                ins = tr(PS[:, 4 + 3 * s, (k % 2) * P:(k % 2 + 1) * P], actb[:, k * P:(k + 1) * P], ident)
                            ins.then_inc(sem(f"l{l}_at_turned"), 1)
                        pe.wait_ge(w_loaded[l][3 * j + 2], (it + 1) * 16)
                        for n in range(2):
                            for k in range(4):
                                if n == 0 and k % 2 == 0:
                                    pe.wait_ge(sem(f"l{l}_at_copied"), it * 4 + (2 * j + k // 2 + 1))
                                ins = mm(PS[:, 5 + n, :], lhsT=aT[:, k, :], rhs=wd[:, k, n * 512:(n + 1) * 512],
                                         start=(k == 0), stop=(k == 3))
                        ins.then_inc(sem(f"l{l}_down_done"), 1)
                for t in range(NT):
                    pe.wait_ge(sem("combined"), NT * l + t + 1)
                    if t >= 2:
                        pe.wait_ge(sem("comb_added"), NT * l + t - 1)
                    for k in range(KD):
                        ins = tr(PS[:, 2 * (t % 2) + k // 4, (k % 4) * P:(k % 4 + 1) * P],
                                 cg[:, 2 * t, k * P:(k + 1) * P], ident)
                    ins.then_inc(sem("comb_turned"), 1)

            pe.wait_ge(sem("pool_const"), 2)
            pe.wait_ge(sem("params_loaded"), 16 * 9)
            for i in range(12):
                if i == 4:
                    norm(0)
                if i == 8:
                    pe.wait_ge(sem("rows_loaded"), 16 * (len(ROWS1) + len(ROWS2)))
                    n1 = sum(n for _, n in ROWS1)
                    tr(PS[:, 4, 0:n1], work[0:n1, 4096:4096 + P], ident[0:n1, 0:n1])
                    tr(PS[:, 4, P:2 * P], work[:, 4096 + P:4096 + 2 * P], ident).then_inc(sem("x_turned"), 1)
                ada_sums(i)
            projections(0)
            rwkv()
            outproj(0)
            norm(1)
            experts(0)
            norm(2)
            projections(1)
            ssd()
            outproj(1)
            norm(3)
            experts(1)
            norm(4)
            pe.wait_ge(sem("h_ready"), KD * 5)
            for t in range(NT):
                if t >= 2:
                    pe.wait_ge(sem("rows_copied"), NT * DEPTH + t - 1)
                for k in range(KD):
                    ins = tr(PS[:, 2 * (t % 2) + k // 4, (k % 4) * P:(k % 4 + 1) * P], h[:, k, t * P:(t + 1) * P], ident)
                ins.then_inc(sem("rows_turned"), 1)

        @block.vector
        def _(dve):
            steps = {}

            def link(ins):
                signal(ins, "dve_order")

            def signal(ins, name):
                steps[name] = steps.get(name, 0) + 1
                ins.then_inc(sem(name), 1)
                dve.wait_ge(sem(name), steps[name])

            def tt(out, a, b, op):
                return dve.tensor_tensor(out, a, b, op)

            def tsc(out, a, s1, op0, s2=None, op1=None):
                return dve.tensor_scalar(out, a, s1, s2, op0, op1) if op1 else dve.tensor_scalar(out, a, s1, None, op0)

            def stt(out, a, s, b, op0, op1):
                return dve.scalar_tensor_tensor(out=out, in0=a, scalar=s, in1=b, op0=op0, op1=op1)

            def f2(ap):
                return ap.rearrange("p a b -> p (a b)")

            def sigmoid_tail(ap):
                link(tsc(ap, ap, 1.0, ALU.add))
                link(dve.reciprocal(ap, ap))

            dve.wait_ge(sem("setup_exp"), 1)
            signal(tt(cond, cexp, PS[:, 5, 0:KD], ALU.mult), "setup_step")

            def ada_chunk(i):
                arrived(dve, ("ada", 0, i))
                if i >= 2:
                    dve.wait_ge(sem("ada_summed"), i - 1)
                w = ring_ap(("ada", 0, i))
                a = acc[:, i % 2, :]
                link(tsc(a, w[:, 0, :], cond[:, 0:1], ALU.mult))
                for k in range(1, KD - 1):
                    link(stt(a, w[:, k, :], cond[:, k:k + 1], a, ALU.mult, ALU.add))
                signal(stt(a, w[:, KD - 1, :], cond[:, KD - 1:KD], a, ALU.mult, ALU.add), "ada_used")

            def parameters():
                dve.wait_ge(sem("x_turned"), KD + 2)
                n1 = sum(n for _, n in ROWS1)
                link(dve.tensor_copy(prm[:, 0, 0:n1], PS[:, 4, 0:n1]))
                link(dve.tensor_copy(prm[:, 1, :], PS[:, 4, P:2 * P]))
                dve.wait_ge(sem("params_loaded"), 16 * 9)
                for par in range(2):
                    pp = slice(64 * par, 64 * par + 64)
                    link(dve.tensor_copy(skipc[pp, :], rs_skip[pp, par:8:2]))
                link(tsc(negw0, prm_col("a_w0", 0, 4), -1.0, ALU.mult))
                link(tsc(nega0, prm_col("a_a0", 0, 4), -1.0, ALU.mult))
                link(tsc(omu, prm_col("a_mu", 0, 14), -1.0, ALU.mult, 1.0, ALU.add))

            def modulation(l):
                if l == 0:
                    dve.wait_ge(sem("ada_summed"), 12)
                else:
                    dve.wait_ge(sem("half_summed"), HALVES)
                link(tt(mod[:, l, :], PS[:, 7, 0:48], prm_col("b_ada", 48 * l, 48), ALU.add))
                for place in range(2):
                    c = 8 + 24 * place
                    ins = stt(amul[:, l, place, :], mod[:, l, c:c + 8], 1.0,
                              prm_col("norm_gain", (2 * l + place) * 8, 8), ALU.add, ALU.mult)
                    if place == 0:
                        link(ins)
                signal(ins, "amul_ready")

            def norm(n):
                dve.wait_ge(sem("rstd_ready"), n + 1)
                for k in range(KD):
                    tt(h[:, k, :], xT[:, k, :], rs, ALU.mult).then_inc(sem("xn_ready"), 1)

            def projections(l):
                for n, (c, c0, w, kind, j) in enumerate(BLOCKS[l]):
                    ps = PS[:, n % 2, :]
                    if kind in WITH_ACT:
                        dve.wait_ge(sem("proj_act"), act_blocks(l, n + 1))
                    dve.wait_ge(sem("proj_done"), l * NB[0] + n + 1)
                    if kind == "shift":
                        o = shifted[j]
                        ins = stt(o[:, 1:T], ps[:, 0:T - 1], prm_col("a_mu", j), o[:, 1:T], ALU.mult, ALU.add)
                    elif kind == "q":
                        ins = tsc(lq[:, j, :], ps, 0.125 if l == 0 else 1.0, ALU.mult)
                    elif kind == "k":
                        ins = dve.tensor_copy(lk[:, j, :], ps)
                    elif kind == "v":
                        ins = dve.tensor_copy(lv[:, j, :], ps)
                    elif kind == "lora":
                        ins = dve.tensor_copy(le[0:16, 0:T], ps[0:16, :])
                    elif kind == "gate":
                        ins = tt(lgate[:, j, :], lgate[:, j, :], ps, ALU.mult)
                    elif kind == "z":
                        ins = tt(zs[:, j, :], zs[:, j, :], ps, ALU.mult)
                    elif kind == "f":
                        link(tsc(lg[:, j, :], lg[:, j, :], omlb[:, j:j + 1], ALU.mult, lb[:, j:j + 1], ALU.add))
                        ins = tsc(lk[:, j, :], lg[:, j, :], -1.0, ALU.mult, 1.0, ALU.add)
                    elif kind == "dt":
                        ins = tt(dt, ps[:, 0:32].rearrange("p (a b) -> p a b", b=8), bc(dtb, NT, 1), ALU.add)
                    elif kind == "conv":
                        cw = [prm_col("d_conv_w", 6 * i + j) for i in range(4)]
                        link(tsc(cva, ps, cw[3], ALU.mult, prm_col("d_conv_b", j), ALU.add))
                        for i in (2, 1):
                            s = 3 - i
                            link(stt(cva[:, s:T], ps[:, 0:T - s], cw[i], cva[:, s:T], ALU.mult, ALU.add))
                        signal(stt(cva[:, 3:T], ps[:, 0:T - 3], cw[0], cva[:, 3:T], ALU.mult, ALU.add), "proj_copied")
                        dve.wait_ge(sem("conv_act"), sum(b[3] == "conv" for b in BLOCKS[l][:n + 1]))
                        if j < 4:
                            link(tt(xsF[:, j, :], cve, cva, ALU.mult))
                        elif j == 4:
                            link(tt(Bf, cve, cva, ALU.mult))
                        else:
                            for g in range(2):
                                gp = slice(64 * g, 64 * g + 64)
                                link(tt(Cp[gp, g, :], cve[gp, :], cva[gp, :], ALU.mult))
                    if kind != "conv":
                        signal(ins, "proj_copied")
                    for step in steps_after(l, n):
                        attention(l, step)
                    if l == 1 and n == 19:
                        ssd_decays()

            def attention(l, step):
                if step == LOGS and l == 0:
                    dve.wait_ge(sem("alpha_ready"), 1)
                    for j in range(2):
                        link(tsc(lg[:, j, :], PS[:, AB + j, :], prm_col("b_alpha_bias", j), ALU.add))
                    signal(stt(le, lgf, -1.0, lgf, ALU.mult, ALU.min), "log_pre")
                elif step == LOGS:
                    signal(dve.memset(f2(lqp), 0.0), "log_pre")
                elif step == SUMS:
                    decay_sums(l)
                elif step < TILE_DECAYS:
                    level(l, step - LEVELS)
                elif step == TILE_DECAYS:
                    tile_decays(l)
                elif step == KEYS_TURNED:
                    dve.wait_ge(sem("kd_turned"), l + 1)
                    signal(dve.tensor_copy(f2(lq)[:, 0:512], PS[:, 6, :]), "kdT_ready")
                elif step < OUTPUTS + NT - 1:
                    state(l, step - OUTPUTS)
                elif step >= GATED:
                    gated(l, step - GATED)

            def diff(l, n):
                hh = LV[n]
                lo, hi = halves(lgf, hh)
                ref = lo[:, :, hh - 1:hh]
                m = 1024 // (2 * hh)
                refb = ref.to_broadcast([P, m, hh])
                eq = le[:, 0:512].rearrange("p (n h) -> p n h", h=hh)
                ek = le[:, 512:1024].rearrange("p (n h) -> p n h", h=hh)
                link(tt(eq, hi, refb, ALU.subtract))
                signal(tt(ek, refb, lo, ALU.subtract), "lev_diff")

            def products(l, n):
                hh = LV[n]
                dve.wait_ge(sem("lev_exp"), lev_n * l + n + 1)
                eq = le[:, 0:512].rearrange("p (t n h) -> p t n h", t=2, h=hh)
                ek = le[:, 512:1024].rearrange("p (n h) -> p n h", h=hh)
                for par in range(2):
                    pp = slice(64 * par, 64 * par + 64)
                    for t2 in range(2):
                        q_hi = halves(lq[pp, t2, :], hh)[1]
                        o_hi = halves(lqp[pp, 2 * t2 + par, :], hh)[1]
                        link(tt(o_hi, q_hi, eq[pp, t2], ALU.mult))
                signal(tt(halves(f2(lkp), hh)[0], halves(f2(lk), hh)[0], ek, ALU.mult), "lev_ready")

            def merge(l, n, mask):
                dve.wait_ge(sem("lev_scored"), (lev_n + 1) * l + n + 1)
                ps = PS[:, AB:AB + NT, :].rearrange("p a (b c) -> p (a b) c", c=P)
                if n == 0:
                    signal(tt(lA, ps, bc(ident, 16, 1), ALU.mult), "lev_merged")
                else:
                    signal(dve.copy_predicated(lA, bc(mask, 16, 1).bitcast(I32), ps), "lev_merged")

            def decay_sums(l):
                dve.wait_ge(sem("log_done"), l + 1)
                if l == 0:
                    link(stt(lgf, lgf, 0.0, le, ALU.min, ALU.subtract))
                    link(tsc(lgf, lgf, 1.0 / 16, ALU.mult))
                for j in range(2):
                    link(dve.tensor_tensor_scan(lg[:, j, :], reset128, lg[:, j, :], 0.0, ALU.mult, ALU.add))
                link(dve.memset(f2(lqp), 0.0))

                diff(l, 0)
                for par in range(2):
                    pp = slice(64 * par, 64 * par + 64)
                    link(dve.tensor_copy(lqp[pp, par::2, :], lq[pp]))
                signal(dve.tensor_copy(lkp, lk), "lev_ready")

            def level(l, n):
                merge(l, n, lev_up[LV[n - 1]] if n else None)
                if n < lev_n:
                    products(l, n)
                if n + 1 < lev_n:
                    diff(l, n + 1)

            def tile_decays(l):
                dve.wait_ge(sem("tile_decay"), 2 * l + 1)
                le2 = le.rearrange("p (a b) -> p a b", b=T)
                for par in range(2):
                    pp = slice(64 * par, 64 * par + 64)
                    link(tt(lqp[pp, par::2, :], lq[pp], le2[pp], ALU.mult))
                link(dve.tensor_copy(ebl, le.rearrange("p (a t s) -> p a t s", a=2, s=P)[:, :, :, P - 1]))
                b3 = lgf.rearrange("p (n s) -> p n s", s=P)
                signal(tt(le.rearrange("p (n s) -> p n s", s=P), b3[:, :, P - 1:P].to_broadcast([P, 8, P]), b3,
                          ALU.subtract), "end_keys")
                dve.wait_ge(sem("tile_decay"), 2 * l + 2)
                signal(tt(f2(lkp), f2(lk), le, ALU.mult), "end_keys")

            def state(l, t):
                dve.wait_ge(sem("ls_ps"), 3 * l + t + 1)
                if t == 0:
                    link(dve.tensor_copy(f2(lq)[:, 512:768], PS[:, 6, 256:512]))
                for j in range(2):
                    ps = PS[:, 6, j * P:(j + 1) * P]
                    if t == 0:
                        ins = dve.tensor_copy(lS[:, j, :], ps)
                    else:
                        ins = stt(lS[:, j, :], lS[:, j, :], ebl[:, j, t:t + 1], ps, ALU.mult, ALU.add)
                    if j == 0:
                        link(ins)
                signal(ins, "ls_ready")

            def gated(l, hd):
                if l == 0 and hd == 0:
                    dve.wait_ge(sem("half_used"), HALVES)
                gain = prm_col(("b_norm_gain", "c_norm_gain")[l])
                dve.wait_ge(sem("o_rstd"), 4 * l + hd + 1)
                link(stt(lsq[:, hd, :], PS[:, AB + hd, :], gain, lrms[:, hd, :], ALU.mult, ALU.mult))
                ins = tt(y[:, 4 * (1 - l) + hd, :], lsq[:, hd, :], lgate[:, hd, :], ALU.mult)
                if hd < 3:
                    link(ins)
                else:
                    signal(ins, "yhalf")

            def col(name):
                return prm_col(name, 0, 4).unsqueeze(2).to_broadcast([P, 4, P])

            def front(t, piece):
                ts = slice(t * P, (t + 1) * P)
                r_t, k_t, v_t = rr[:, :, ts], kk_[:, :, ts], vv[:, :, ts]
                sg, aa, cs, eb, kk, kt, ka, be, b1, alp, rho = (
                    buffer[t % 2] for buffer in (SG, AA, CS, EB, KK, KT, KA, BE, B1, ALP, RHO))
                if piece == 0:
                    link(tt(kk, k_t, col("a_k_k"), ALU.mult))
                    signal(tt(b1, kk, kk, ALU.mult), "kk_sq")
                elif piece == 1:
                    dve.wait_ge(sem("front_act"), 3 * t + 1)
                    link(dve.tensor_tensor_scan(f2(cs), reset64, f2(sg), 0.0, ALU.mult, ALU.add))
                    signal(tt(sg, cs, sg, ALU.subtract), "cs_ready")
                    link(stt(kt, aa, -1.0, col("a_k_a"), ALU.add, ALU.mult))
                    link(stt(kt, kt, 1.0, k_t, ALU.add, ALU.mult))
                elif piece == 2:
                    dve.wait_ge(sem("front_act"), 3 * t + 2)
                    link(tt(ka, kt, cs, ALU.mult))
                    link(tt(be, aa, cs, ALU.mult))
                    if t == 1:
                        dve.wait_ge(sem("rows_cleared"), 16)
                    for par in range(2):
                        pp = slice(64 * par, 64 * par + 64)
                        link(tt(rho[pp, par::2, :], r_t[pp], eb[pp], ALU.mult))
                elif piece == 3:
                    dve.wait_ge(sem("front_act"), 3 * t + 3)
                    link(tt(kk, kk, b1, ALU.mult))
                    link(stt(sg, kk, -1.0, sg, ALU.mult, ALU.mult))
                    for par in range(2):
                        pp = slice(64 * par, 64 * par + 64)
                        link(dve.tensor_copy(alp[pp, par::2, :], sg[pp]))
                    link(tt(be, be, kk, ALU.mult))
                elif piece == 4:
                    link(tt(b1, r_t, kt, ALU.mult))
                    signal(tt(b1, b1, col("a_r_k"), ALU.mult), "feat_ready")
                elif piece == 5:
                    dve.wait_ge(sem("bonus_sum"), t + 1)
                    signal(tt(b1, PS[:, 3, :].rearrange("p (a b) -> p a b", b=P), v_t, ALU.mult), "bonus_used")

            def score_copy(t, n):
                b, dst, mask = ((5, X, strict_lo), (0, LKT, strict_up), (2, PKT, incl_up), (5, PBT, incl_up))[n]
                dve.wait_ge(sem("score_ready"), 4 * t + n + 1)
                ps = PS[:, b:b + 2, :].rearrange("p a (b c) -> p (a b) c", c=P)
                signal(tt(dst, ps, bc(mask, 8, 1), ALU.mult), "score_copied")

            def half(ap, g):
                return ap[:, 4 * g:4 * g + 4, :]

            def blocks_of_two():
                for g in range(2):
                    link(dve.tensor_copy(half(Tm, g), bc(ident, 4, 1)))
                    signal(dve.copy_predicated(half(Tm, g), bc(lev_lo[1], 4, 1).bitcast(I32), half(X, g)), "inv_ready")

            def inversion(t):
                for n in range(5):
                    for g in range(2):
                        dve.wait_ge(sem("p_ready"), 10 * t + 2 * n + g + 1)
                        signal(dve.copy_predicated(half(TT, g), bc(lev_up[LV[n + 1]], 4, 1).bitcast(I32),
                                                   PS[:, g, :].rearrange("p (b c) -> p b c", c=P)), "inv_ready")
                    if t and n == 0:
                        head_norm(t - 1, 2)
                    if t + 1 < NT:
                        for piece in ((), (0,), (), (1,), (2, 3, 4))[n]:
                            front(t + 1, piece)

            def states(t):
                for c in range(2):
                    po = 64 * c
                    dve.wait_ge(sem("un_ready"), 2 * t + c + 1)
                    dve.wait_ge(sem("rw_copied"), 2 * t + 2)
                    signal(tt(Un[po:po + 64, :], PS[po:po + 64, 3, :], U0[po:po + 64, :], ALU.add), "un_done")
                    dve.wait_ge(sem("st_ps"), 2 * t + c + 1)
                    for par in range(2):
                        pp = slice(64 * par, 64 * par + 64)
                        s_par = ST[pp, par::2, :]
                        link(tt(s_par, PS[pp, 4, 0:256].rearrange("p (a b) -> p a b", b=64), s_par, ALU.add))
                        ins = tt(s_par, s_par, EB[t % 2][pp, :, po + 63:po + 64].to_broadcast([64, 4, 64]), ALU.mult)
                        if par == 0:
                            link(ins)
                    signal(ins, "st_done")

            def head_norm(t, n):
                ts = slice(t * P, (t + 1) * P)
                sg, cs, eb, b1 = (buffer[t % 2] for buffer in (SG, CS, EB, B1))
                if n == 0:
                    dve.wait_ge(sem("ys_copied"), t + 1)
                    signal(tt(f2(cs), PS[:, 5, :], f2(sg), ALU.add), "gn_in")
                elif n == 1:
                    dve.wait_ge(sem("gn_sum"), 2 * t + 1)
                    link(stt(f2(cs), PS[:, 7, :], -1.0 / 64, f2(cs), ALU.mult, ALU.add))
                    signal(tt(eb, cs, cs, ALU.mult), "gn_in")
                else:
                    dve.wait_ge(sem("gn_rstd"), t + 1)
                    link(tt(cs, cs, eb, ALU.mult))
                    link(tt(cs, cs, col("a_ln_gain"), ALU.mult))
                    link(tt(cs, cs, col("a_ln_bias"), ALU.add))
                    link(tt(cs, cs, b1, ALU.add))
                    signal(tt(y[:, 0:4, ts], y[:, 0:4, ts], cs, ALU.mult), "rwkv_done")

            def rwkv():
                for ap in (*ALP, *RHO):
                    link(dve.memset(f2(ap), 0.0))
                signal(dve.memset(f2(ST), 0.0), "st_done")
                for piece in range(6):
                    front(0, piece)
                score_copy(0, 0)
                blocks_of_two()
                for n in range(1, 4):
                    score_copy(0, n)
                for t in range(NT):
                    inversion(t)
                    states(t)
                    head_norm(t, 0)
                    if t + 1 < NT:
                        front(t + 1, 5)
                    head_norm(t, 1)
                    if t + 1 < NT:
                        score_copy(t + 1, 0)
                        blocks_of_two()
                        for n in range(1, 4):
                            score_copy(t + 1, n)
                head_norm(NT - 1, 2)

            def lower_bounds():
                c0, c1 = prm_col("c_lb", 0, 2), prm_col("c_lb", 2, 2)
                link(tt(lbt[:, 0:2], c0, c1, ALU.max))
                link(tt(lbt[:, 4:6], c0, lbt[:, 0:2], ALU.subtract))
                signal(tt(lbt[:, 6:8], c1, lbt[:, 0:2], ALU.subtract), "setup_step")

            def lower_bounds_end():
                e0, e1 = lbt[:, 4:6], lbt[:, 6:8]
                dve.wait_ge(sem("setup_exp"), 2)
                link(tt(lbt[:, 0:2], e0, e1, ALU.add))
                link(dve.reciprocal(lbt[:, 0:2], lbt[:, 0:2]))
                link(tt(e0, e0, lbt[:, 0:2], ALU.mult))
                link(tt(e1, e1, lbt[:, 0:2], ALU.mult))
                link(tt(lbt[:, 0:2], e0, e1, ALU.add))
                link(tt(lb, lbt[:, 0:2], e0, ALU.subtract))
                link(tsc(omlb, lb, -1.0, ALU.mult, 1.0, ALU.add))

            def ssd_decays():
                signal(stt(f2(dz), f2(dt), -1.0, f2(dt), ALU.mult, ALU.min), "setup_step")
                dve.wait_ge(sem("setup_exp"), 4)
                link(tsc(f2(dz2), f2(dz), 2.0, ALU.add))
                link(dve.reciprocal(f2(dz2), f2(dz2)))
                link(tt(f2(dz), f2(dz), f2(dz2), ALU.mult))
                link(tt(f2(dz2), f2(dz), f2(dz), ALU.mult))
                terms = [2.0 / (2 * i + 1) for i in range(9)]
                link(tsc(f2(dpl), f2(dz2), terms[8], ALU.mult, terms[7], ALU.add))
                for i in range(6, -1, -1):
                    link(tt(f2(dpl), f2(dpl), f2(dz2), ALU.mult))
                    link(tsc(f2(dpl), f2(dpl), terms[i], ALU.add))
                link(tt(f2(dpl), f2(dpl), f2(dz), ALU.mult))
                link(stt(f2(dt), f2(dt), 0.0, f2(dpl), ALU.max, ALU.add))
                signal(stt(da, dt, -1.0, bc(alog, NT, 1), ALU.mult, ALU.mult), "ssd_inputs")

            def ssd_tile(t):
                Es, dte_t, CBm = Es2[t % 2], dte2[t % 2], CBm2[t % 2]
                b = 2 + 3 * (t % 2)
                dve.wait_ge(sem("cb_ready"), t + 1)
                for hd in range(8):
                    link(tsc(Es[:, hd, :], PS[:, b + hd // 4, (hd % 4) * P:(hd % 4 + 1) * P],
                             cumc[:, t, hd:hd + 1], ALU.subtract, 0.0, ALU.min))
                last = PS[:, b:b + 2, :].rearrange("p a (b c) -> p (a b) c", c=P)[:, :, P - 1]
                signal(tt(dte_t, last, cumc[:, t, :], ALU.subtract), "seg_diff")
                link(tt(CBm, PS[:, b + 2, 0:256].rearrange("p (a b) -> p a b", b=P), bc(upper, 2, 1), ALU.mult))
                link(tt(xdt2[t % 2].rearrange("p (a b) -> p a b", b=64), xsT[:, t, :].rearrange("p (a b) -> p a b", b=64),
                        dt[:, t, :].unsqueeze(2).to_broadcast([P, 8, 64]), ALU.mult))

            def ssd_scores(t):
                Es, ec, Csp, dte_t = Es2[t % 2], ec2[t % 2], Csp2[t % 2], dte2[t % 2]
                dve.wait_ge(sem("seg_exp"), 2 * t + 1)
                Eg = Es.rearrange("p (g q) c -> p g q c", g=2)
                link(tt(Eg, Eg, bc(CBm2[t % 2], 4, 2), ALU.mult))
                dve.wait_ge(sem("seg_exp"), 2 * t + 2)
                link(tt(xdd2[t % 2].rearrange("p (a b) -> p a b", b=64), xdt2[t % 2].rearrange("p (a b) -> p a b", b=64),
                        dte_t.unsqueeze(2).to_broadcast([P, 8, 64]), ALU.mult))
                for g in range(2):
                    gp = slice(64 * g, 64 * g + 64)
                    ins = tt(Csp[gp, 4 * g:4 * g + 4, :], ec[gp, 4 * g:4 * g + 4, :],
                             bc(Cp[gp, g, t * P:(t + 1) * P], 4, 1), ALU.mult)
                    if g == 0:
                        link(ins)
                signal(ins, "ssd_in")

            def ssd_state(t):
                dve.wait_ge(sem("ssd_st_ps"), t + 1)
                ps = PS[:, 1, 0:256].rearrange("p (a b) -> p a b", b=64)
                if t == 0:
                    link(dve.tensor_copy(Sst, ps))
                else:
                    for g in range(2):
                        gp = slice(64 * g, 64 * g + 64)
                        link(tt(Stm[gp], Sst[gp], ec2[t % 2][gp, 4 * g:4 * g + 4, P - 1:P].to_broadcast([64, 4, 64]),
                                ALU.mult))
                    link(tt(Sst, Stm, ps, ALU.add))

            def ssd():
                dve.wait_ge(sem("xs_turned"), 1)
                link(dve.tensor_copy(xsT, PS[:, 0:4, :]))
                signal(dve.tensor_copy(f2(Bt), PS[:, 4, :]), "ssd_inputs")
                dve.wait_ge(sem("xs_turned"), 2)
                signal(dve.tensor_copy(f2(cumc), PS[:, 5, 0:32]), "ssd_inputs")
                for ap in Csp2:
                    link(dve.memset(f2(ap), 0.0))
                ssd_tile(0)
                ssd_scores(0)
                for t in range(NT):
                    ts = slice(t * P, (t + 1) * P)
                    if t + 1 < NT:
                        ssd_tile(t + 1)
                    dve.wait_ge(sem("ssd_y_ready"), t + 1)
                    for j in range(4):
                        ins = stt(yF[:, j, ts], xsF[:, j, ts], skipc[:, j:j + 1], PS[:, 0, j * P:(j + 1) * P],
                                  ALU.mult, ALU.add)
                        if j < 3:
                            link(ins)
                    signal(ins, "ssd_y_copied")
                    if t + 1 < NT:
                        ssd_state(t)
                        ssd_scores(t + 1)
                signal(tt(yF, yF, zs, ALU.mult), "yz_ready")
                for j in range(4):
                    if j % 2 == 0:
                        dve.wait_ge(sem("o_rstd"), 8 + j // 2 + 1)
                    rstd = f2(Es2[0])[:, 512 * (j // 2):512 * (j // 2) + 512]
                    link(stt(y[:, 4 + j, :], yF[:, j, :], prm_col("d_norm_gain", j), rstd, ALU.mult, ALU.mult))

            def outproj(l):
                signal(dve.tensor_copy(lsum[:, 0:1], lsum[:, 1:2]), "mix_done")
                for n in range(KD):
                    dve.wait_ge(sem("outproj_done"), 8 * l + n + 1)
                    signal(stt(xT[:, n, :], PS[:, n % 4, :], mod[:, l, 16 + n:17 + n], xT[:, n, :], ALU.mult, ALU.add),
                           "x_ready")

            def choose(l):
                dve.wait_ge(sem("logits_exp"), l + 1)
                sigmoid_tail(sc)
                link(tt(sel, sc, bc(rbias, NT, 1), ALU.add))
                v = sel.rearrange("p t (n two) -> p t n two", two=2)
                link(tt(r1, v[:, :, :, 0], v[:, :, :, 1], ALU.max))
                link(tt(r2, v[:, :, :, 0], v[:, :, :, 1], ALU.min))
                mx = r1.rearrange("p t (g two) -> p t g two", two=2)
                mn = r2.rearrange("p t (g two) -> p t g two", two=2)
                link(tt(gs, mx[:, :, :, 0], mx[:, :, :, 1], ALU.min))
                link(tt(gm, mn[:, :, :, 0], mn[:, :, :, 1], ALU.max))
                link(tt(gm, gm, gs, ALU.max))
                link(tt(gs, mx[:, :, :, 0], mx[:, :, :, 1], ALU.max))
                link(tt(gs, gs, gm, ALU.add))

                def first_max(vals, n, onehot):
                    link(dve.tensor_reduce(m1, vals, AX_X, ALU.max))
                    m1b = m1.unsqueeze(2).to_broadcast([P, NT, n])
                    t_ = idc[:, :, 0:n]
                    link(tt(t_, vals, m1b, ALU.is_lt))
                    link(stt(t_, t_, BIG, bc(iota16[:, 0:n], NT, 1), ALU.mult, ALU.add))
                    link(dve.tensor_reduce(m1, t_, AX_X, ALU.min))
                    link(tt(onehot, bc(iota16[:, 0:n], NT, 1), m1b, ALU.is_equal))

                first_max(gs, GRP, gm)
                link(tsc(gs, gm, -1.0, ALU.add, BIG, ALU.mult))
                s4 = sel.rearrange("p t (g i) -> p t g i", i=4)
                link(tt(s4, s4, gs.unsqueeze(3).to_broadcast([P, NT, GRP, 4]), ALU.add))
                ohv = [oh[:, k, :].rearrange("p (t e) -> p t e", e=E) for k in range(2)]
                first_max(sel, E, ohv[0])
                link(stt(sel, ohv[0], -4 * BIG, sel, ALU.mult, ALU.add))
                first_max(sel, E, ohv[1])
                signal(tt(both, ohv[0], ohv[1], ALU.add), "choices_ready")

                def pick(out, src):
                    link(tt(picked, oh, bc(src.rearrange("p a b -> p (a b)"), 2, 1), ALU.mult))
                    link(dve.tensor_reduce(out, picked.rearrange("p k (t e) -> p k t e", e=E), AX_X, ALU.add))

                link(tsc(mult3, iota16[:, 1:4], float(P), ALU.mult))
                pick(gk, sc)
                link(tt(gsum, gk[:, 0, :], gk[:, 1, :], ALU.add))
                link(dve.reciprocal(gsum, gsum))
                link(tt(gk, gk, bc(gsum, 2, 1), ALU.mult))

                dve.wait_ge(sem("rank_ready"), l + 1)
                link(tt(rank, PS[:, 5, 0:NT * E].rearrange("p (a b) -> p a b", b=E), both, ALU.subtract))
                link(dve.tensor_copy(cnt, PS[:, 5, NT * E:(NT + 1) * E]))

                def whole_blocks(out, src, n, op):
                    cmp = cmp3[:, 0:n, :]
                    link(tt(cmp, src.unsqueeze(2).to_broadcast([P, n, 3]), bc(mult3, n, 1), op))
                    link(dve.tensor_reduce(out, cmp, AX_X, ALU.add))

                def f2(ap):
                    return ap.rearrange("p a b -> p (a b)")

                whole_blocks(nov, cnt, E, ALU.is_gt)
                link(dve.tensor_tensor_scan(ove, ones[:, 0:E], nov, 0.0, ALU.mult, ALU.add))
                link(tt(over, ove, nov, ALU.subtract))
                link(tt(over, over, iota16, ALU.subtract))
                whole_blocks(f2(qq), f2(rank), NT * E, ALU.is_ge)
                link(tsc(q0, qq, 0.0, ALU.is_gt))
                link(stt(blk, qq, 15.0, bc(over, NT, 1), ALU.add, ALU.add))
                link(tt(blk, blk, q0, ALU.mult))
                link(tt(blk, blk, bc(iota16, NT, 1), ALU.add))
                link(stt(rin, qq, -float(P), rank, ALU.mult, ALU.add))
                pick(selb, blk)
                pick(selr, rin)

                link(tt(ohr, bc(iota128, 2 * NT, 1), f2(selr).unsqueeze(2).to_broadcast([P, 2 * NT, P]), ALU.is_equal))
                link(tt(ohb, bc(iota24, 2 * NT, 1), f2(selb).unsqueeze(2).to_broadcast([P, 2 * NT, MAX_BLOCKS]),
                        ALU.is_equal))
                ohb4 = ohb.rearrange("p (k t) b -> p k t b", k=2)
                signal(tt(ohb4, ohb4, bc(tokid.unsqueeze(2).to_broadcast([P, NT, MAX_BLOCKS]), 2, 1), ALU.mult),
                       "place_ready")

                cmp8 = f2(cmp3)[:, 0:8 * E].rearrange("p (b e) -> p b e", e=E)
                link(tt(cmp8, bc(ove, 8, 1), iota16[:, 0:8].unsqueeze(2).to_broadcast([P, 8, E]), ALU.is_le))
                link(dve.tensor_reduce(tabf[:, E:E + 8], cmp8, AX_X, ALU.add))
                link(tsc(tabf[:, E:E + 8], tabf[:, E:E + 8], float(E - 1), ALU.min))
                link(dve.tensor_copy(tabf[:, 0:E], iota16))
                link(dve.tensor_copy(table[:, 0:24], tabf[:, 0:24]))
                link(tt(cmp8[:, 0, 0:4], ove[:, E - 1:E].to_broadcast([P, 4]), iota16[:, 0:8:2], ALU.is_gt))
                link(dve.tensor_reduce(tabf[:, 24:25], cmp8[:, 0, 0:4], AX_X, ALU.add))
                link(tsc(tabf[:, 25:26], tabf[:, 24:25], 7.0, ALU.add))
                link(tsc(tabf[:, 24:25], tabf[:, 24:25], 8.0, ALU.add))
                link(dve.tensor_copy(table[:, 30 + l:31 + l], tabf[:, 24:25]))
                link(dve.tensor_copy(table[:, 26 + l:27 + l], tabf[:, 25:26]))
                link(stt(destf, selb, float(P), selr, ALU.mult, ALU.add))
                link(dve.tensor_copy(idx_dest[:, :], f2(destf)))
                dve.wait_ge(sem("place_used"), l + 1)
                signal(dve.tensor_copy(idx_tok[:, 0:MAX_BLOCKS], PS[:, 6, 0:MAX_BLOCKS]), "table_ready")

            def experts(l):
                choose(l)
                pairs = pairs_of(dve, l)
                so = sem(f"l{l}_silu_order")
                with dve.Fori(0, pairs) as it:
                    for j in range(2):
                        b1 = it * 2 + (j + 1)
                        dve.wait_ge(sem(f"l{l}_gate_exp"), b1)
                        tsc(sgt, sgt, 1.0, ALU.add).then_inc(so, 1)
                        dve.wait_ge(so, it * 6 + (3 * j + 1))
                        dve.reciprocal(sgt, sgt).then_inc(so, 1)
                        dve.wait_ge(so, it * 6 + (3 * j + 2))
                        tt(sgt, sgt, PS[:, 0, :], ALU.mult).then_inc(so, 1)
                        dve.wait_ge(so, it * 6 + (3 * j + 3))
                        dve.wait_ge(sem(f"l{l}_up_done"), b1)
                        for s in range(2):
                            half = slice(s * 256, s * 256 + 256)
                            tt(actb[:, half], sgt[:, half], PS[:, 1, half], ALU.mult)\
                                .then_inc(sem(f"l{l}_act_done"), 1)
                        for s in range(2):
                            dve.wait_ge(sem(f"l{l}_at_turned"), it * 4 + (2 * j + s + 1))
                            dve.tensor_copy(aT[:, 2 * s:2 * s + 2, :],
                                            PS[:, 4 + 3 * s, 0:256].rearrange("p (a b) -> p a b", b=P))\
                               .then_inc(sem(f"l{l}_at_copied"), 1)
                def combine(t):
                    dve.wait_ge(sem(f"expert_rows{t}"), 32 * (l + 1))
                    c0, c1 = cg[:, 2 * t, :], cg[:, 2 * t + 1, :]
                    link(tsc(c0, c0, gk[:, 0, t:t + 1], ALU.mult))
                    signal(stt(c0, c1, gk[:, 1, t:t + 1], c0, ALU.mult, ALU.add), "combined")

                combine(0)
                for t in range(NT):
                    if t + 1 < NT:
                        combine(t + 1)
                    dve.wait_ge(sem("comb_turned"), NT * l + t + 1)
                    for k in range(KD):
                        xs = xT[:, k, t * P:(t + 1) * P]
                        ps = PS[:, 2 * (t % 2) + k // 4, (k % 4) * P:(k % 4 + 1) * P]
                        ins = stt(xs, ps, mod[:, l, 40 + k:41 + k], xs, ALU.mult, ALU.add)
                        if k < KD - 1:
                            link(ins)
                    signal(ins, "comb_added")
                signal(dve.tensor_copy(lsum[:, 0:1], lsum[:, 1:2]), "x_ready")

            link(dve.memset(lsum, 0.0))
            for i in range(12):
                ada_chunk(i)
                if i == 5:
                    norm(0)
                if i == 9:
                    parameters()
                    lower_bounds()
            dve.wait_ge(sem("pool_const"), 2)
            modulation(0)
            projections(0)
            modulation(1)
            lower_bounds_end()
            rwkv()
            outproj(0)
            norm(1)
            experts(0)
            link(dve.memset(f2(Cp), 0.0))
            norm(2)
            projections(1)
            ssd()
            outproj(1)
            norm(3)
            experts(1)
            norm(4)


_INS = ['x', 'c', 'norm_gain', 'w_ada', 'b_ada', 'w_in_even', 'w_in_odd', 'w_out', 'a_mu', 'a_w0', 'a_w_up', 'a_a0',
        'a_a_up', 'a_g_up', 'a_k_k', 'a_k_a', 'a_r_k', 'a_ln_gain', 'a_ln_bias', 'b_alpha_up', 'b_alpha_bias',
        'b_norm_gain', 'c_lb', 'c_norm_gain', 'd_conv_w', 'd_conv_b', 'd_dt_bias', 'd_a_log', 'd_skip', 'd_norm_gain',
        'w_router', 'router_bias', 'w_gate', 'w_up', 'w_down', 'final_gain']


def kernel(**inputs):
    import numpy as np
    import concourse.bacc as bacc
    from concourse.bass_utils import run_bass_kernel_spmd

    nc = bacc.Bacc("TRN2", target_bir_lowering=False, num_devices=1)
    arrays, aps = {}, {}
    for name in _INS:
        a = np.ascontiguousarray(inputs[name])
        arrays[f"in_{name}_dram"] = a
        aps[name] = nc.dram_tensor(f"in_{name}_dram", a.shape, mybir.dt.from_np(a.dtype), kind="ExternalInput").ap()
    out = nc.dram_tensor("out_0_dram", (1, T, D), F32, kind="ExternalOutput").ap()
    trunk(nc, aps, out)
    r = run_bass_kernel_spmd(nc, [arrays], core_ids=[0])
    return r.results[0]["out_0_dram"]
```
